# Optimizing a Trainium2 kernel written in Bass

```python
import math
import jax
import jax.numpy as jnp
from jax import lax
import numpy as np
import jax, jax.numpy as jnp

D_MODEL = 1024
BATCH = 1
SEQ = 512
DEPTH = 1

D_MIX = D_MODEL
D_S5 = D_MIX // 2
S5_GROUP = 16
N_S5_GROUPS = D_S5 // S5_GROUP
S5_STATE = 64
D_GDN = D_MIX - D_S5
GDN_HEAD_DIM = 128
N_GDN_HEADS = D_GDN // GDN_HEAD_DIM
CONV_WIDTH = 4
CHUNK = 64
D_IN = D_S5 + 4 * D_GDN + 2 * N_GDN_HEADS
N_EXPERT_GROUPS = 4
EXPERTS_PER_GROUP = 8
N_EXPERTS = N_EXPERT_GROUPS * EXPERTS_PER_GROUP
TOP_K_IN_GROUP = 2
D_EXPERT = D_MODEL // 4
N_MOD = 6
EPS = 1e-6


def rmsnorm(x, g):
    x32 = x.astype(jnp.float32)
    y = x32 * lax.rsqrt(jnp.mean(x32 * x32, axis=-1, keepdims=True) + EPS)
    return (y * g.astype(jnp.float32)).astype(x.dtype)

def l2norm(x):
    return x * lax.rsqrt(jnp.sum(x * x, axis=-1, keepdims=True) + EPS)

def modulate(h, shift, scale):
    return h * (1.0 + scale[:, None, :]) + shift[:, None, :]

def _linear_recurrence_combine(e1, e2):
    a1, b1 = e1
    a2, b2 = e2
    return a1 * a2, a2 * b1 + b2

def s5_mixer(u, lam_re, lam_im, log_step, b_re, b_im, c_re, c_im, d_skip, w_glu, b_glu):
    f32 = jnp.float32
    bsz, seq, _ = u.shape
    u32 = u.astype(f32)
    ug = u32.reshape(bsz, seq, N_S5_GROUPS, S5_GROUP)
    lam = lax.complex(lam_re.astype(f32), lam_im.astype(f32))
    step = jnp.exp(log_step.astype(f32))[:, None]
    lam_bar = jnp.exp(lam * step)
    b_c = lax.complex(b_re.astype(f32), b_im.astype(f32))
    b_bar = ((lam_bar - 1.0) / lam)[..., None] * b_c
    bu = lax.complex(jnp.einsum('gph,blgh->blgp', b_bar.real, ug),
                     jnp.einsum('gph,blgh->blgp', b_bar.imag, ug))
    a = jnp.broadcast_to(lam_bar, bu.shape)
    _, states = lax.associative_scan(_linear_recurrence_combine, (a, bu), axis=1)
    c_c = lax.complex(c_re.astype(f32), c_im.astype(f32))
    y = jnp.einsum('ghp,blgp->blgh', c_c, states).real.reshape(bsz, seq, D_S5)
    y = y + d_skip.astype(f32) * u32
    y = jax.nn.gelu(y)
    y = y * jax.nn.sigmoid(y @ w_glu.astype(f32) + b_glu.astype(f32))
    return y.astype(u.dtype)

def causal_depthwise_conv(x, w):
    k, ch = w.shape
    return lax.conv_general_dilated(x, w[:, None, :], window_strides=(1,),
                                    padding=[(k - 1, 0)],
                                    dimension_numbers=('NWC', 'WIO', 'NWC'),
                                    feature_group_count=ch)

def gated_delta_rule(q, k, v, g, beta):
    bsz, nh, seq, dk = q.shape
    dv = v.shape[-1]
    n_chunks = seq // CHUNK
    q = q.reshape(bsz, nh, n_chunks, CHUNK, dk)
    k = k.reshape(bsz, nh, n_chunks, CHUNK, dk)
    v = v.reshape(bsz, nh, n_chunks, CHUNK, dv)
    beta = beta.reshape(bsz, nh, n_chunks, CHUNK)
    g = jnp.cumsum(g.reshape(bsz, nh, n_chunks, CHUNK), axis=-1)
    idx = jnp.arange(CHUNK)
    causal = idx[:, None] >= idx[None, :]
    strict = idx[:, None] > idx[None, :]
    decay = jnp.exp(jnp.where(causal, g[..., :, None] - g[..., None, :], -jnp.inf))
    k_beta = k * beta[..., None]
    v_beta = v * beta[..., None]
    kkt = jnp.einsum('bhncd,bhnsd->bhncs', k_beta, k) * decay
    a_mat = jnp.where(strict, kkt, 0.0) + jnp.eye(CHUNK, dtype=q.dtype)
    rhs = jnp.concatenate([v_beta, k_beta * jnp.exp(g)[..., None]], axis=-1)
    sol = lax.linalg.triangular_solve(a_mat, rhs, left_side=True, lower=True,
                                      unit_diagonal=True)
    value, k_cumdecay = sol[..., :dv], sol[..., dv:]
    qk = jnp.einsum('bhncd,bhnsd->bhncs', q, k) * decay
    q_decay = q * jnp.exp(g)[..., None]
    k_tail = k * jnp.exp(g[..., -1:] - g)[..., None]
    g_last = jnp.exp(g[..., -1])

    def chunk_step(state, inp):
        qk_i, qd_i, kc_i, val_i, kt_i, gl_i = inp
        v_new = val_i - jnp.einsum('bhcd,bhde->bhce', kc_i, state)
        o_i = (jnp.einsum('bhcd,bhde->bhce', qd_i, state)
               + jnp.einsum('bhcs,bhse->bhce', qk_i, v_new))
        state = state * gl_i[..., None, None] + jnp.einsum('bhcd,bhce->bhde', kt_i, v_new)
        return state, o_i

    xs = tuple(jnp.moveaxis(t, 2, 0) for t in (qk, q_decay, k_cumdecay, value, k_tail, g_last))
    state0 = jnp.zeros((bsz, nh, dk, dv), q.dtype)
    _, o = lax.scan(chunk_step, state0, xs)
    return jnp.moveaxis(o, 0, 2).reshape(bsz, nh, seq, dv)

def gdn_mixer(qkv, z, a_gate, b_gate, conv_w, a_log, dt_bias, gdn_norm_g):
    f32 = jnp.float32
    bsz, seq, _ = qkv.shape
    qkv = jax.nn.silu(causal_depthwise_conv(qkv, conv_w)).astype(f32)
    q, k, v = jnp.split(qkv, 3, axis=-1)

    def heads(t):
        return t.reshape(bsz, seq, N_GDN_HEADS, GDN_HEAD_DIM).transpose(0, 2, 1, 3)

    q = l2norm(heads(q)) * (GDN_HEAD_DIM ** -0.5)
    k = l2norm(heads(k))
    v = heads(v)
    beta = jax.nn.sigmoid(b_gate.astype(f32)).transpose(0, 2, 1)
    g = (-jnp.exp(a_log.astype(f32))
         * jax.nn.softplus(a_gate.astype(f32) + dt_bias.astype(f32))).transpose(0, 2, 1)
    o = gated_delta_rule(q, k, v, g, beta).transpose(0, 2, 1, 3)
    zh = z.astype(f32).reshape(bsz, seq, N_GDN_HEADS, GDN_HEAD_DIM)
    o = rmsnorm(o, gdn_norm_g) * jax.nn.silu(zh)
    return o.reshape(bsz, seq, D_GDN).astype(z.dtype)

def hybrid_mixer(h, w_in, lam_re, lam_im, log_step, s5_b_re, s5_b_im, s5_c_re, s5_c_im,
                 s5_d, w_glu, b_glu, conv_w, a_log, dt_bias, gdn_norm_g, w_out):
    proj = h @ w_in
    splits = [D_S5, D_S5 + 3 * D_GDN, D_S5 + 4 * D_GDN, D_S5 + 4 * D_GDN + N_GDN_HEADS]
    u_s5, qkv, z, a_gate, b_gate = jnp.split(proj, splits, axis=-1)
    y_s5 = s5_mixer(u_s5, lam_re, lam_im, log_step, s5_b_re, s5_b_im, s5_c_re, s5_c_im,
                    s5_d, w_glu, b_glu)
    y_gdn = gdn_mixer(qkv, z, a_gate, b_gate, conv_w, a_log, dt_bias, gdn_norm_g)
    return jnp.concatenate([y_s5, y_gdn], axis=-1) @ w_out

def hier_moe(h, w_router_grp, w_router_exp, w_gate, w_up, w_down):
    f32 = jnp.float32
    bsz, seq, d = h.shape
    hf = h.reshape(bsz * seq, d)
    grp_logits = (hf @ w_router_grp).astype(f32)
    grp_prob = jax.nn.softmax(grp_logits, axis=-1)
    grp_idx = jnp.argmax(grp_logits, axis=-1)
    grp_onehot = jax.nn.one_hot(grp_idx, N_EXPERT_GROUPS, dtype=f32)
    p_grp = jnp.sum(grp_prob * grp_onehot, axis=-1)
    exp_logits = (hf @ w_router_exp).astype(f32).reshape(-1, N_EXPERT_GROUPS, EXPERTS_PER_GROUP)
    sel_logits = jnp.einsum('tg,tge->te', grp_onehot, exp_logits)
    top_val, top_idx = lax.top_k(sel_logits, TOP_K_IN_GROUP)
    w_k = jax.nn.softmax(top_val, axis=-1) * p_grp[:, None]
    expert_id = grp_idx[:, None] * EXPERTS_PER_GROUP + top_idx
    combine = jnp.einsum('tk,tke->te', w_k,
                         jax.nn.one_hot(expert_id, N_EXPERTS, dtype=f32)).astype(h.dtype)

    def expert_step(acc, ws):
        wg, wu, wd, gate_col = ws
        y = (jax.nn.silu(hf @ wg) * (hf @ wu)) @ wd
        return acc + gate_col[:, None] * y, None

    acc0 = jnp.zeros_like(hf)
    out, _ = lax.scan(expert_step, acc0, (w_gate, w_up, w_down, combine.T))
    return out.reshape(bsz, seq, d)

def first_inputs(seed: int = 0) -> dict:
    key = jax.random.key(seed)
    ks = jax.random.split(key, 32)
    f32 = jnp.float32

    def nrm(k, shape, scale):
        return jax.random.normal(k, shape, f32) * scale

    nl = DEPTH
    gp = (nl, N_S5_GROUPS, S5_STATE)
    n_idx = jnp.arange(S5_STATE, dtype=f32)
    dt_init = jnp.exp(jax.random.uniform(ks[21], (nl, N_GDN_HEADS), f32,
                                         math.log(1e-3), math.log(1e-1)))
    return {
        'x': nrm(ks[0], (BATCH, SEQ, D_MODEL), 1.0),
        'c': nrm(ks[1], (BATCH, D_MODEL), 1.0),
        'norm1_g': 1.0 + nrm(ks[2], (nl, D_MODEL), 0.02),
        'norm2_g': 1.0 + nrm(ks[3], (nl, D_MODEL), 0.02),
        'w_ada': nrm(ks[4], (nl, D_MODEL, N_MOD * D_MODEL), 0.5 * D_MODEL ** -0.5),
        'b_ada': nrm(ks[5], (nl, N_MOD * D_MODEL), 0.02),
        'w_in': nrm(ks[6], (nl, D_MODEL, D_IN), D_MODEL ** -0.5),
        'lam_re': -0.5 + nrm(ks[7], gp, 0.01),
        'lam_im': math.pi * n_idx + nrm(ks[8], gp, 0.01),
        'log_step': jax.random.uniform(ks[9], (nl, N_S5_GROUPS), f32,
                                       math.log(1e-3), math.log(1e-1)),
        's5_b_re': nrm(ks[10], (nl, N_S5_GROUPS, S5_STATE, S5_GROUP), (2 * S5_GROUP) ** -0.5),
        's5_b_im': nrm(ks[11], (nl, N_S5_GROUPS, S5_STATE, S5_GROUP), (2 * S5_GROUP) ** -0.5),
        's5_c_re': nrm(ks[12], (nl, N_S5_GROUPS, S5_GROUP, S5_STATE), S5_STATE ** -0.5),
        's5_c_im': nrm(ks[13], (nl, N_S5_GROUPS, S5_GROUP, S5_STATE), S5_STATE ** -0.5),
        's5_d': nrm(ks[14], (nl, D_S5), 0.5),
        'w_glu': nrm(ks[15], (nl, D_S5, D_S5), D_S5 ** -0.5),
        'b_glu': nrm(ks[16], (nl, D_S5), 0.02),
        'conv_w': nrm(ks[17], (nl, CONV_WIDTH, 3 * D_GDN), CONV_WIDTH ** -0.5),
        'a_log': jnp.log(jax.random.uniform(ks[18], (nl, N_GDN_HEADS), f32, 1.0, 16.0)),
        'dt_bias': dt_init + jnp.log(-jnp.expm1(-dt_init)),
        'gdn_norm_g': 1.0 + nrm(ks[19], (nl, GDN_HEAD_DIM), 0.02),
        'w_out': nrm(ks[20], (nl, D_MIX, D_MODEL), D_MIX ** -0.5),
        'w_router_grp': nrm(ks[22], (nl, D_MODEL, N_EXPERT_GROUPS), D_MODEL ** -0.5),
        'w_router_exp': nrm(ks[23], (nl, D_MODEL, N_EXPERTS), D_MODEL ** -0.5),
        'w_gate': nrm(ks[24], (nl, N_EXPERTS, D_MODEL, D_EXPERT), D_MODEL ** -0.5),
        'w_up': nrm(ks[25], (nl, N_EXPERTS, D_MODEL, D_EXPERT), D_MODEL ** -0.5),
        'w_down': nrm(ks[26], (nl, N_EXPERTS, D_EXPERT, D_MODEL), D_EXPERT ** -0.5),
        'normf_g': 1.0 + nrm(ks[27], (D_MODEL,), 0.02),
    }

def first_block(x, c, norm1_g, norm2_g, w_ada, b_ada, w_in, lam_re, lam_im, log_step,
              s5_b_re, s5_b_im, s5_c_re, s5_c_im, s5_d, w_glu, b_glu, conv_w, a_log,
              dt_bias, gdn_norm_g, w_out, w_router_grp, w_router_exp, w_gate, w_up,
              w_down, normf_g):
    h = x
    c_act = jax.nn.silu(c)
    for l in range(DEPTH):
        mod = c_act @ w_ada[l] + b_ada[l]
        sh1, sc1, gt1, sh2, sc2, gt2 = jnp.split(mod, N_MOD, axis=-1)
        a_in = modulate(rmsnorm(h, norm1_g[l]), sh1, sc1)
        mix = hybrid_mixer(a_in, w_in[l], lam_re[l], lam_im[l], log_step[l], s5_b_re[l],
                           s5_b_im[l], s5_c_re[l], s5_c_im[l], s5_d[l], w_glu[l], b_glu[l],
                           conv_w[l], a_log[l], dt_bias[l], gdn_norm_g[l], w_out[l])
        h = h + gt1[:, None, :] * mix
        m_in = modulate(rmsnorm(h, norm2_g[l]), sh2, sc2)
        moe = hier_moe(m_in, w_router_grp[l], w_router_exp[l], w_gate[l], w_up[l], w_down[l])
        h = h + gt2[:, None, :] * moe
    return rmsnorm(h, normf_g)


POOL_WIDTH = D_MODEL // 2
POOL_GROUPS = 4
POOL_GROUP_DIM = POOL_WIDTH // POOL_GROUPS
POOL_WINDOWS = (2, 4, 8, 16)
LRU_WIDTH = D_MODEL
LRU_HEADS = 16
LRU_HEAD_DIM = LRU_WIDTH // LRU_HEADS
RG_C = 8.0
IN_COLS = POOL_WIDTH + 2 * LRU_WIDTH + 2 * D_MODEL
N_GROUPS = 4
EXP_PER_GROUP = 4
N_EXP = N_GROUPS * EXP_PER_GROUP
TOP_K = 2
D_EXPERT_2 = D_MODEL // 2


def rms_norm(x, g):
    xf = x.astype(jnp.float32)
    y = xf * lax.rsqrt(jnp.mean(xf * xf, axis=-1, keepdims=True) + EPS)
    return (y * g.astype(jnp.float32)).astype(x.dtype)

def pooling_mixer(u, pool_w, pool_scale):
    b_, s_, _ = u.shape
    ug = u.astype(jnp.float32).reshape(b_, s_, POOL_GROUPS, POOL_GROUP_DIM)
    c = jnp.cumsum(ug, axis=1)
    pos = jnp.arange(1, s_ + 1, dtype=jnp.float32)
    pooled = []
    for g, w in enumerate(POOL_WINDOWS):
        cg = c[:, :, g]
        prev = jnp.pad(cg[:, :s_ - w], ((0, 0), (w, 0), (0, 0)))
        cnt = jnp.minimum(pos, float(w))
        pooled.append((cg - prev) / cnt[None, :, None])
    z = (jnp.stack(pooled, axis=2) - ug).astype(u.dtype)
    y = jnp.einsum('bsgc,gcd->bsgd', z, pool_w).reshape(b_, s_, POOL_WIDTH)
    return y * pool_scale

def rglru_mixer(u, gate_in, conv_w, conv_b, w_r, b_r, w_i, b_i, lam):
    b_, s_, c_ = u.shape
    xc = lax.conv_general_dilated(
        u, conv_w[:, None, :], window_strides=(1,), padding=[(CONV_WIDTH - 1, 0)],
        dimension_numbers=('NWC', 'WIO', 'NWC'), feature_group_count=c_) + conv_b
    xh = xc.reshape(b_, s_, LRU_HEADS, LRU_HEAD_DIM)
    r = jax.nn.sigmoid(jnp.einsum('bshc,hcd->bshd', xh, w_r).reshape(b_, s_, c_) + b_r)
    i = jax.nn.sigmoid(jnp.einsum('bshc,hcd->bshd', xh, w_i).reshape(b_, s_, c_) + b_i)
    log_a = -RG_C * r.astype(jnp.float32) * jax.nn.softplus(-lam.astype(jnp.float32))
    a = jnp.exp(log_a)
    mult = jnp.sqrt(-jnp.expm1(2.0 * log_a))
    bt = mult * (i * xc).astype(jnp.float32)

    def combine(lhs, rhs):
        a1, b1 = lhs
        a2, b2 = rhs
        return a1 * a2, a2 * b1 + b2

    _, h = lax.associative_scan(combine, (a, bt), axis=1)
    return h.astype(u.dtype) * jax.nn.gelu(gate_in)

def hier_moe_2(h, rg_w, rg_b, re_w, re_b, e_gate, e_up, e_down):
    b_, s_, d_ = h.shape
    xt = h.reshape(b_ * s_, d_)
    g_logits = (xt @ rg_w + rg_b).astype(jnp.float32)
    g_prob = jax.nn.softmax(g_logits, axis=-1)
    p_top, g_idx = lax.top_k(g_prob, 1)
    e_logits = (xt @ re_w + re_b).astype(jnp.float32).reshape(-1, N_GROUPS, EXP_PER_GROUP)
    sel = jnp.take_along_axis(e_logits, g_idx[:, :, None], axis=1)[:, 0]
    v, e_idx = lax.top_k(sel, TOP_K)
    w2 = jax.nn.softmax(v, axis=-1) * p_top
    ids = g_idx * EXP_PER_GROUP + e_idx
    comb = jnp.einsum('tk,tke->te', w2, jax.nn.one_hot(ids, N_EXP, dtype=jnp.float32)).astype(h.dtype)
    y = jnp.zeros_like(xt)
    for e in range(N_EXP):
        he = jax.nn.silu(xt @ e_gate[e]) * (xt @ e_up[e])
        y = y + comb[:, e:e + 1] * (he @ e_down[e])
    return y.reshape(b_, s_, d_)

def second_inputs(seed: int = 0) -> dict:
    key = jax.random.key(seed)
    ks = jax.random.split(key, 24)
    f32 = jnp.float32
    L = DEPTH

    def nrm(k, shape, scale):
        return jax.random.normal(k, shape, f32) * scale

    u = jax.random.uniform(ks[10], (L, LRU_WIDTH), f32, 0.9, 0.999)
    s = u ** (1.0 / RG_C)
    lam = jnp.log(s) - jnp.log1p(-s)
    return {
        'x': nrm(ks[0], (BATCH, SEQ, D_MODEL), 1.0),
        'norm1_g': 1.0 + nrm(ks[1], (L, D_MODEL), 0.02),
        'w_in': nrm(ks[2], (L, D_MODEL, IN_COLS), D_MODEL ** -0.5),
        'pool_w': nrm(ks[3], (L, POOL_GROUPS, POOL_GROUP_DIM, POOL_GROUP_DIM), POOL_GROUP_DIM ** -0.5),
        'pool_scale': 1.0 + nrm(ks[4], (L, POOL_WIDTH), 0.02),
        'conv_w': nrm(ks[5], (L, CONV_WIDTH, LRU_WIDTH), CONV_WIDTH ** -0.5),
        'conv_b': nrm(ks[6], (L, LRU_WIDTH), 0.01),
        'rg_w_r': nrm(ks[7], (L, LRU_HEADS, LRU_HEAD_DIM, LRU_HEAD_DIM), LRU_HEAD_DIM ** -0.5),
        'rg_b_r': nrm(ks[8], (L, LRU_WIDTH), 0.01),
        'rg_w_i': nrm(ks[9], (L, LRU_HEADS, LRU_HEAD_DIM, LRU_HEAD_DIM), LRU_HEAD_DIM ** -0.5),
        'rg_b_i': nrm(ks[11], (L, LRU_WIDTH), 0.01),
        'rg_lambda': lam,
        'proj_a': nrm(ks[12], (L, POOL_WIDTH, D_MODEL), POOL_WIDTH ** -0.5),
        'proj_b': nrm(ks[13], (L, LRU_WIDTH, D_MODEL), LRU_WIDTH ** -0.5),
        'w_out': nrm(ks[14], (L, D_MODEL, D_MODEL), D_MODEL ** -0.5),
        'norm2_g': 1.0 + nrm(ks[15], (L, D_MODEL), 0.02),
        'router_group_w': nrm(ks[16], (L, D_MODEL, N_GROUPS), D_MODEL ** -0.5),
        'router_group_b': nrm(ks[17], (L, N_GROUPS), 0.01),
        'router_expert_w': nrm(ks[18], (L, D_MODEL, N_EXP), D_MODEL ** -0.5),
        'router_expert_b': nrm(ks[19], (L, N_EXP), 0.01),
        'exp_w_gate': nrm(ks[20], (L, N_EXP, D_MODEL, D_EXPERT_2), D_MODEL ** -0.5),
        'exp_w_up': nrm(ks[21], (L, N_EXP, D_MODEL, D_EXPERT_2), D_MODEL ** -0.5),
        'exp_w_down': nrm(ks[22], (L, N_EXP, D_EXPERT_2, D_MODEL), D_EXPERT_2 ** -0.5),
        'norm_f_g': 1.0 + nrm(ks[23], (D_MODEL,), 0.02),
    }

def second_block(x, norm1_g, w_in, pool_w, pool_scale, conv_w, conv_b, rg_w_r, rg_b_r, rg_w_i, rg_b_i,
              rg_lambda, proj_a, proj_b, w_out, norm2_g, router_group_w, router_group_b,
              router_expert_w, router_expert_b, exp_w_gate, exp_w_up, exp_w_down, norm_f_g):
    o1 = POOL_WIDTH
    o2 = o1 + LRU_WIDTH
    o3 = o2 + LRU_WIDTH
    o4 = o3 + D_MODEL
    for l in range(DEPTH):
        h = rms_norm(x, norm1_g[l])
        z = h @ w_in[l]
        u_pool, u_lru, u_gate = z[..., :o1], z[..., o1:o2], z[..., o2:o3]
        g_a = jax.nn.sigmoid(z[..., o3:o4])
        g_b = jax.nn.sigmoid(z[..., o4:])
        y_a = pooling_mixer(u_pool, pool_w[l], pool_scale[l]) @ proj_a[l]
        y_b = rglru_mixer(u_lru, u_gate, conv_w[l], conv_b[l], rg_w_r[l], rg_b_r[l],
                          rg_w_i[l], rg_b_i[l], rg_lambda[l]) @ proj_b[l]
        x = x + (g_a * y_a + g_b * y_b) @ w_out[l]
        h2 = rms_norm(x, norm2_g[l])
        x = x + hier_moe_2(h2, router_group_w[l], router_group_b[l], router_expert_w[l],
                         router_expert_b[l], exp_w_gate[l], exp_w_up[l], exp_w_down[l])
    return rms_norm(x, norm_f_g)


def setup_inputs(seed=0):
    out = dict(first_inputs(seed))
    for name, value in second_inputs(seed + 1).items():
        if name != "x":
            out[name + "_2"] = value
    return out


def reference(
    x, c, norm1_g, norm2_g, w_ada, b_ada, w_in, lam_re, lam_im, log_step, s5_b_re, s5_b_im,
    s5_c_re, s5_c_im, s5_d, w_glu, b_glu, conv_w, a_log, dt_bias, gdn_norm_g, w_out,
    w_router_grp, w_router_exp, w_gate, w_up, w_down, normf_g, norm1_g_2, w_in_2, pool_w_2,
    pool_scale_2, conv_w_2, conv_b_2, rg_w_r_2, rg_b_r_2, rg_w_i_2, rg_b_i_2, rg_lambda_2,
    proj_a_2, proj_b_2, w_out_2, norm2_g_2, router_group_w_2, router_group_b_2,
    router_expert_w_2, router_expert_b_2, exp_w_gate_2, exp_w_up_2, exp_w_down_2, norm_f_g_2,
):
    x = first_block(
        x, c, norm1_g, norm2_g, w_ada, b_ada, w_in, lam_re, lam_im, log_step, s5_b_re, s5_b_im,
        s5_c_re, s5_c_im, s5_d, w_glu, b_glu, conv_w, a_log, dt_bias, gdn_norm_g, w_out,
        w_router_grp, w_router_exp, w_gate, w_up, w_down, normf_g,
    )
    return second_block(
        x, norm1_g_2, w_in_2, pool_w_2, pool_scale_2, conv_w_2, conv_b_2, rg_w_r_2, rg_b_r_2,
        rg_w_i_2, rg_b_i_2, rg_lambda_2, proj_a_2, proj_b_2, w_out_2, norm2_g_2,
        router_group_w_2, router_group_b_2, router_expert_w_2, router_expert_b_2, exp_w_gate_2,
        exp_w_up_2, exp_w_down_2, norm_f_g_2,
    )


_drawn_inputs = setup_inputs


def setup_inputs(seed=0):
    import zlib

    import numpy as np

    out = dict(_drawn_inputs(seed))
    spreads = {}
    factors = {'norm1_g': 4.548,
     'norm2_g': 3.514,
     'lam_re': 200.0,
     'lam_im': 3.611,
     'log_step': 3.437,
     's5_b_re': 6.56,
     's5_b_im': 21.31,
     's5_c_re': 4.607,
     's5_c_im': 21.588,
     'w_glu': 4.769,
     'b_glu': 55.818,
     'gdn_norm_g': 5.109,
     'norm1_g_2': 3.65,
     'pool_scale_2': 4.949,
     'conv_b_2': 2.999,
     'rg_b_r_2': 32.185,
     'rg_b_i_2': 8.0,
     'norm2_g_2': 2.743,
     'router_group_b_2': 5.149,
     'router_expert_b_2': 24.968,
     'norm_f_g_2': 22.9}
    for name, (base, spread) in spreads.items():
        noise = np.random.default_rng([zlib.crc32(name.encode()), seed]).standard_normal(out[name].shape)
        drawn = base * np.exp(spread * noise) if base else spread * noise
        out[name] = jnp.asarray(drawn.astype(out[name].dtype))
    for name, factor in factors.items():
        out[name] = (out[name] * factor).astype(out[name].dtype)
    return out
```

```python
from contextlib import ExitStack

import concourse.bass as bass
from concourse import mybir

F32 = mybir.dt.float32
I32 = mybir.dt.int32
U32 = mybir.dt.uint32
ALU = mybir.AluOpType
ACT = mybir.ActivationFunctionType
AX = mybir.AxisListType

P = 128
T = 512
NT = T // P
D = 1024
KD = D // P
HALF = 512
EPS = 1e-6
EXTRA = 7
LAST_SEM = 256
CH = 64
NH = 4
G16 = 16
NS5 = 16
TWO_PI = 6.283185307179586
ROUND = 12582912.0
BIG = 1.0e30

COLS = [("c", 8), ("s5_d", 4), ("b_glu", 4), ("conv_w", 48), ("gdn_g", 1), ("lam_re", 16), ("lam_im", 16),
        ("log_step", 16), ("b_re", 256), ("b_im", 256), ("c_re", 256), ("c_im", 256), ("w_gates", 64),
        ("w_router", 288), ("pool_scale", 4), ("conv_w2", 32), ("conv_b2", 8), ("b_r", 8), ("b_i", 8),
        ("lam2", 8), ("w_router2", 160)]
NCOL = sum(n for _, n in COLS)
ROWS = [("a_log", 4), ("dt_bias", 4), ("router_b2", 20)]
NROW = sum(n for _, n in ROWS)

ADA0, NADA = 0, 12
IN0, NIN = 12, 5
GLU0 = 17
OUT0 = 18
MOE0 = 20
IN20, NIN2 = 84, 9
PRA0 = 93
PRB0 = 94
OUT20 = 96
RG0 = 98
MOE20 = 100
NCHUNK = 164
POOL_AFTER = [26, 28, 30, 32]
RING = 4
SLOT = 4096


class Shared:
    pass


class Experts:

    def __init__(self, tag, NE, NG, EG, NJ, HV, first, router, bias, gu, dn, gate, x_rows, y_rows, got, got_over, got_back):
        self.tag, self.NE, self.NG, self.EG, self.NJ, self.HV = tag, NE, NG, EG, NJ, HV
        self.first, self.router, self.bias, self.gu, self.dn, self.gate = first, router, bias, gu, dn, gate
        self.x_rows, self.y_rows = x_rows, y_rows
        self.got, self.got_over, self.got_back = got, got_over, got_back


class Steps:

    def __init__(self, eng, sem):
        self.eng, self.sem, self.n = eng, sem, 0

    def mark(self, ins):
        ins.then_inc(self.sem, 1)
        self.n = self.n + 1
        return self.n

    def link(self, ins):
        self.eng.wait_ge(self.sem, self.mark(ins))


def at(ap, name):
    o = 0
    for n, k in COLS:
        if n == name:
            return ap[:, o:o + k]
        o += k


def row_at(ap, name):
    o = 0
    for n, k in ROWS:
        if n == name:
            return ap[:, o:o + k]
        o += k


def over(ap, k):
    return ap.unsqueeze(2).to_broadcast([ap.shape[0], ap.shape[1], k])


def rows_of(ap, k):
    return ap.unsqueeze(1).to_broadcast([ap.shape[0], k, ap.shape[1]])


class Stream:

    def __init__(self, m, src):
        self.m, self.src, self.stop = m, src, len(src)

    def load(self, sp, lo, hi):
        for n in range(lo, min(hi, self.stop)):
            s, dst = n % RING, self.m.ring[:, n % RING, :]
            if self.src[n] is None:
                continue
            if n >= RING:
                sp.wait_ge(self.m.w_free[s], self.frees(n - RING))
            src = self.src[n]
            sp.dma_start(dst[:, 0:src.shape[1]], src).then_inc(self.m.w_ready[s], 16)

    def loads(self, n):
        return 16 * sum(1 for k in range(n % RING, n + 1, RING) if self.src[k] is not None)

    def frees(self, n):
        return self.loads(n) // 16

    def wait(self, pe, n):
        pe.wait_ge(self.m.w_ready[n % RING], self.loads(n))

    def free(self, ins, n):
        ins.then_inc(self.m.w_free[n % RING], 1)

    def wait_used(self, eng, n):
        eng.wait_ge(self.m.w_free[n % RING], self.frees(n))


def constants_and_modulation(nc, m, d):
    with ExitStack() as ctx:
        sem = lambda name: ctx.enter_context(nc.semaphore(name))
        c_bc = ctx.enter_context(nc.sbuf_tensor("c_bc", [P, KD, P], F32))
        c_act = ctx.enter_context(nc.sbuf_tensor("c_act", [P, KD], F32))
        b_row = ctx.enter_context(nc.sbuf_tensor("b_row", [1, 6 * D], F32))
        g_row = ctx.enter_context(nc.sbuf_tensor("g_row", [P, 2, D], F32))
        ps = ctx.enter_context(nc.psum_tensor("ada_ps", [P, 2, HALF], F32))
        par, const, c_done, cb_done = sem("a_par"), sem("a_const"), sem("a_cact"), sem("a_cbc")
        mm, ev, g_in, own, pool_own = sem("a_mm"), sem("a_ev"), sem("a_g"), sem("a_own"), sem("a_pool")

        with nc.Block() as block:

            @block.sync
            def _(sp):
                m.stream.load(sp, ADA0, ADA0 + 2)
                sp.wait_ge(par, 48)
                m.stream.load(sp, ADA0 + 2, RING)
                sp.dma_start(m.x[:], d["x"]).then_inc(m.x_in, 16)
                with sp.Fori(1, NADA // RING) as r:
                    for s in range(RING):
                        sp.wait_ge(m.w_free[s], r)
                        sp.dma_start(m.ring[:, s, :], d["w_ada"][bass.ds(r * RING + s, 1)].rearrange("o p n -> (o p) n"))\
                          .then_inc(m.w_ready[s], 16)
                m.stream.load(sp, IN0, IN0 + RING)

            @block.gpsimd
            def _(pool):
                st = Steps(pool, pool_own)
                pool.memset(m.ones[:], 1.0).then_inc(const, 1)
                st.link(pool.memset(m.ident[:], 0.0))
                pool.affine_select(out=m.ident[:], in_=m.ident[:], compare_op=ALU.not_equal, fill=1.0, base=0,
                                   pattern=[[-1, P]], channel_multiplier=1).then_inc(const, 1)
                st.link(pool.memset(m.tri[:], 1.0))
                pool.affine_select(out=m.tri[:], in_=m.tri[:], compare_op=ALU.is_gt, fill=0.0, base=0,
                                   pattern=[[1, P]], channel_multiplier=-1).then_inc(const, 1)
                st.link(pool.memset(m.upto[:], 1.0))
                st.link(pool.affine_select(out=m.upto[:], in_=m.upto[:], compare_op=ALU.is_ge, fill=0.0, base=0,
                                           pattern=[[1, P]], channel_multiplier=-1))
                st.link(pool.memset(m.upto[0:CH, CH:P], 0.0))
                st.link(pool.memset(m.same[:], 1.0))
                st.link(pool.memset(m.same[0:CH, CH:P], 0.0))
                st.link(pool.memset(m.same[CH:P, 0:CH], 0.0))
                for n in range(6):
                    b = 1 << n
                    mk = m.level[:, n, :]
                    v = mk.rearrange("p (q r) -> p q r", r=2 * b)
                    st.link(pool.memset(mk, 1.0))
                    st.link(pool.affine_select(out=v, in_=v, compare_op=ALU.is_ge, fill=0.0, base=0,
                                               pattern=[[-2 * b, P // (2 * b)], [0, 2 * b]], channel_multiplier=1))
                    st.link(pool.affine_select(out=v, in_=v, compare_op=ALU.is_gt, fill=0.0, base=b,
                                               pattern=[[2 * b, P // (2 * b)], [0, 2 * b]], channel_multiplier=-1))
                    st.link(pool.memset(v[:, :, 0:b], 0.0))
                st.link(pool.iota(m.t_row[:], [[1, T]], base=0, channel_multiplier=0,
                                  allow_small_or_imprecise_dtypes=True))

            @block.scalar
            def _(act):
                act.dma_start(m.par[:], d["cols"]).then_inc(par, 16)
                act.dma_start(b_row[:], d["b_ada"]).then_inc(par, 16)
                act.dma_start(m.rows[:], d["rows"].partition_broadcast(P)).then_inc(par, 16)
                act.dma_start(g_row[:, 0, :], d["norm1_g"].partition_broadcast(P)).then_inc(g_in, 16)
                act.dma_start(g_row[:, 1, :], d["norm2_g"].partition_broadcast(P)).then_inc(g_in, 16)
                act.wait_ge(par, 48)
                act.activation(c_act[:], at(m.par, "c"), ACT.Silu).then_inc(c_done, 1)
                with act.Fori(0, NADA // 2) as r:
                    for b in range(2):
                        act.wait_ge(mm, r * 2 + b + 1)
                        act.activation(m.mods[:, bass.ds((r * 2 + b) * HALF, HALF)], ps[:, b, :], ACT.Copy)\
                           .then_inc(ev, 1)

            @block.vector
            def _(dve):
                dve.wait_ge(c_done, 1)
                dve.wait_ge(const, 1)
                for k in range(KD):
                    dve.tensor_scalar(c_bc[:, k, :], m.ones[:], c_act[:, k:k + 1], None, ALU.mult).then_inc(cb_done, 1)
                dve.wait_ge(ev, NADA)
                dve.wait_ge(g_in, 32)
                for n in range(2):
                    sc = m.mods[:, (3 * n + 1) * D:(3 * n + 2) * D]
                    dve.scalar_tensor_tensor(sc, sc, 1.0, g_row[:, n, :], ALU.add, ALU.mult).then_inc(own, 1)
                dve.wait_ge(own, 2)

            @block.tensor
            def _(pe):
                pe.wait_ge(cb_done, KD)
                pe.wait_ge(par, 48)
                pe.wait_ge(const, 1)

                def chunks(r):
                    for s in range(RING):
                        pe.wait_ge(m.w_ready[s], r * 16 + 16)
                        if not (isinstance(r, int) and s < 2):
                            pe.wait_ge(ev, r * RING + s - 1)
                        w = m.ring[:, s, :].rearrange("p (k n) -> p k n", k=KD)
                        for k in range(KD):
                            last = pe.matmul(ps[:, s % 2, :], c_bc[:, k, :], w[:, k, :], start=(k == 0), stop=False)
                        m.stream.free(last, s)
                        last = pe.matmul(ps[:, s % 2, :], m.ones[0:1, :], b_row[0:1, bass.ds((r * RING + s) * HALF, HALF)],
                                         start=False, stop=True)
                        last.then_inc(mm, 1)

                chunks(0)
                with pe.Fori(1, NADA // RING) as r:
                    chunks(r)


def norm_and_transpose(nc, m, tag, scale, shift, rows_out, a_t, g_src=None, final_out=None, in_place=False):
    with ExitStack() as ctx:
        sem = lambda name: ctx.enter_context(nc.semaphore(f"{tag}_{name}"))
        sb = lambda name, shape: ctx.enter_context(nc.sbuf_tensor(f"{tag}_{name}", shape, F32))
        a = sb("a", [P, 2, D])
        junk = sb("junk", [P, D])
        ss, ms, rstd = sb("ss", [P, NT]), sb("ms", [P, NT]), sb("rstd", [P, NT])
        if g_src is not None:
            g_row = sb("g", [P, D])
            scale = g_row[:]
        ps = ctx.enter_context(nc.psum_tensor(f"{tag}_ps", [P, 4, HALF], F32))
        sq, inv, root, a_ready, tr, ev_a, ev_v = (sem(n) for n in ("sq", "inv", "root", "a", "tr", "eva", "evv"))
        own, g_in, stored = sem("own"), sem("gin"), [sem("st0"), sem("st1")]
        out = rows_out if final_out is None else final_out
        turned = final_out is None and not in_place

        with nc.Block() as block:

            @block.sync
            def _(sp):
                if g_src is not None:
                    sp.dma_start(g_row[:], g_src.partition_broadcast(P)).then_inc(g_in, 16)
                if out is not None:
                    for t in range(NT):
                        sp.wait_ge(a_ready, t + 1)
                        sp.dma_start(out[t * P:(t + 1) * P, :], a[:, t % 2, :]).then_inc(stored[t % 2], 16)
                    for s in stored:
                        sp.wait_ge(s, 16 * NT // 2)

            @block.scalar
            def _(act):
                act.wait_ge(m.x_in, 16)
                for t in range(NT):
                    if t:
                        act.wait_ge(sq, t)
                    act.activation(junk[:], m.x[:, t, :], ACT.Square, accum_out=ss[:, t:t + 1]).then_inc(sq, 1)
                act.wait_ge(inv, 1)
                act.activation(rstd[:], ms[:], ACT.Sqrt).then_inc(root, 1)
                if turned:
                    for u in range(0, 2 * NT, 2):
                        act.wait_ge(tr, u + 1)
                        t, h = u // 2, u % 2
                        act.activation(a_t[:, 4 * h:4 * h + 4, t * P:(t + 1) * P],
                                       ps[:, u % 4, :].rearrange("p (k n) -> p k n", k=4), ACT.Copy).then_inc(ev_a, 1)

            @block.vector
            def _(dve):
                st = Steps(dve, own)
                dve.wait_ge(sq, NT)
                st.link(dve.tensor_scalar(ms[:], ss[:], 1.0 / D, EPS, ALU.mult, ALU.add))
                dve.reciprocal(ms[:], ms[:]).then_inc(inv, 1)
                dve.wait_ge(root, 1)
                if g_src is not None:
                    dve.wait_ge(g_in, 16)
                for t in range(NT):
                    if t >= 2 and turned:
                        dve.wait_ge(tr, 2 * (t - 1))
                    if t >= 2 and out is not None:
                        dve.wait_ge(stored[t % 2], 16)
                    to = m.x[:, t, :] if in_place else a[:, t % 2, :]
                    row = dve.scalar_tensor_tensor(to, m.x[:, t, :], rstd[:, t:t + 1], scale, ALU.mult, ALU.mult)
                    if shift is not None:
                        st.link(row)
                        row = dve.tensor_tensor(a[:, t % 2, :], a[:, t % 2, :], shift, ALU.add)
                    row.then_inc(a_ready, 1)
                    if t and turned:
                        u = 2 * t - 1
                        dve.wait_ge(tr, u + 1)
                        dve.tensor_copy(a_t[:, 4:8, (t - 1) * P:t * P],
                                        ps[:, u % 4, :].rearrange("p (k n) -> p k n", k=4)).then_inc(ev_v, 1)
                if turned:
                    dve.wait_ge(tr, 2 * NT)
                    dve.tensor_copy(a_t[:, 4:8, (NT - 1) * P:NT * P],
                                    ps[:, 3, :].rearrange("p (k n) -> p k n", k=4)).then_inc(ev_v, 1)

            @block.tensor
            def _(pe):
                if not turned:
                    return
                for t in range(NT):
                    pe.wait_ge(a_ready, t + 1)
                    for h in range(2):
                        u = 2 * t + h
                        if u >= 4:
                            pe.wait_ge((ev_a, ev_v)[h], t - 1)
                        for k in range(4):
                            c = 4 * h + k
                            last = pe.transpose(ps[:, u % 4, k * P:(k + 1) * P], a[:, t % 2, c * P:(c + 1) * P], m.ident[:])
                        last.then_inc(tr, 1)


def project_and_s5(nc, m, d):
    with ExitStack() as ctx:
        sem = lambda name: ctx.enter_context(nc.semaphore(f"s5_{name}"))
        sb = lambda name, shape: ctx.enter_context(nc.sbuf_tensor(f"s5_{name}", shape, F32))
        sc = sb("sc", [P, 20, NS5])
        (STEP, XR, RHO1, TH, K, R, HS, SN, CH2, BRE, BIM, DEN, CR, CI, RHO, TURN, T0, T1, T2, T3) = \
            (sc[:, n, :] for n in range(20))
        prod = [m.spare.rearrange("p (n t) -> p n t", n=4), sb("prod", [P, 4, T])[:]]
        wide = m.spare[:, 0:1024].rearrange("p (r n c) -> p r n c", r=2, n=NS5)
        bb = m.spare[:, 1024:1536].rearrange("p (r n c) -> p r n c", r=2, n=NS5)
        tb = m.spare[:, 1536:1792].rearrange("p (n c) -> p n c", n=NS5)
        b_t = sb("b_t", [P, 2, 4, P])
        c_t = sb("c_t", [P, 2, NS5, 32])
        tables = sb("tables", [P, 4, T])
        cos, sin = tables[:, 0:2, :], tables[:, 2:4, :]
        turn, near = sb("turn", [P, T]), sb("near", [P, T])
        zre, zim = sb("zre", [P, T]), sb("zim", [P, T])
        half_pi = sb("half_pi", [P, 1])
        dst = [m.u_t[:, n, :] for n in range(4)] + [m.qkv[:, n, :] for n in range(12)] + [m.z_t[:, n, :] for n in range(4)]
        pp = ctx.enter_context(nc.psum_tensor("s5_pp", [P, 2, HALF], F32))
        pb = ctx.enter_context(nc.psum_tensor("s5_pb", [P, 4, HALF], F32))
        py = ctx.enter_context(nc.psum_tensor("s5_py", [P, 2, HALF], F32))
        own, aown, lam_a, lam_v, pool_own = sem("own"), sem("aown"), sem("lam_a"), sem("lam_v"), sem("pown")
        wide_ready, btr, b_ready = sem("wide"), sem("btr"), sem("bready")
        turn_ready, table, table_used, bu, bu_used = sem("turn"), sem("table"), sem("tused"), sem("bu"), sem("buused")
        prods, prods_used, y_used, gel, gel_mm, sig, yout = \
            (sem(n) for n in ("prods", "pused", "yused", "gel", "gmm", "sig", "yout"))

        mm, copied, gm, gev, zeroed, filled = (sem(n) for n in ("mm", "copied", "gm", "gev", "zeroed", "filled"))
        zero = prod[1].rearrange("p n t -> p (n t)")[:, 0:D]

        def product_of(eng, n):
            if n % 4 == 3:
                m.stream.wait_used(eng, IN0 + n // 4)
            else:
                eng.wait_ge(mm, n // 4 * 3 + n % 4 + 1)

        with nc.Block() as block:

            @block.sync
            def _(sp):
                sp.wait_ge(zeroed, 1)
                for n in range(EXTRA):
                    sp.dma_start(d["y_rows"][(32 + n) * P:(33 + n) * P, :], zero).then_inc(filled, 16)
                m.stream.load(sp, IN0 + RING, GLU0 + 1 + RING)

            @block.gpsimd
            def _(pool):
                pool.memset(zero, 0.0).then_inc(zeroed, 1)

            @block.vector
            def _(dve):
                st = Steps(dve, own)
                tt, ts = dve.tensor_tensor, dve.tensor_scalar
                dve.wait_ge(gm, 1)
                dve.tensor_copy(m.gates[:], pb[:, 0, 0:NT * 8]).then_inc(gev, 1)
                dve.wait_ge(lam_a, 1)
                lre, lim = at(m.par, "lam_re"), at(m.par, "lam_im")
                st.link(tt(XR, lre, STEP, ALU.mult))
                st.link(tt(TH, lim, STEP, ALU.mult))
                st.link(ts(T0, XR, 1.0 / 256, None, ALU.mult))
                st.link(ts(T1, T0, 1.0 / 6, 1.0, ALU.mult, ALU.add))
                for c in (5.0, 4.0, 3.0, 2.0):
                    st.link(tt(T1, T1, T0, ALU.mult))
                    st.link(ts(T1, T1, 1.0 / c, 1.0, ALU.mult, ALU.add))
                st.link(tt(RHO1, T1, T0, ALU.mult))
                for _ in range(8):
                    st.link(dve.scalar_tensor_tensor(RHO1, RHO1, 2.0, RHO1, ALU.add, ALU.mult))
                st.link(ts(RHO, RHO1, 1.0, None, ALU.add))
                st.link(ts(T0, TH, 1.0 / TWO_PI, None, ALU.mult))
                st.link(ts(K, T0, ROUND, -ROUND, ALU.add, ALU.add))
                st.link(tt(TURN, T0, K, ALU.subtract))
                dve.tensor_scalar(R, TURN, TWO_PI, None, ALU.mult).then_inc(lam_v, 1)
                dve.wait_ge(lam_a, 2)
                st.link(tt(T0, HS, HS, ALU.mult))
                st.link(ts(T0, T0, -2.0, None, ALU.mult))
                st.link(dve.scalar_tensor_tensor(T1, T0, 1.0, RHO1, ALU.add, ALU.mult))
                st.link(tt(BRE, T1, T0, ALU.add))
                st.link(tt(BIM, RHO, SN, ALU.mult))
                st.link(tt(T0, lre, lre, ALU.mult))
                st.link(tt(T1, lim, lim, ALU.mult))
                st.link(tt(DEN, T0, T1, ALU.add))
                st.link(dve.reciprocal(DEN, DEN))
                st.link(tt(T0, BRE, lre, ALU.mult))
                st.link(tt(T1, BIM, lim, ALU.mult))
                st.link(tt(T0, T0, T1, ALU.add))
                st.link(tt(CR, T0, DEN, ALU.mult))
                st.link(tt(T0, BIM, lre, ALU.mult))
                st.link(tt(T1, BRE, lim, ALU.mult))
                st.link(tt(T0, T0, T1, ALU.subtract))
                st.link(tt(CI, T0, DEN, ALU.mult))
                br = at(m.par, "b_re").rearrange("p (n h) -> p n h", h=G16)
                bi = at(m.par, "b_im").rearrange("p (n h) -> p n h", h=G16)
                for n, (x, y, op) in enumerate(((br, bi, ALU.subtract), (bi, br, ALU.add))):
                    st.link(tt(bb[:, n], x, over(CR, G16), ALU.mult))
                    st.link(tt(tb[:], y, over(CI, G16), ALU.mult))
                    st.link(tt(bb[:, n], bb[:, n], tb[:], op))
                st.link(dve.memset(wide[:], 0.0))
                for g in range(2):
                    s = slice(CH * g, CH * g + CH)
                    st.link(dve.tensor_copy(wide[s, 0, :, G16 * g:G16 * g + G16], bb[s, 0]))
                    dve.tensor_copy(wide[s, 1, :, G16 * g:G16 * g + G16], bb[s, 1]).then_inc(wide_ready, 1)
                st.link(dve.memset(c_t[:], 0.0))
                cr = at(m.par, "c_re").rearrange("p (n h) -> p n h", h=G16)
                ci = at(m.par, "c_im").rearrange("p (n h) -> p n h", h=G16)
                for g in range(2):
                    s = slice(CH * g, CH * g + CH)
                    h = slice(G16 * g, G16 * g + G16)
                    st.link(ts(c_t[s, 0, :, h], cr[s], 1.0, None, ALU.mult))
                    st.link(ts(c_t[s, 1, :, h], ci[s], -1.0, None, ALU.mult))
                for n in range(4):
                    dve.wait_ge(btr, n + 1)
                    dve.tensor_copy(b_t[:, 0:2, n, :], pb[:, n, 0:2 * P].rearrange("p (a c) -> p a c", a=2))\
                       .then_inc(b_ready, 1)

                def add_skip(q):
                    dve.wait_ge(prods_used, 4 * q + 4)
                    dve.scalar_tensor_tensor(m.u_t[:, q, :], m.u_t[:, q, :], at(m.par, "s5_d")[:, q:q + 1], py[:, q % 2, :],
                                             ALU.mult, ALU.add).then_inc(y_used, 1)

                dve.wait_ge(copied, 4)
                dve.wait_ge(filled, 16 * EXTRA)
                for i in range(NS5 + 1):
                    if i < NS5:
                        if i:
                            dve.wait_ge(table, 2 * i)
                        st.link(ts(turn[:], m.t_row[:], TURN[:, i:i + 1], None, ALU.mult))
                        st.link(ts(near[:], turn[:], ROUND, -ROUND, ALU.add, ALU.add))
                        tt(turn[:], turn[:], near[:], ALU.subtract).then_inc(turn_ready, 1)
                    if i == 0:
                        continue
                    j = i - 1
                    cs, sn = cos[:, j % 2, :], sin[:, j % 2, :]
                    b_re, b_im = pb[:, 2 * (j % 2), :], pb[:, 2 * (j % 2) + 1, :]
                    dve.wait_ge(table, 2 * j + 2)
                    dve.wait_ge(bu, j + 1)
                    if j >= 2:
                        dve.wait_ge(prods_used, j - 1)
                    t0, t1 = prod[j % 2][:, 0, :], prod[j % 2][:, 1, :]
                    st.link(tt(t0, b_re, cs, ALU.mult))
                    st.link(tt(t1, b_im, sn, ALU.mult))
                    st.link(tt(t0, t0, t1, ALU.add))
                    st.link(dve.tensor_tensor_scan(zre[:], RHO[:, j:j + 1].to_broadcast([P, T]), t0, 0.0, ALU.mult, ALU.add))
                    st.link(tt(t0, b_im, cs, ALU.mult))
                    bu_last = tt(t1, b_re, sn, ALU.mult)
                    bu_last.then_inc(bu_used, 1)
                    dve.wait_ge(bu_used, j + 1)
                    st.link(tt(t0, t0, t1, ALU.subtract))
                    st.link(dve.tensor_tensor_scan(zim[:], RHO[:, j:j + 1].to_broadcast([P, T]), t0, 0.0, ALU.mult, ALU.add))
                    for n, (tab, sign, z) in enumerate(((cs, 1.0, zre), (sn, -1.0, zim), (sn, 1.0, zre), (cs, 1.0, zim))):
                        dve.scalar_tensor_tensor(prod[j % 2][:, n, :], tab, sign, z[:], ALU.mult, ALU.mult).then_inc(prods, 1)
                    dve.wait_ge(prods, 4 * j + 4)
                    if i % 4 == 1 and i > 4:
                        add_skip((i - 5) // 4)
                add_skip(3)
                for q in range(4):
                    dve.wait_ge(sig, q + 1)
                    tt(m.y_t[:, q, :], m.u_t[:, q, :], prod[1][:, q, :], ALU.mult).then_inc(yout, 1)

            @block.scalar
            def _(act):
                st = Steps(act, aown)

                def copy_out(n):
                    product_of(act, n)
                    act.activation(dst[n], pp[:, n % 2, :], ACT.Copy).then_inc(copied, 1)

                st.link(act.activation(half_pi[:], m.ones[:, 0:1], ACT.Copy, scale=TWO_PI / 4))
                act.activation(STEP, at(m.par, "log_step"), ACT.Exp).then_inc(lam_a, 1)
                copy_out(0)
                copy_out(1)
                act.wait_ge(lam_v, 1)
                st.link(act.activation(HS, R, ACT.Sin, scale=0.5))
                act.activation(SN, R, ACT.Sin).then_inc(lam_a, 1)
                copy_out(2)
                copy_out(3)
                for i in range(NS5):
                    act.wait_ge(turn_ready, i + 1)
                    if i >= 2:
                        act.wait_ge(prods, 4 * (i - 1))
                    act.activation(sin[:, i % 2, :], turn[:], ACT.Sin, scale=TWO_PI).then_inc(table, 1)
                    st.link(act.activation(near[:], turn[:], ACT.Abs))
                    act.activation(cos[:, i % 2, :], near[:], ACT.Sin, scale=-TWO_PI, bias=half_pi[:]).then_inc(table, 1)
                    copy_out(4 + i)
                for q in range(4):
                    act.wait_ge(y_used, q + 1)
                    act.activation(m.u_t[:, q, :], m.u_t[:, q, :], ACT.Gelu_apprx_tanh).then_inc(gel, 1)
                for q in range(4):
                    if q == 3:
                        m.stream.wait_used(act, GLU0)
                    else:
                        act.wait_ge(gel_mm, q + 1)
                    act.activation(prod[1][:, q, :], pb[:, q, :], ACT.Sigmoid, bias=at(m.par, "b_glu")[:, q:q + 1])\
                       .then_inc(sig, 1)

            @block.tensor
            def _(pe):
                def product(n):
                    c, j = IN0 + n // 4, n % 4
                    w = m.ring[:, c % RING, :].rearrange("p (k n) -> p k n", k=KD)
                    if j == 0:
                        m.stream.wait(pe, c)
                    if n >= 2:
                        pe.wait_ge(copied, n - 1)
                    for k in range(KD):
                        last = pe.matmul(pp[:, n % 2, :], w[:, k, j * P:(j + 1) * P], m.a_t[:, k, :],
                                         start=(k == 0), stop=(k == KD - 1))
                    if j == 3:
                        m.stream.free(last, c)
                    else:
                        last.then_inc(mm, 1)

                for t in range(NT):
                    for k in range(KD):
                        last = pe.matmul(pb[:, 0, t * 8:t * 8 + 8], m.a_t[:, k, t * P:(t + 1) * P],
                                         at(m.par, "w_gates")[:, k * 8:k * 8 + 8], start=(k == 0), stop=(k == KD - 1))
                last.then_inc(gm, 1)
                for n in range(4):
                    product(n)
                pe.wait_ge(gev, 1)
                pe.wait_ge(wide_ready, 2)
                for n in range(4):
                    for r in range(2):
                        last = pe.transpose(pb[:, n, r * P:(r + 1) * P],
                                            wide[:, r, 4 * n:4 * n + 4, :].rearrange("p a b -> p (a b)"), m.ident[:])
                    last.then_inc(btr, 1)
                pe.wait_ge(b_ready, 4)

                def inputs(i):
                    s = slice(32 * (i % 4), 32 * (i % 4) + 32)
                    if i >= 2:
                        pe.wait_ge(bu_used, i - 1)
                    for r in range(2):
                        last = pe.matmul(pb[:, 2 * (i % 2) + r, :], b_t[s, r, i // 4, :], m.u_t[s, i // 4, :],
                                         start=True, stop=True)
                    last.then_inc(bu, 1)

                def outputs(i):
                    q, s = i // 4, slice(32 * (i % 4), 32 * (i % 4) + 32)
                    pe.wait_ge(prods, 4 * i + 4)
                    if i % 4 == 0 and q >= 2:
                        pe.wait_ge(y_used, q - 1)
                    for n, w in enumerate((0, 0, 1, 1)):
                        last = pe.matmul(py[s, q % 2, :], c_t[:, w, i, :], prod[i % 2][:, n, :], start=(n == 0), stop=(n == 3))
                    last.then_inc(prods_used, 1)

                pe.wait_ge(copied, 4)
                inputs(0)
                for i in range(NS5):
                    product(4 + i)
                    if i + 1 < NS5:
                        inputs(i + 1)
                    if i:
                        outputs(i - 1)
                outputs(NS5 - 1)
                pe.wait_ge(gel, 4)
                m.stream.wait(pe, GLU0)
                w = m.ring[:, GLU0 % RING, 0:2048].rearrange("p (k n) -> p k n", k=4)
                pe.wait_ge(bu_used, NS5)
                for q in range(4):
                    for k in range(4):
                        last = pe.matmul(pb[:, q, :], w[:, k, q * P:(q + 1) * P], m.u_t[:, k, :], start=(k == 0), stop=(k == 3))
                    if q == 3:
                        m.stream.free(last, GLU0)
                    else:
                        last.then_inc(gel_mm, 1)


def delta_rule(nc, m):
    with ExitStack() as ctx:
        sb = lambda name, shape: ctx.enter_context(nc.sbuf_tensor(f"dr_{name}", shape, F32))
        g = Shared()
        by_head = lambda ap: ap.rearrange("p t (h n) -> p t h n", h=NH)
        g.lt = by_head(sb("lt", [P, NT, HALF])[:])
        g.xt = by_head(sb("xt", [P, NT, HALF])[:])
        g.qk = by_head(sb("qk", [P, NT, HALF])[:])
        g.xi = by_head(m.spare.rearrange("p (t n) -> p t n", t=NT))
        g.w = by_head(m.u_t[:])
        g.s = sb("s", [P, 2, HALF])
        g.tmp = sb("tmp", [P, 2, HALF])
        g.col = sb("col", [P, 12, NT * NH])
        g.gl = sb("gl", [P, NT, NH, 2])
        g.ps = ctx.enter_context(nc.psum_tensor("dr_ps", [P, 8, HALF], F32))
        conv_and_gates(nc, m, g)
        decay_and_scores(nc, m, g)
        invert(nc, m, g)
        values(nc, m, g)
        recur(nc, m, g)
        gate_output(nc, m, g)


def conv_and_gates(nc, m, g):
    with ExitStack() as ctx:
        sem = lambda name: ctx.enter_context(nc.semaphore(f"cv_{name}"))
        conv, sil, sq, ssum, rec, root, normed = (sem(n) for n in ("conv", "sil", "sq", "ssum", "rec", "root", "normed"))
        own, aown, ga, gv, gm, gc, gd = (sem(n) for n in ("own", "aown", "ga", "gv", "gm", "gc", "gd"))
        tmp = m.y_t
        (AD, NAB, SP, G, BETA, GC, EGC, BG, DT, EKT, EA, REL) = (g.col[:, n, :] for n in range(12))
        gates = m.gates[:].rearrange("p (t n) -> p t n", t=NT)
        v3 = lambda ap: ap.rearrange("p (t h) -> p t h", t=NT)
        g.G, g.BETA, g.GC, g.BG, g.EKT = G, BETA, GC, BG, EKT
        with nc.Block() as block:

            @block.scalar
            def _(act):
                st = Steps(act, aown)
                act.activation(v3(BETA), gates[:, :, 4:8], ACT.Sigmoid).then_inc(ga, 1)
                for n in range(12):
                    act.wait_ge(conv, n + 1)
                    act.activation(m.qkv[:, n, :], tmp[:, 4 + n % 2, :], ACT.Silu).then_inc(sil, 1)
                act.wait_ge(gv, 1)
                st.link(act.activation(NAB, AD, ACT.Abs))
                st.link(act.activation(NAB, NAB, ACT.Exp, scale=-1.0))
                st.link(act.activation(SP, NAB, ACT.Ln, bias=1.0))
                act.activation(EA[:, 0:NH], row_at(m.rows, "a_log"), ACT.Exp).then_inc(ga, 1)
                act.wait_ge(gc, 1)
                act.activation(EGC, GC, ACT.Exp).then_inc(gd, 1)
                act.activation(EKT, DT, ACT.Exp).then_inc(gd, 1)
                for n in range(8):
                    act.wait_ge(sil, n + 1)
                    if n >= 2:
                        act.wait_ge(ssum, n - 1)
                    act.activation(tmp[:, 6 + n % 2, :], m.qkv[:, n, :], ACT.Square).then_inc(sq, 1)
                    if n:
                        act.wait_ge(rec, n)
                        act.activation(g.w[:, (n - 1) % 4], g.w[:, (n - 1) % 4], ACT.Sqrt).then_inc(root, 1)
                act.wait_ge(rec, 8)
                act.activation(g.w[:, 3], g.w[:, 3], ACT.Sqrt).then_inc(root, 1)

            @block.vector
            def _(dve):
                st = Steps(dve, own)
                ts, tt, stt = dve.tensor_scalar, dve.tensor_tensor, dve.scalar_tensor_tensor
                tt(v3(AD), gates[:, :, 0:4], rows_of(row_at(m.rows, "dt_bias"), NT), ALU.add).then_inc(gv, 1)
                taps = at(m.par, "conv_w")
                for n in range(12):
                    o, q = tmp[:, 4 + n % 2, :], m.qkv[:, n, :]
                    w = lambda k: taps[:, 4 * n + k:4 * n + k + 1]
                    if n >= 2:
                        dve.wait_ge(sil, n - 1)
                    st.link(ts(o, q, w(3), None, ALU.mult))
                    st.link(stt(o[:, 1:], q[:, :T - 1], w(2), o[:, 1:], ALU.mult, ALU.add))
                    st.link(stt(o[:, 2:], q[:, :T - 2], w(1), o[:, 2:], ALU.mult, ALU.add))
                    stt(o[:, 3:], q[:, :T - 3], w(0), o[:, 3:], ALU.mult, ALU.add).then_inc(conv, 1)
                dve.wait_ge(ga, 2)
                st.link(stt(SP, AD, 0.0, SP, ALU.max, ALU.add))
                tt(v3(G), v3(SP), rows_of(EA[:, 0:NH], NT), ALU.mult).then_inc(gv, 1)
                dve.wait_ge(gv, 2)
                st.link(ts(G, G, -1.0, None, ALU.mult))
                dve.tensor_scalar(REL, G, 1.0, None, ALU.mult).then_inc(gv, 1)
                dve.wait_ge(gm, 1)
                st.link(dve.tensor_copy(GC, g.ps[:, 2, 0:16]))
                tt(DT, g.ps[:, 2, 16:32], GC, ALU.subtract).then_inc(gc, 1)
                dve.wait_ge(gd, 1)
                st.link(tt(BG, BETA, EGC, ALU.mult))
                for n in range(9):
                    if n < 8:
                        dve.wait_ge(ssum, n + 1)
                        r = g.w[:, n % 4].rearrange("p h n -> p (h n)")
                        st.link(ts(r, g.ps[:, n % 2, :], EPS, None, ALU.add))
                        dve.reciprocal(r, r).then_inc(rec, 1)
                    if n:
                        dve.wait_ge(root, n)
                        r = g.w[:, (n - 1) % 4].rearrange("p h n -> p (h n)")
                        q = m.qkv[:, n - 1, :]
                        stt(q, q, P ** -0.5 if n - 1 < 4 else 1.0, r, ALU.mult, ALU.mult).then_inc(normed, 1)

            @block.tensor
            def _(pe):
                pe.wait_ge(gv, 3)
                pe.matmul(g.ps[:, 2, 0:16], m.upto[:], G, start=True, stop=True)
                pe.matmul(g.ps[:, 2, 16:32], m.same[:], G, start=True, stop=True).then_inc(gm, 1)
                for n in range(8):
                    pe.wait_ge(sq, n + 1)
                    if n >= 2:
                        pe.wait_ge(rec, n - 1)
                    pe.matmul(g.ps[:, n % 2, :], m.ones[:], tmp[:, 6 + n % 2, :], start=True, stop=True).then_inc(ssum, 1)


def decay_and_scores(nc, m, g):
    with ExitStack() as ctx:
        sem = lambda name: ctx.enter_context(nc.semaphore(f"ds_{name}"))
        bc, bc_used, rows, scores, diff, dec, masked, lt, x1, xi_ps, xi_ev, egr, qd, own, pown = \
            (sem(n) for n in ("bc", "bcu", "rows", "sc", "diff", "dec", "msk", "lt", "x1", "xp", "xe", "egr", "qd", "own", "pown"))
        gb, bb = m.y_t[:, 4, :], m.y_t[:, 5, :]
        eg = m.y_t[:, 6, :]
        h4 = lambda ap: ap.rearrange("p (h n) -> p h n", h=NH)
        with nc.Block() as block:

            @block.gpsimd
            def _(pool):
                st = Steps(pool, pown)
                for t in range(NT):
                    if t:
                        pool.wait_ge(rows, t)
                    pool.tensor_copy(h4(gb), over(g.G[:, 4 * t:4 * t + 4], P)).then_inc(bc, 1)
                    pool.tensor_copy(h4(bb), over(g.BETA[:, 4 * t:4 * t + 4], P)).then_inc(bc, 1)
                    pool.wait_ge(dec, t + 1)
                    d = h4(g.tmp[:, t % 2, :])
                    pool.tensor_tensor(d, d, rows_of(m.upto[:], NH), ALU.mult).then_inc(masked, 1)
                    pool.wait_ge(lt, t + 1)
                    st.link(pool.tensor_tensor(g.xt[:, t], g.lt[:, t], rows_of(m.level[:, 0, :], NH), ALU.mult))
                    pool.tensor_tensor(g.xt[:, t], rows_of(m.ident[:], NH), g.xt[:, t], ALU.subtract).then_inc(x1, 1)

            @block.tensor
            def _(pe):
                for t in range(NT):
                    b = 4 * (t % 2)
                    s = slice(t * P, (t + 1) * P)
                    pe.wait_ge(bc, 2 * t + 2)
                    if t >= 2:
                        pe.wait_ge(lt, t - 1)
                        pe.wait_ge(egr, t - 1)
                    for h in range(NH):
                        n = slice(h * P, (h + 1) * P)
                        pe.matmul(g.ps[:, b, n], gb[:, n], m.upto[:], start=True, stop=True)
                        last = pe.matmul(g.ps[:, b + 1, n], bb[:, n], m.ident[:], start=True, stop=True)
                    last.then_inc(rows, 1)
                    for h in range(NH):
                        n = slice(h * P, (h + 1) * P)
                        k = m.qkv[:, 4 + h, s]
                        pe.matmul(g.ps[:, b + 2, n], k, k, start=True, stop=True)
                        last = pe.matmul(g.ps[:, b + 3, n], k, m.qkv[:, h, s], start=True, stop=True)
                    last.then_inc(scores, 1)
                for t in range(NT):
                    pe.wait_ge(x1, t + 1)
                    pe.wait_ge(lt, NT)
                    for h in range(NH):
                        last = pe.transpose(g.ps[:, t, h * P:(h + 1) * P], g.xt[:, t, h, :], m.ident[:])
                    last.then_inc(xi_ps, 1)

            @block.vector
            def _(dve):
                st = Steps(dve, own)
                tt = dve.tensor_tensor
                for t in range(NT):
                    b = 4 * (t % 2)
                    d = h4(g.tmp[:, t % 2, :])
                    dve.wait_ge(rows, t + 1)
                    if t >= 2:
                        dve.wait_ge(lt, t - 1)
                    st.link(tt(d, h4(g.ps[:, b, :]), over(g.GC[:, 4 * t:4 * t + 4], P), ALU.subtract))
                    dve.tensor_scalar(d, d, 0.0, None, ALU.min).then_inc(diff, 1)
                    dve.wait_ge(egr, t + 1)
                    dve.wait_ge(scores, t + 1)
                    q = m.qkv[:, 0:NH, t * P:(t + 1) * P]
                    dve.tensor_copy(g.gl[:, t], h4(eg).rearrange("p h (c n) -> p h c n", c=2)[:, :, :, CH - 1]).then_inc(qd, 1)
                    dve.tensor_tensor(q, q, h4(eg), ALU.mult).then_inc(qd, 1)
                    dve.wait_ge(masked, t + 1)
                    st.link(tt(g.lt[:, t], h4(g.ps[:, b + 2, :]), d, ALU.mult))
                    st.link(tt(g.qk[:, t], h4(g.ps[:, b + 3, :]), d, ALU.mult))
                    tt(g.lt[:, t], g.lt[:, t], h4(g.ps[:, b + 1, :]), ALU.mult).then_inc(lt, 1)

            @block.scalar
            def _(act):
                for t in range(NT):
                    b = 4 * (t % 2)
                    act.wait_ge(diff, t + 1)
                    d = g.tmp[:, t % 2, :]
                    act.activation(d, d, ACT.Exp).then_inc(dec, 1)
                    if t:
                        act.wait_ge(qd, 2 * t)
                    act.activation(eg, g.ps[:, b, :], ACT.Exp).then_inc(egr, 1)
                for t in range(NT):
                    act.wait_ge(xi_ps, t + 1)
                    act.activation(g.xi[:, t], g.ps[:, t, :].rearrange("p (h n) -> p h n", h=NH), ACT.Copy).then_inc(xi_ev, 1)


def invert(nc, m, g):
    LV = 5
    steps = [(lv, t) for lv in range(1, LV + 1) for t in range(NT)]
    with ExitStack() as ctx:
        sem = lambda name: ctx.enter_context(nc.semaphore(f"iv_{name}"))
        cm_ready, cx, w_ev, upd, done, pown = (sem(n) for n in ("cm", "cx", "wev", "upd", "done", "pown"))
        cm = m.y_t[:, 4:6, :]
        h4 = lambda ap: ap.rearrange("p (h n) -> p h n", h=NH)
        with nc.Block() as block:

            @block.gpsimd
            def _(pool):
                for i, (lv, t) in enumerate(steps):
                    if i >= 2:
                        pool.wait_ge(cx, i - 1)
                    pool.tensor_tensor(h4(cm[:, i % 2, :]), g.lt[:, t], rows_of(m.level[:, lv, :], NH), ALU.mult)\
                        .then_inc(cm_ready, 1)

            @block.tensor
            def _(pe):
                def first(i):
                    lv, t = steps[i]
                    pe.wait_ge(cm_ready, i + 1)
                    if i >= 2:
                        pe.wait_ge(w_ev, i - 1)
                    if lv > 1:
                        pe.wait_ge(done, 2 * (i - NT) + 2)
                    for h in range(NH):
                        last = pe.matmul(g.ps[:, i % 2, h * P:(h + 1) * P], cm[:, i % 2, h * P:(h + 1) * P], g.xi[:, t, h, :],
                                         start=True, stop=True)
                    last.then_inc(cx, 1)

                def second(i):
                    lv, t = steps[i]
                    pe.wait_ge(w_ev, i + 1)
                    if i >= 2:
                        pe.wait_ge(done, 2 * (i - 2) + 2)
                    for h in range(NH):
                        n = slice(h * P, (h + 1) * P)
                        pe.matmul(g.ps[:, 2 + 2 * (i % 2), n], g.xt[:, t, h, :], g.w[:, t, h, :], start=True, stop=True)
                        last = pe.matmul(g.ps[:, 3 + 2 * (i % 2), n], g.w[:, t, h, :], g.xt[:, t, h, :], start=True, stop=True)
                    last.then_inc(upd, 1)

                first(0)
                for i in range(len(steps)):
                    if i + 1 < len(steps):
                        first(i + 1)
                    second(i)

            @block.scalar
            def _(act):
                for i, (lv, t) in enumerate(steps):
                    act.wait_ge(cx, i + 1)
                    if lv > 1:
                        act.wait_ge(upd, i - NT + 1)
                    act.activation(g.w[:, t], h4(g.ps[:, i % 2, :]), ACT.Copy).then_inc(w_ev, 1)

            @block.vector
            def _(dve):
                for i, (lv, t) in enumerate(steps):
                    dve.wait_ge(upd, i + 1)
                    dve.tensor_tensor(g.xi[:, t], g.xi[:, t], h4(g.ps[:, 2 + 2 * (i % 2), :]), ALU.subtract).then_inc(done, 1)
                    dve.tensor_tensor(g.xt[:, t], g.xt[:, t], h4(g.ps[:, 3 + 2 * (i % 2), :]), ALU.subtract).then_inc(done, 1)


def values(nc, m, g):
    with ExitStack() as ctx:
        sem = lambda name: ctx.enter_context(nc.semaphore(f"vl_{name}"))
        tr, sc, mm, ev = (sem(n) for n in ("tr", "sc", "mm", "ev"))
        vb, kb = m.y_t[:, 4:6, :], m.y_t[:, 6:8, :]
        h4 = lambda ap: ap.rearrange("p (h n) -> p h n", h=NH)
        with nc.Block() as block:

            @block.tensor
            def _(pe):
                def turn(t):
                    s = slice(t * P, (t + 1) * P)
                    if t >= 2:
                        pe.wait_ge(sc, 3 * (t - 1))
                    for h in range(NH):
                        n = slice(h * P, (h + 1) * P)
                        pe.transpose(g.ps[:, 2 * (t % 2), n], m.qkv[:, 8 + h, s], m.ident[:])
                        last = pe.transpose(g.ps[:, 2 * (t % 2) + 1, n], m.qkv[:, 4 + h, s], m.ident[:])
                    last.then_inc(tr, 1)

                turn(0)
                for t in range(NT):
                    if t + 1 < NT:
                        turn(t + 1)
                    pe.wait_ge(sc, 3 * t + 3)
                    if t >= 2:
                        pe.wait_ge(ev, 2 * (t - 1))
                    b = 4 + 2 * (t % 2)
                    for h in range(NH):
                        n = slice(h * P, (h + 1) * P)
                        pe.matmul(g.ps[:, b, n], g.xt[:, t, h, :], vb[:, t % 2, n], start=True, stop=True)
                        last = pe.matmul(g.ps[:, b + 1, n], kb[:, t % 2, n], g.xt[:, t, h, :], start=True, stop=True)
                    last.then_inc(mm, 1)

            @block.vector
            def _(dve):
                for t in range(NT):
                    dve.wait_ge(tr, t + 1)
                    if t >= 2:
                        dve.wait_ge(mm, t - 1)
                    c = slice(4 * t, 4 * t + 4)
                    pv, pk = h4(g.ps[:, 2 * (t % 2), :]), h4(g.ps[:, 2 * (t % 2) + 1, :])
                    dve.tensor_tensor(h4(vb[:, t % 2, :]), pv, over(g.BETA[:, c], P), ALU.mult).then_inc(sc, 1)
                    dve.tensor_tensor(h4(kb[:, t % 2, :]), pk, over(g.BG[:, c], P), ALU.mult).then_inc(sc, 1)
                    dve.tensor_tensor(g.lt[:, t], pk, over(g.EKT[:, c], P), ALU.mult).then_inc(sc, 1)

            @block.scalar
            def _(act):
                for t in range(NT):
                    act.wait_ge(mm, t + 1)
                    b = 4 + 2 * (t % 2)
                    act.activation(g.xi[:, t], h4(g.ps[:, b, :]), ACT.Copy).then_inc(ev, 1)
                    act.activation(g.w[:, t], h4(g.ps[:, b + 1, :]), ACT.Copy).then_inc(ev, 1)


def recur(nc, m, g):
    NCH = T // CH
    with ExitStack() as ctx:
        sem = lambda name: ctx.enter_context(nc.semaphore(f"rc_{name}"))
        vp, vn_r, so, oo, o_ev, sg_r, s_r = (sem(n) for n in ("vp", "vn", "so", "oo", "oev", "sg", "s"))
        vn = g.tmp
        h4 = lambda ap: ap.rearrange("p (h n) -> p h n", h=NH)
        with nc.Block() as block:

            @block.tensor
            def _(pe):
                for c in range(NCH):
                    t, s = c // 2, slice(CH * (c % 2), CH * (c % 2) + CH)
                    col = slice(CH * c, CH * c + CH)
                    state = g.s[:, c % 2, :]
                    if c:
                        pe.wait_ge(s_r, c)
                        for h in range(NH):
                            n = slice(h * P, (h + 1) * P)
                            last = pe.matmul(g.ps[s, c % 2, n], g.w[:, t, h, s], state[:, n], start=True, stop=True)
                        last.then_inc(vp, 1)
                        if c >= 2:
                            pe.wait_ge(o_ev, c - 1)
                    po = h4(g.ps[:, 2 + c % 2, 0:NH * CH])
                    pe.wait_ge(vn_r, c + 1)
                    if c < NCH - 1:
                        for h in range(NH):
                            n = slice(h * P, (h + 1) * P)
                            last = pe.matmul(g.ps[:, 4 + c % 2, n], g.lt[s, t, h, :], vn[s, c % 2, n], start=True, stop=True)
                        last.then_inc(so, 1)
                    for h in range(NH):
                        n = slice(h * P, (h + 1) * P)
                        if c:
                            pe.matmul(po[:, h, :], state[:, n], m.qkv[:, h, col], start=True, stop=False)
                        last = pe.matmul(po[:, h, :], vn[s, c % 2, n], g.qk[s, t, h, s], start=(c == 0), stop=True)
                    last.then_inc(oo, 1)

            @block.vector
            def _(dve):
                for c in range(NCH):
                    t, s = c // 2, slice(CH * (c % 2), CH * (c % 2) + CH)
                    if c >= 2:
                        dve.wait_ge(oo, c - 1)
                    if c == 0:
                        dve.tensor_copy(h4(vn[s, 0, :]), g.xi[s, t]).then_inc(vn_r, 1)
                    else:
                        dve.wait_ge(vp, c)
                        dve.tensor_tensor(h4(vn[s, c % 2, :]), g.xi[s, t], h4(g.ps[s, c % 2, :]), ALU.subtract).then_inc(vn_r, 1)
                    if c < NCH - 1:
                        if c == 0:
                            dve.wait_ge(so, 1)
                            dve.tensor_copy(g.s[:, 1, :], g.ps[:, 4, :]).then_inc(s_r, 1)
                        else:
                            dve.wait_ge(oo, c)
                            dve.tensor_tensor(h4(g.s[:, (c + 1) % 2, :]), h4(g.s[:, c % 2, :]), over(g.gl[:, t, :, c % 2], P),
                                              ALU.mult).then_inc(sg_r, 1)
                            dve.wait_ge(sg_r, c)
                            dve.wait_ge(so, c + 1)
                            dve.tensor_tensor(g.s[:, (c + 1) % 2, :], g.s[:, (c + 1) % 2, :], g.ps[:, 4 + c % 2, :], ALU.add)\
                               .then_inc(s_r, 1)

            @block.scalar
            def _(act):
                for c in range(NCH):
                    act.wait_ge(oo, c + 1)
                    act.activation(m.y_t[:, 4:8, CH * c:CH * c + CH], h4(g.ps[:, 2 + c % 2, 0:NH * CH]), ACT.Copy)\
                       .then_inc(o_ev, 1)


def gate_output(nc, m, g):
    with ExitStack() as ctx:
        sem = lambda name: ctx.enter_context(nc.semaphore(f"go_{name}"))
        sq, ssum, rec, root, zs, own, fin = (sem(n) for n in ("sq", "ssum", "rec", "root", "zs", "own", "fin"))
        sqb = [g.tmp[:, 0, :], g.tmp[:, 1, :], g.s[:, 0, :], g.s[:, 1, :]]
        flat = lambda ap: ap.rearrange("p h n -> p (h n)")
        with nc.Block() as block:

            @block.scalar
            def _(act):
                for h in range(NH):
                    act.activation(sqb[h], m.y_t[:, 4 + h, :], ACT.Square).then_inc(sq, 1)
                for h in range(NH):
                    act.activation(m.z_t[:, h, :], m.z_t[:, h, :], ACT.Silu).then_inc(zs, 1)
                for h in range(NH):
                    act.wait_ge(rec, h + 1)
                    act.activation(g.w[:, h], g.w[:, h], ACT.Sqrt).then_inc(root, 1)

            @block.tensor
            def _(pe):
                for h in range(NH):
                    pe.wait_ge(sq, h + 1)
                    pe.matmul(g.ps[:, h, :], m.ones[:], sqb[h], start=True, stop=True).then_inc(ssum, 1)

            @block.vector
            def _(dve):
                st = Steps(dve, own)
                for h in range(NH):
                    dve.wait_ge(ssum, h + 1)
                    r = flat(g.w[:, h])
                    st.link(dve.tensor_scalar(r, g.ps[:, h, :], 1.0 / P, EPS, ALU.mult, ALU.add))
                    dve.reciprocal(r, r).then_inc(rec, 1)
                for h in range(NH):
                    dve.wait_ge(root, h + 1)
                    y = m.y_t[:, 4 + h, :]
                    st.link(dve.scalar_tensor_tensor(y, y, at(m.par, "gdn_g"), flat(g.w[:, h]), ALU.mult, ALU.mult))
                    dve.wait_ge(zs, h + 1)
                    dve.tensor_tensor(y, y, m.z_t[:, h, :], ALU.mult).then_inc(fin, 1)


def mix_out(nc, m, chunk0=OUT0, gate=None):
    with ExitStack() as ctx:
        sem = lambda name: ctx.enter_context(nc.semaphore(f"mo{chunk0}_{name}"))
        ps = ctx.enter_context(nc.psum_tensor(f"mo{chunk0}_ps", [P, 4, HALF], F32))
        tmp = ctx.enter_context(nc.sbuf_tensor(f"mo{chunk0}_tmp", [P, 2, HALF], F32))
        mm, sc, ev = sem("mm"), sem("sc"), sem("ev")
        with nc.Block() as block:

            @block.sync
            def _(sp):
                if gate is None:
                    m.stream.load(sp, chunk0 + RING + 2, chunk0 + RING + 4)
                m.stream.load(sp, chunk0 + RING, chunk0 + RING + 2)

            @block.tensor
            def _(pe):
                for n in range(2 * NT):
                    c, t = n // NT, n % NT
                    if t == 0:
                        m.stream.wait(pe, chunk0 + c)
                    if n >= 4:
                        pe.wait_ge(ev, n - 3)
                    w = m.ring[:, (chunk0 + c) % RING, :].rearrange("p (k n) -> p k n", k=KD)
                    for k in range(KD):
                        last = pe.matmul(ps[:, n % 4, :], m.y_t[:, k, t * P:(t + 1) * P], w[:, k, :], start=(k == 0),
                                         stop=(k == KD - 1))
                    if t == NT - 1:
                        m.stream.free(last, chunk0 + c)
                    else:
                        last.then_inc(mm, 1)

            @block.vector
            def _(dve):
                for n in range(2 * NT):
                    c, t = n // NT, n % NT
                    if t == NT - 1:
                        m.stream.wait_used(dve, chunk0 + c)
                    else:
                        dve.wait_ge(mm, c * (NT - 1) + t + 1)
                    x = m.x[:, t, c * HALF:(c + 1) * HALF]
                    y = ps[:, n % 4, :]
                    if gate is not None:
                        if n >= 2:
                            dve.wait_ge(ev, n - 1)
                        y = tmp[:, n % 2, :]
                        dve.tensor_tensor(y, ps[:, n % 4, :], gate[:, c * HALF:(c + 1) * HALF], ALU.mult).then_inc(sc, 1)
                        dve.wait_ge(sc, n + 1)
                    dve.tensor_tensor(x, x, y, ALU.add).then_inc(ev, 1)


def route(nc, m, c):
    NE, NG, EG = c.NE, c.NG, c.EG
    NL, NS = NG + NE, NE + EXTRA
    with ExitStack() as ctx:
        sem = lambda name: ctx.enter_context(nc.semaphore(f"{c.tag}r_{name}"))
        sb = lambda name, shape, dt=F32: ctx.enter_context(nc.sbuf_tensor(f"{c.tag}r_{name}", shape, dt))
        ps = ctx.enter_context(nc.psum_tensor(f"{c.tag}r_ps", [P, 3, HALF], F32))
        logit, ready, a_done, v_done, own, rank, hot, table = (sem(n) for n in ("lg", "ready", "act", "v", "own", "rank", "hot", "tab"))
        gl, goh, gex, gpen = (sb(n, [P, NT, NG]) for n in ("gl", "goh", "gex", "gpen"))
        el, oh1, oh2, cand, slots = (sb(n, [P, NT, NE]) for n in ("el", "oh1", "oh2", "cand", "slots"))
        both = sb("both", [P, NT, NE])
        one = sb("one", [P, 12, NT])
        (GMAX, GI, PSUM_, V1, I1, V2, I2, E2, R, DV, RLO, TMP) = (one[:, n, :] for n in range(12))
        iot, iot_far = sb("iot", [P, NS]), sb("iotf", [P, NS])
        r128 = sb("r128", [P, P])
        ids = sb("ids", [P, NT])
        ext = sb("ext", [P, 6, NE])
        (CNT, EX, INC, OFF1, DOFF, ZER) = (ext[:, n, :] for n in range(6))
        slot2, job2, lo2 = sb("slot2", [P, NT, 2]), sb("job2", [P, NT, 2]), sb("lo2", [P, NT, 2])
        roh, joh = sb("roh", [P, NT * 2, P]), sb("joh", [P, NT * 2, NS])
        ovf = sb("ovf", [1, 1 + EXTRA])
        in_x = sb("in_x", [1, 2, NE])
        flat = lambda ap: ap.rearrange("p a b -> p (a b)")
        e4 = lambda ap: ap.rearrange("p t (g e) -> p (t g) e", g=NG)
        with nc.Block() as block:

            @block.gpsimd
            def _(pool):
                for ap, pat, base, chan in ((iot[:], [[1, NS]], 0, 0), (iot_far[:], [[1, NS]], 64, 0), (r128[:], [[1, P]], 0, 0),
                                            (ids[:], [[P, NT]], 0, 1), (OFF1, [[P, NE]], 0, 0)):
                    pool.iota(ap, pat, base=base, channel_multiplier=chan, allow_small_or_imprecise_dtypes=True).then_inc(ready, 1)

            @block.tensor
            def _(pe):
                w = at(m.par, c.router).rearrange("p (k n) -> p k n", k=KD)
                for t in range(NT):
                    for k in range(KD):
                        last = pe.matmul(ps[:, 0, t * NL:(t + 1) * NL], m.a_t[:, k, t * P:(t + 1) * P], w[:, k, :],
                                         start=(k == 0), stop=(k == KD - 1))
                last.then_inc(logit, 1)
                pe.wait_ge(v_done, 2)
                for t in range(NT):
                    for i in range(t + 1):
                        pe.matmul(ps[:, 1, t * NE:(t + 1) * NE], (m.tri if i == t else m.ones)[:], both[:, i, :],
                                  start=(i == 0), stop=(i == t))
                for i in range(NT):
                    last = pe.matmul(ps[:, 1, NT * NE:(NT + 1) * NE], m.ones[:], both[:, i, :], start=(i == 0), stop=(i == NT - 1))
                last.then_inc(rank, 1)
                pe.wait_ge(hot, 1)
                for i in range(2 * NT):
                    last = pe.matmul(ps[:, 2, 0:NS], roh[:, i, :], joh[:, i, :], start=(i == 0), stop=(i == 2 * NT - 1))
                last.then_inc(table, 1)

            @block.scalar
            def _(act):
                act.wait_ge(v_done, 1)
                act.activation(gex[:], gex[:], ACT.Exp).then_inc(a_done, 1)
                act.wait_ge(v_done, 3)
                act.activation(E2, DV, ACT.Exp).then_inc(a_done, 1)

            @block.vector
            def _(dve):
                st = Steps(dve, own)
                tt, ts, stt, red = dve.tensor_tensor, dve.tensor_scalar, dve.scalar_tensor_tensor, dve.tensor_reduce

                def first_of(values, best, index, hot_out, tmp, n):
                    st.link(tt(tmp, values, over(best, n), ALU.is_ge))
                    st.link(stt(tmp, tmp, -64.0, rows_of(iot_far[:, 0:n], NT), ALU.mult, ALU.add))
                    st.link(red(index, tmp, AX.X, ALU.min))
                    st.link(tt(hot_out, rows_of(iot[:, 0:n], NT), over(index, n), ALU.is_equal))

                dve.wait_ge(ready, 5)
                dve.wait_ge(logit, 1)
                lg = ps[:, 0, 0:NT * NL].rearrange("p (t n) -> p t n", t=NT)
                if c.bias is None:
                    st.link(dve.tensor_copy(gl[:], lg[:, :, 0:NG]))
                    st.link(dve.tensor_copy(el[:], lg[:, :, NG:NL]))
                else:
                    st.link(tt(gl[:], lg[:, :, 0:NG], rows_of(c.bias[:, 0:NG], NT), ALU.add))
                    st.link(tt(el[:], lg[:, :, NG:NL], rows_of(c.bias[:, NG:NL], NT), ALU.add))
                st.link(red(GMAX, gl[:], AX.X, ALU.max))
                tt(gex[:], gl[:], over(GMAX, NG), ALU.subtract).then_inc(v_done, 1)
                first_of(gl[:], GMAX, GI, goh[:], gpen[:], NG)
                st.link(ts(gpen[:], goh[:], BIG, -BIG, ALU.mult, ALU.add))
                st.link(tt(e4(el[:]), e4(el[:]), over(flat(goh[:]), EG), ALU.mult))
                st.link(tt(e4(el[:]), e4(el[:]), over(flat(gpen[:]), EG), ALU.add))
                st.link(red(V1, el[:], AX.X, ALU.max))
                first_of(el[:], V1, I1, oh1[:], cand[:], NE)
                st.link(stt(el[:], oh1[:], -3 * BIG, el[:], ALU.mult, ALU.add))
                st.link(red(V2, el[:], AX.X, ALU.max))
                first_of(el[:], V2, I2, oh2[:], cand[:], NE)
                tt(both[:], oh1[:], oh2[:], ALU.add).then_inc(v_done, 1)
                tt(DV, V2, V1, ALU.subtract).then_inc(v_done, 1)
                dve.wait_ge(a_done, 2)
                st.link(red(PSUM_, gex[:], AX.X, ALU.add))
                st.link(ts(R, E2, 1.0, None, ALU.add))
                st.link(tt(R, R, PSUM_, ALU.mult))
                st.link(dve.reciprocal(c.wt[:, :, 0], R))
                st.link(tt(c.wt[:, :, 1], c.wt[:, :, 0], E2, ALU.mult))
                dve.wait_ge(rank, 1)
                st.link(dve.tensor_copy(CNT, ps[:, 1, NT * NE:(NT + 1) * NE]))
                st.link(ts(EX, CNT, float(P), None, ALU.is_gt))
                for q in (2.0, 3.0):
                    st.link(stt(EX, CNT, q * P, EX, ALU.is_gt, ALU.add))
                st.link(dve.tensor_tensor_scan(INC, m.ones[:, 0:NE], EX, 0.0, ALU.mult, ALU.add))
                st.link(tt(DOFF, INC, EX, ALU.subtract))
                st.link(dve.tensor_copy(ovf[:, 0:1], INC[0:1, NE - 1:NE]))
                for n in range(EXTRA):
                    st.link(ts(in_x[:, 0], DOFF[0:1], float(n), None, ALU.is_le))
                    st.link(stt(in_x[:, 1], INC[0:1], float(n), in_x[:, 0], ALU.is_gt, ALU.mult))
                    st.link(tt(in_x[:, 1], in_x[:, 1], iot[0:1, 0:NE], ALU.mult))
                    st.link(red(ovf[:, 1 + n:2 + n], in_x[:, 1], AX.X, ALU.add))
                st.link(dve.tensor_copy(c.over[:], ovf[:]))
                st.link(ts(DOFF, DOFF, float(P), float((NE - 1) * P), ALU.mult, ALU.add))
                st.link(tt(DOFF, DOFF, OFF1, ALU.subtract))
                rk = ps[:, 1, 0:NT * NE].rearrange("p (t e) -> p t e", t=NT)
                st.link(ts(cand[:], rk, float(P), None, ALU.is_ge))
                st.link(tt(cand[:], cand[:], rows_of(DOFF, NT), ALU.mult))
                st.link(tt(slots[:], rk, rows_of(OFF1, NT), ALU.add))
                st.link(tt(slots[:], slots[:], cand[:], ALU.add))
                for k, oh in enumerate((oh1, oh2)):
                    st.link(tt(cand[:], slots[:], oh[:], ALU.mult))
                    st.link(red(slot2[:, :, k], cand[:], AX.X, ALU.add))
                st.link(dve.tensor_copy(c.slot[:], slot2[:]))
                st.link(ts(job2[:], slot2[:], 63.5, 1.0 / P, ALU.subtract, ALU.mult))
                st.link(ts(job2[:], job2[:], ROUND, -ROUND, ALU.add, ALU.add))
                st.link(stt(lo2[:], job2[:], -float(P), slot2[:], ALU.mult, ALU.add))
                st.link(tt(roh[:], rows_of(r128[:], 2 * NT), over(flat(lo2[:]), P), ALU.is_equal))
                st.link(tt(joh[:], rows_of(iot[:], 2 * NT), over(flat(job2[:]), NS), ALU.is_equal))
                j3 = joh[:].rearrange("p (t k) n -> p t (k n)", t=NT)
                tt(j3, j3, over(ids[:], 2 * NS), ALU.mult).then_inc(hot, 1)
                dve.wait_ge(table, 1)
                st.link(dve.tensor_copy(c.token[:], ps[:, 2, 0:NS]))


def experts(nc, m, c):
    NJ, HV = c.NJ, c.HV
    with ExitStack() as ctx:
        sem = lambda name: ctx.enter_context(nc.semaphore(f"{c.tag}x_{name}"))
        sb = lambda name, shape, dt=F32: ctx.enter_context(nc.sbuf_tensor(f"{c.tag}x_{name}", shape, dt))
        xg, xt = sb("xg", [P, 2, D]), sb("xt", [P, KD, P])
        hs, h, ht, ysb = sb("hs", [P, 256]), sb("h", [P, 256]), sb("ht", [P, 2, P]), sb("y", [P, 2, D])
        idx = sb("idx", [P, 2], U32)
        ps = ctx.enter_context(nc.psum_tensor(f"{c.tag}x_ps", [P, 8, HALF], F32))
        got = c.got
        stored = [sem("st0"), sem("st1")]
        idx_r, tr, xa, xd, sl, hr, htr, hte, ya, yd = (sem(n) for n in ("idx", "tr", "xa", "xd", "sl", "hr", "htr", "hte", "ya", "yd"))
        GS, DS = [c.first % RING, (c.first + 2) % RING], [(c.first + 1) % RING, (c.first + 3) % RING]
        G0, D0 = ([m.stream.frees(c.first - RING + o + 2 * u) for u in range(2)] for o in (0, 1))
        with nc.Block() as block:

            def up_done(eng, j, u):
                eng.wait_ge(m.w_free[GS[u]], (j - u) // 2 + 1 + G0[u])

            def down_done(eng, j, u):
                eng.wait_ge(m.w_free[DS[u]], (j - u) // 2 + 1 + D0[u])

            @block.sync
            def _(sp):
                def loads(j, u):
                    up_done(sp, j - 2, u)
                    sp.dma_start(m.ring[:, GS[u], :], c.gu[bass.ds(j, 1)].rearrange("o p n -> (o p) n")).then_inc(m.w_ready[GS[u]], 16)
                    down_done(sp, j - 2, u)
                    sp.dma_start(m.ring[:, DS[u], 0:2048], c.dn[bass.ds(j, 1)].rearrange("o p n -> (o p) n"))\
                      .then_inc(m.w_ready[DS[u]], 16)

                def store(i, v):
                    sp.wait_ge(ya, i + 1)
                    sp.wait_ge(yd, i + 1)
                    sp.dma_start(c.y_rows[bass.ds(i * P, P), :], ysb[:, v, :]).then_inc(stored[v], 16)

                with sp.Fori(0, NJ // 2 - 1) as i:
                    for u in range(2):
                        loads(i * 2 + 2 + u, u)
                        if HV == 1:
                            store(i * 2 + u, u)
                    if HV == 2:
                        store(i, 0)
                if HV == 1:
                    store(NJ - 2, 0)
                    store(NJ - 1, 1)
                    sp.wait_ge(stored[0], 16 * NJ // 2)
                    sp.wait_ge(stored[1], 16 * NJ // 2)
                else:
                    store(NJ // 2 - 1, 0)
                    sp.wait_ge(stored[0], 16 * NJ // 2)
                m.stream.load(sp, c.first + 2 * NJ, c.first + 2 * NJ + RING)

            @block.gpsimd
            def _(pool):
                def gather(i, v):
                    pool.tensor_copy(idx[:, v:v + 1], c.token[:, bass.ds(i, 1)]).then_inc(idx_r, 1)
                    pool.drain()
                    pool.indirect_dma_start(xg[:, v, :], None, c.x_rows, bass.IndirectOffsetOnAxis(idx[:, v:v + 1], 0))\
                        .then_inc(got[v], 16)

                NI = NJ // HV
                gather(0, 0)
                gather(1, 1)
                with pool.Fori(1, NI // 2) as i:
                    for v in range(2):
                        pool.wait_ge(tr, i * 2 + v - 1)
                        gather(i * 2 + v, v)

            @block.tensor
            def _(pe):
                def turn(i, v, r):
                    pe.wait_ge(got[v], r * 16 + 16)
                    pe.wait_ge(xa, i)
                    pe.wait_ge(xd, i)
                    for k in range(KD):
                        last = pe.transpose(ps[:, k // 4, (k % 4) * P:(k % 4 + 1) * P], xg[:, v, k * P:(k + 1) * P], m.ident[:])
                    last.then_inc(tr, 1)

                def up(j, u, i):
                    pe.wait_ge(m.w_ready[GS[u]], ((j - u) // 2 + 1 + G0[u]) * 16)
                    pe.wait_ge(xa, i + 1)
                    pe.wait_ge(xd, i + 1)
                    w = m.ring[:, GS[u], :].rearrange("p (k n) -> p k n", k=KD)
                    for k in range(KD):
                        last = pe.matmul(ps[:, 2 + u, :], xt[:, k, :], w[:, k, :], start=(k == 0), stop=(k == KD - 1))
                    last.then_inc(m.w_free[GS[u]], 1)

                def turn_h(j):
                    pe.wait_ge(hr, j + 1)
                    for k in range(2):
                        last = pe.transpose(ps[:, 4, k * P:(k + 1) * P], h[:, k * P:(k + 1) * P], m.ident[:])
                    last.then_inc(htr, 1)

                def down(j, u, i):
                    pe.wait_ge(m.w_ready[DS[u]], ((j - u) // 2 + 1 + D0[u]) * 16)
                    pe.wait_ge(hte, j + 1)
                    if HV == 1 or u == 0:
                        pe.wait_ge(ya, i)
                        pe.wait_ge(yd, i)
                    w = m.ring[:, DS[u], 0:2048].rearrange("p (k n) -> p k n", k=2)
                    for k in range(2):
                        for n in range(2):
                            last = pe.matmul(ps[:, 6 + n, :], ht[:, k, :], w[:, k, n * HALF:(n + 1) * HALF],
                                             start=(k == 0 and (HV == 1 or u == 0)), stop=(k == 1 and (HV == 1 or u == 1)))
                    last.then_inc(m.w_free[DS[u]], 1)

                if HV == 1:
                    def two(r):
                        for u, j, n in ((1, r * 2 + 1, r), (0, r * 2 + 2, r + 1)):
                            turn(j, u, n)
                            turn_h(j - 1)
                            up(j, u, j)
                            down(j - 1, 1 - u, j - 1)

                    turn(0, 0, 0)
                    up(0, 0, 0)
                    two(0)
                    with pe.Fori(1, NJ // 2 - 1) as r:
                        two(r)
                    turn(NJ - 1, 1, NJ // 2 - 1)
                    turn_h(NJ - 2)
                    up(NJ - 1, 1, NJ - 1)
                    down(NJ - 2, 0, NJ - 2)
                    turn_h(NJ - 1)
                    down(NJ - 1, 1, NJ - 1)
                else:
                    def halves(i, v, r, first=False):
                        turn(i, v, r)
                        if not first:
                            turn_h(i * 2 - 1)
                        up(i * 2, 0, i)
                        if not first:
                            down(i * 2 - 1, 1, i - 1)
                        turn_h(i * 2)
                        up(i * 2 + 1, 1, i)
                        down(i * 2, 0, i)

                    halves(0, 0, 0, True)
                    halves(1, 1, 0)
                    with pe.Fori(1, NJ // 4) as r:
                        for v in range(2):
                            halves(r * 2 + v, v, r)
                    turn_h(NJ - 1)
                    down(NJ - 1, 1, NJ // 2 - 1)

            def stores_before(i, v):
                return ((i - v) // 2) * 16 if HV == 1 else i * 16

            def run(eng, x_in, mid, h_t, y_out):
                if HV == 1:
                    x_in(0)
                    mid(0, 0)
                    x_in(1)
                    h_t(0)
                    mid(1, 1)
                    y_out(0, 0, 0, 0)
                    x_in(2)
                    h_t(1)
                    mid(2, 0)
                    y_out(1, 1, 1, 1)
                    with eng.Fori(1, NJ // 2 - 1) as r:
                        for u, j in ((1, r * 2 + 1), (0, r * 2 + 2)):
                            x_in(j)
                            h_t(j - 1)
                            mid(j, u)
                            y_out(j - 1, 1 - u, j - 1, 1 - u)
                    x_in(NJ - 1)
                    h_t(NJ - 2)
                    mid(NJ - 1, 1)
                    y_out(NJ - 2, 0, NJ - 2, 0)
                    h_t(NJ - 1)
                    y_out(NJ - 1, 1, NJ - 1, 1)
                else:
                    x_in(0)
                    mid(0, 0)
                    h_t(0)
                    mid(1, 1)
                    x_in(1)
                    h_t(1)
                    mid(2, 0)
                    y_out(1, 1, 0, 0)
                    h_t(2)
                    mid(3, 1)
                    with eng.Fori(2, NJ // 2) as i:
                        x_in(i)
                        h_t(i * 2 - 1)
                        mid(i * 2, 0)
                        y_out(i * 2 - 1, 1, i - 1, 0)
                        h_t(i * 2)
                        mid(i * 2 + 1, 1)
                    h_t(NJ - 1)
                    y_out(NJ - 1, 1, NJ // 2 - 1, 0)

            @block.scalar
            def _(act):
                def x_in(i):
                    act.wait_ge(tr, i + 1)
                    act.activation(xt[:, 0:4, :], ps[:, 0, :].rearrange("p (k n) -> p k n", k=4), ACT.Copy).then_inc(xa, 1)

                def silu(j, u):
                    up_done(act, j, u)
                    act.wait_ge(hr, j)
                    act.activation(hs[:], ps[:, 2 + u, 0:256], ACT.Silu).then_inc(sl, 1)

                def h_t(j):
                    act.wait_ge(htr, j + 1)
                    act.activation(ht[:].rearrange("p k n -> p (k n)"), ps[:, 4, 0:256], ACT.Copy).then_inc(hte, 1)

                def y_out(j, u, i, v):
                    down_done(act, j, u)
                    if not (isinstance(i, int) and i < 2):
                        act.wait_ge(stored[v], stores_before(i, v))
                    act.activation(ysb[:, v, 0:HALF], ps[:, 6, :], ACT.Copy).then_inc(ya, 1)

                run(act, x_in, silu, h_t, y_out)

            @block.vector
            def _(dve):
                def x_in(i):
                    dve.wait_ge(tr, i + 1)
                    dve.tensor_copy(xt[:, 4:8, :], ps[:, 1, :].rearrange("p (k n) -> p k n", k=4)).then_inc(xd, 1)

                def times_up(j, u):
                    dve.wait_ge(sl, j + 1)
                    dve.wait_ge(htr, j)
                    dve.tensor_tensor(h[:], hs[:], ps[:, 2 + u, 256:512], ALU.mult).then_inc(hr, 1)

                def y_out(j, u, i, v):
                    down_done(dve, j, u)
                    if not (isinstance(i, int) and i < 2):
                        dve.wait_ge(stored[v], stores_before(i, v))
                    dve.tensor_copy(ysb[:, v, HALF:D], ps[:, 7, :]).then_inc(yd, 1)

                run(dve, x_in, times_up, lambda j: None, y_out)


def overflow(nc, m, c):
    with ExitStack() as ctx:
        sem = lambda name: ctx.enter_context(nc.semaphore(f"{c.tag}o_{name}"))
        sb = lambda name, shape, dt=F32: ctx.enter_context(nc.sbuf_tensor(f"{c.tag}o_{name}", shape, dt))
        HV = c.HV
        wg, wd = sb("wg", [P, KD, HALF]), sb("wd", [P, 2, D])
        xg, xt = sb("xg", [P, D]), sb("xt", [P, KD, P])
        hs, h, ht, ysb = sb("hs", [P, 256]), sb("h", [P, 256]), sb("ht", [P, 2, P]), sb("y", [P, D])
        idx = sb("idx", [P, 1], U32)
        ps = ctx.enter_context(nc.psum_tensor(f"{c.tag}o_ps", [P, 8, HALF], F32))
        got = c.got_over
        wr, wr2, stored, idx_r, tr, xe, up, sl, hr, htr, hte, down, ye = \
            (sem(n) for n in ("wr", "wr2", "st", "idx", "tr", "xe", "up", "sl", "hr", "htr", "hte", "dn", "ye"))

        def tiles(eng, body):
            n = eng.value_load(c.over[0:1, 0:1], min_val=0, max_val=EXTRA)
            with eng.If(n > 0):
                with eng.Fori(0, n) as i:
                    body(i)

        with nc.Block() as block:

            @block.sync
            def _(sp):
                def body(i):
                    e = sp.value_load(c.over[0:1, bass.ds(i + 1, 1)], min_val=0, max_val=c.NE - 1)
                    row, begun = sp.snap((i + c.NE) * P), sp.snap(i + 1)
                    jobs = [sp.snap(e * HV + v) for v in range(HV)]
                    used = [sp.snap(i * HV + v) for v in range(HV)]
                    for v, job in enumerate(jobs):
                        if v == 0:
                            sp.wait_ge(idx_r, begun)
                        else:
                            sp.wait_ge(down, used[v])
                        sp.dma_start(wg[:].rearrange("p k n -> p (k n)"),
                                     c.gu[bass.ds(job, 1)].rearrange("o p n -> (o p) n")).then_inc(wr, 16)
                        sp.dma_start(wd[:].rearrange("p k n -> p (k n)"),
                                     c.dn[bass.ds(job, 1)].rearrange("o p n -> (o p) n")).then_inc(wr2, 16)
                    sp.wait_ge(ye, i * 2 + 2)
                    sp.dma_start(c.y_rows[bass.ds(row, P), :], ysb[:]).then_inc(stored, 16)

                tiles(sp, body)

            @block.gpsimd
            def _(pool):
                def body(i):
                    pool.tensor_copy(idx[:], c.token[:, bass.ds(i + c.NE, 1)]).then_inc(idx_r, 1)
                    pool.drain()
                    pool.indirect_dma_start(xg[:], None, c.x_rows, bass.IndirectOffsetOnAxis(idx[:], 0)).then_inc(got, 16)
                    pool.wait_ge(got, i * 16 + 16)
                    pool.wait_ge(tr, i + 1)
                    pool.wait_ge(stored, i * 16 + 16)

                tiles(pool, body)

            @block.tensor
            def _(pe):
                def body(i):
                    pe.wait_ge(got, i * 16 + 16)
                    for k in range(KD):
                        last = pe.transpose(ps[:, k // 4, (k % 4) * P:(k % 4 + 1) * P], xg[:, k * P:(k + 1) * P], m.ident[:])
                    last.then_inc(tr, 1)
                    pe.wait_ge(xe, i * 2 + 2)
                    for v in range(HV):
                        pe.wait_ge(wr, (i * HV + v) * 16 + 16)
                        pe.wait_ge(wr2, (i * HV + v) * 16 + 16)
                        for k in range(KD):
                            last = pe.matmul(ps[:, 2, :], xt[:, k, :], wg[:, k, :], start=(k == 0), stop=(k == KD - 1))
                        last.then_inc(up, 1)
                        pe.wait_ge(hr, i * HV + v + 1)
                        for k in range(2):
                            last = pe.transpose(ps[:, 4, k * P:(k + 1) * P], h[:, k * P:(k + 1) * P], m.ident[:])
                        last.then_inc(htr, 1)
                        pe.wait_ge(hte, i * HV + v + 1)
                        for k in range(2):
                            for n in range(2):
                                last = pe.matmul(ps[:, 6 + n, :], ht[:, k, :], wd[:, k, n * HALF:(n + 1) * HALF],
                                                 start=(k == 0 and v == 0), stop=(k == 1 and v == HV - 1))
                        last.then_inc(down, 1)

                tiles(pe, body)

            @block.scalar
            def _(act):
                def body(i):
                    act.wait_ge(tr, i + 1)
                    for q in range(2):
                        act.activation(xt[:, 4 * q:4 * q + 4, :], ps[:, q, :].rearrange("p (k n) -> p k n", k=4), ACT.Copy)\
                           .then_inc(xe, 1)
                    for v in range(HV):
                        act.wait_ge(up, i * HV + v + 1)
                        act.activation(hs[:], ps[:, 2, 0:256], ACT.Silu).then_inc(sl, 1)
                        act.wait_ge(htr, i * HV + v + 1)
                        act.activation(ht[:].rearrange("p k n -> p (k n)"), ps[:, 4, 0:256], ACT.Copy).then_inc(hte, 1)
                    act.wait_ge(down, i * HV + HV)
                    for q in range(2):
                        act.activation(ysb[:, q * HALF:(q + 1) * HALF], ps[:, 6 + q, :], ACT.Copy).then_inc(ye, 1)
                    act.wait_ge(stored, i * 16 + 16)

                tiles(act, body)

            @block.vector
            def _(dve):
                def body(i):
                    for v in range(HV):
                        dve.wait_ge(sl, i * HV + v + 1)
                        dve.tensor_tensor(h[:], hs[:], ps[:, 2, 256:512], ALU.mult).then_inc(hr, 1)

                tiles(dve, body)


def combine(nc, m, c):
    with ExitStack() as ctx:
        sem = lambda name: ctx.enter_context(nc.semaphore(f"{c.tag}c_{name}"))
        y = ctx.enter_context(nc.sbuf_tensor(f"{c.tag}c_y", [P, NT, 2, D], F32))
        got = c.got_back
        own, done = sem("own"), sem("done")
        with nc.Block() as block:

            @block.gpsimd
            def _(pool):
                for n in range(2 * NT):
                    pool.indirect_dma_start(y[:, n // 2, n % 2, :], None, c.y_rows,
                                            bass.IndirectOffsetOnAxis(c.slot[:, n // 2, n % 2:n % 2 + 1], 0)).then_inc(got[n], 16)
                for n in range(2 * NT):
                    pool.wait_ge(got[n], 16)

            @block.vector
            def _(dve):
                st = Steps(dve, own)
                for t in range(NT):
                    a, b = y[:, t, 0, :], y[:, t, 1, :]
                    dve.wait_ge(got[2 * t], 16)
                    st.link(dve.tensor_scalar(a, a, c.wt[:, t, 0:1], None, ALU.mult))
                    dve.wait_ge(got[2 * t + 1], 16)
                    st.link(dve.scalar_tensor_tensor(a, b, c.wt[:, t, 1:2], a, ALU.mult, ALU.add))
                    if c.gate is not None:
                        st.link(dve.tensor_tensor(a, a, c.gate, ALU.mult))
                    dve.tensor_tensor(m.x[:, t, :], m.x[:, t, :], a, ALU.add).then_inc(done, 1)
                dve.wait_ge(done, NT)


def second_mixer(nc, m, d, mix):
    sbm = lambda name, shape: mix.enter_context(nc.sbuf_tensor(name, shape, F32))
    s = Shared()
    s.gates_t = d["gates_t"]
    m.a_t = m.y_t = sbm("a_t2", [P, KD, T])
    s.lru, s.gate = sbm("lru", [P, 8, T]), sbm("gelu", [P, 8, T])
    s.pool, s.pool_y = sbm("pool", [P, 4, T]), sbm("pool_y", [P, 4, T])
    s.heads, s.pool_w = sbm("heads", [P, 2, 8, 64]), sbm("pool_w", [P, 4, P])
    norm_and_transpose(nc, m, "n3", None, None, None, m.a_t, g_src=d["norm1_g2"])
    project2(nc, m, d, s)
    merge(nc, m, s)
    mix_out(nc, m, OUT20, None)


def project2(nc, m, d, s):
    N = NIN2 * 4
    with ExitStack() as ctx:
        sem = lambda name: ctx.enter_context(nc.semaphore(f"p2_{name}"))
        sb = lambda name, shape: ctx.enter_context(nc.sbuf_tensor(f"p2_{name}", shape, F32))
        pz = ctx.enter_context(nc.psum_tensor("p2_pz", [P, 4, HALF], F32))
        ps = ctx.enter_context(nc.psum_tensor("p2_ps", [P, 4, HALF], F32))
        sg = sb("sg", [P, 2, HALF])
        dense = sb("dense", [P, 2, 2, P])
        c8 = sb("c8", [P, 4, 8])
        part = lambda n: m.mods[:, n * T:(n + 1) * T]
        xc = m.mods[:, 0:2 * T].rearrange("p (b t) -> p b t", b=2)
        r, i_, mu, inv, w2, w3 = (part(n) for n in range(2, 8))
        cnt = m.mods[:, 8 * T:12 * T].rearrange("p (g t) -> p g t", g=4)
        mm, ev_a, ev_v, stored, par = sem("mm"), sem("eva"), sem("evv"), [sem("st0"), sem("st1")], sem("par")
        own, pown, zeroed, dense_r, conv, gmm, ra, aa, sq, mu_r, mu_q, pin, pmm, pev, ca, cv, cnt_r, xdone = \
            (sem(n) for n in ("own", "pown", "zero", "dense", "conv", "gmm", "ra", "aa", "sq", "mur", "muq", "pin", "pmm",
                              "pev", "ca", "cv", "cnt", "xd"))
        taps = at(m.par, "conv_w2")

        def product_of(eng, n):
            if n % 4 == 3:
                m.stream.wait_used(eng, IN20 + n // 4)
            else:
                eng.wait_ge(mm, n // 4 * 3 + n % 4 + 1)

        def copied_out(eng, n):
            if n < 16:
                eng.wait_ge(ev_a if n % 2 else ev_v, n // 2 + 1)
            elif n < 20:
                eng.wait_ge(ev_v, n - 7)
            else:
                eng.wait_ge(ev_a, n - 11)

        def lru_tail(dve, st, n):
            tt, ts = dve.tensor_tensor, dve.tensor_scalar
            dve.wait_ge(aa, 2 * n + 2)
            st.link(ts(inv[:], mu[:], 1.0, None, ALU.add))
            st.link(dve.reciprocal(inv[:], inv[:]))
            dve.scalar_tensor_tensor(mu[:], mu[:], 2.0, inv[:], ALU.mult, ALU.mult).then_inc(mu_r, 1)
            st.link(tt(i_[:], i_[:], xc[:, n % 2, :], ALU.mult))
            dve.wait_ge(mu_q, n + 1)
            st.link(tt(i_[:], i_[:], mu[:], ALU.mult))
            st.link(dve.tensor_tensor_scan(s.lru[:, n, :], r[:], i_[:], 0.0, ALU.mult, ALU.add))
            copied_out(dve, 2 * n + 1)
            tt(s.lru[:, n, :], s.lru[:, n, :], s.gate[:, n, :], ALU.mult).then_inc(xdone, 1)

        with nc.Block() as block:

            @block.sync
            def _(sp):
                sp.dma_start(s.heads[:].rearrange("p a b c -> p (a b c)"), d["heads"]).then_inc(par, 16)
                sp.dma_start(s.pool_w[:].rearrange("p a b -> p (a b)"), d["pool_w"]).then_inc(par, 16)
                m.stream.load(sp, IN20 + RING, IN20 + NIN2)
                for n in range(20, N):
                    q = n - 20
                    copied_out(sp, n)
                    sp.dma_start(d["gates_t"][q], sg[:, q % 2, :]).then_inc(stored[q % 2], 16)
                    if n % 4 == 3:
                        m.stream.load(sp, IN20 + RING + n // 4, IN20 + RING + n // 4 + 1)
                for v in stored:
                    sp.wait_ge(v, 16 * 8)

            @block.tensor
            def _(pe):
                def gates_of(q):
                    pe.wait_ge(dense_r, 4 * q + 4)
                    pe.wait_ge(conv, q + 1)
                    if q >= 2:
                        pe.wait_ge(aa, 2 * (q - 1))
                    for k in range(2):
                        last = pe.matmul(ps[:, 2 * (q % 2) + k, :], dense[:, q % 2, k, :], xc[:, q % 2, :], start=True, stop=True)
                    last.then_inc(gmm, 1)

                pe.wait_ge(par, 32)
                for n in range(N):
                    c, j = IN20 + n // 4, n % 4
                    w = m.ring[:, c % RING, :].rearrange("p (k n) -> p k n", k=KD)
                    if j == 0:
                        m.stream.wait(pe, c)
                    if n >= 4:
                        copied_out(pe, n - 4)
                    for k in range(KD):
                        last = pe.matmul(pz[:, n % 4, :], w[:, k, j * P:(j + 1) * P], m.a_t[:, k, :],
                                         start=(k == 0), stop=(k == KD - 1))
                    if j == 3:
                        m.stream.free(last, c)
                    else:
                        last.then_inc(mm, 1)
                    if n % 2 and 3 <= n < 19:
                        gates_of((n - 3) // 2)
                    if n in POOL_AFTER:
                        g = POOL_AFTER.index(n)
                        pe.wait_ge(pin, g + 1)
                        if g == 0:
                            pe.wait_ge(aa, 16)
                        if g >= 2:
                            pe.wait_ge(pev, g - 1)
                        pe.matmul(ps[:, g % 2, :], s.pool_w[:, g, :], s.pool[:, g, :], start=True, stop=True).then_inc(pmm, 1)

            @block.scalar
            def _(act):
                st = Steps(act, sq)

                def coefficients(n):
                    act.wait_ge(gmm, n + 1)
                    if n:
                        act.wait_ge(xdone, n)
                    b = 2 * (n % 2)
                    act.activation(i_[:], ps[:, b + 1, :], ACT.Sigmoid, bias=at(m.par, "b_i")[:, n:n + 1]).then_inc(ra, 1)
                    st.link(act.activation(r[:], ps[:, b, :], ACT.Sigmoid, bias=at(m.par, "b_r")[:, n:n + 1]))
                    act.activation(mu[:], r[:], ACT.Tanh, scale=c8[:, 1, n:n + 1]).then_inc(aa, 1)
                    act.wait_ge(aa, 2 * n + 1)
                    act.activation(r[:], r[:], ACT.Exp, scale=c8[:, 0, n:n + 1]).then_inc(aa, 1)
                    act.wait_ge(mu_r, n + 1)
                    act.activation(mu[:], mu[:], ACT.Sqrt).then_inc(mu_q, 1)

                lam = at(m.par, "lam2")
                st.link(act.activation(c8[:, 0, :], lam, ACT.Abs))
                st.link(act.activation(c8[:, 0, :], c8[:, 0, :], ACT.Exp, scale=-1.0))
                act.activation(c8[:, 1, :], c8[:, 0, :], ACT.Ln, bias=1.0).then_inc(cv, 1)
                act.wait_ge(cv, 2)
                for n in range(8):
                    product_of(act, 2 * n + 1)
                    act.activation(s.gate[:, n, :], pz[:, (2 * n + 1) % 4, :], ACT.Gelu_apprx_tanh).then_inc(ev_a, 1)
                    if n:
                        coefficients(n - 1)
                coefficients(7)
                for n in range(20, N):
                    q = n - 20
                    product_of(act, n)
                    if q >= 2:
                        act.wait_ge(stored[q % 2], 16 * (q // 2))
                    act.activation(sg[:, q % 2, :], pz[:, n % 4, :], ACT.Sigmoid).then_inc(ev_a, 1)
                    if n in POOL_AFTER:
                        g = POOL_AFTER.index(n)
                        act.wait_ge(pmm, g + 1)
                        act.activation(s.pool_y[:, g, :], ps[:, g % 2, :], ACT.Copy, scale=at(m.par, "pool_scale")[:, g:g + 1])\
                           .then_inc(pev, 1)

            @block.gpsimd
            def _(pool):
                st = Steps(pool, pown)
                pool.memset(dense[:], 0.0).then_inc(zeroed, 1)
                for g in range(4):
                    pool.tensor_scalar(cnt[:, g, :], m.t_row[:], 1.0, float(2 << g), ALU.add, ALU.min).then_inc(cnt_r, 1)
                for g in range(4):
                    copied_out(pool, 16 + g)
                    pool.wait_ge(ca, g + 1)
                    st.link(pool.tensor_copy(w2[:], s.pool[:, g, :]))
                    src, dst = w2, w3
                    for k in range(g + 1):
                        h = 1 << k
                        st.link(pool.tensor_copy(dst[:, 0:h], src[:, 0:h]))
                        st.link(pool.tensor_tensor(dst[:, h:], src[:, h:], src[:, :T - h], ALU.add))
                        src, dst = dst, src
                    st.link(pool.tensor_tensor(src[:], src[:], cnt[:, g, :], ALU.mult))
                    pool.tensor_tensor(s.pool[:, g, :], src[:], s.pool[:, g, :], ALU.subtract).then_inc(pin, 1)
                    pool.wait_ge(pin, g + 1)

            @block.vector
            def _(dve):
                st = Steps(dve, own)
                tt, ts, stt = dve.tensor_tensor, dve.tensor_scalar, dve.scalar_tensor_tensor

                def copy_out(n, dst):
                    product_of(dve, n)
                    dve.tensor_copy(dst, pz[:, n % 4, :]).then_inc(ev_v, 1)

                lam = at(m.par, "lam2")
                dve.wait_ge(cv, 1)
                st.link(ts(c8[:, 2, :], lam, -1.0, 0.0, ALU.mult, ALU.max))
                st.link(tt(c8[:, 3, :], c8[:, 2, :], c8[:, 1, :], ALU.add))
                st.link(ts(c8[:, 0, :], c8[:, 3, :], -8.0, None, ALU.mult))
                ts(c8[:, 1, :], c8[:, 3, :], 8.0, None, ALU.mult).then_inc(cv, 1)
                dve.wait_ge(zeroed, 1)
                dve.wait_ge(par, 32)
                for g in range(4):
                    dve.wait_ge(cnt_r, g + 1)
                    dve.reciprocal(cnt[:, g, :], cnt[:, g, :]).then_inc(ca, 1)
                for n in range(8):
                    b = n % 2
                    copy_out(2 * n, s.lru[:, n, :])
                    if n >= 2:
                        dve.wait_ge(gmm, n - 1)
                        dve.wait_ge(xdone, n - 1)
                    for k in range(2):
                        for h in range(2):
                            p = slice(64 * h, 64 * h + 64)
                            dve.tensor_copy(dense[p, b, k, 64 * h:64 * h + 64], s.heads[p, k, n, :]).then_inc(dense_r, 1)
                    o, q = xc[:, b, :], s.lru[:, n, :]
                    w = lambda k: taps[:, 4 * n + k:4 * n + k + 1]
                    copied_out(dve, 2 * n)
                    st.link(ts(o, q, w(3), at(m.par, "conv_b2")[:, n:n + 1], ALU.mult, ALU.add))
                    st.link(stt(o[:, 1:], q[:, :T - 1], w(2), o[:, 1:], ALU.mult, ALU.add))
                    st.link(stt(o[:, 2:], q[:, :T - 2], w(1), o[:, 2:], ALU.mult, ALU.add))
                    stt(o[:, 3:], q[:, :T - 3], w(0), o[:, 3:], ALU.mult, ALU.add).then_inc(conv, 1)
                    if n:
                        lru_tail(dve, st, n - 1)
                copy_out(16, s.pool[:, 0, :])
                copy_out(17, s.pool[:, 1, :])
                lru_tail(dve, st, 7)
                copy_out(18, s.pool[:, 2, :])
                copy_out(19, s.pool[:, 3, :])


def merge(nc, m, s):
    with ExitStack() as ctx:
        sem = lambda name: ctx.enter_context(nc.semaphore(f"mg_{name}"))
        ps = ctx.enter_context(nc.psum_tensor("mg_ps", [P, 4, HALF], F32))
        sg = ctx.enter_context(nc.sbuf_tensor("mg_sg", [P, 2, 2, T], F32))
        mm, used, own, done, g_in = sem("mm"), sem("used"), sem("own"), sem("done"), [sem("g0"), sem("g1")]
        gates = s.gates_t
        with nc.Block() as block:

            @block.sync
            def _(sp):
                for n in range(8):
                    if n >= 2:
                        sp.wait_ge(done, n - 1)
                    sp.dma_start(sg[:, n % 2, 0, :], gates[n]).then_inc(g_in[n % 2], 16)
                    sp.dma_start(sg[:, n % 2, 1, :], gates[8 + n]).then_inc(g_in[n % 2], 16)
                m.stream.load(sp, PRA0 + RING, PRA0 + RING + 1)

            @block.tensor
            def _(pe):
                m.stream.wait(pe, PRA0)
                wa = m.ring[:, PRA0 % RING, :].rearrange("p (k n) -> p k n", k=4)
                for n in range(8):
                    c, j = PRB0 + n // 4, n % 4
                    if j == 0:
                        m.stream.wait(pe, c)
                    if n >= 2:
                        pe.wait_ge(used, 2 * (n - 1))
                    wb = m.ring[:, c % RING, :].rearrange("p (k n) -> p k n", k=KD)
                    b = 2 * (n % 2)
                    for k in range(4):
                        last = pe.matmul(ps[:, b, :], wa[:, k, n * P:(n + 1) * P], s.pool_y[:, k, :], start=(k == 0), stop=(k == 3))
                    if n == 7:
                        m.stream.free(last, PRA0)
                    for k in range(KD):
                        last = pe.matmul(ps[:, b + 1, :], wb[:, k, j * P:(j + 1) * P], s.lru[:, k, :], start=(k == 0),
                                         stop=(k == KD - 1))
                    if j == 3:
                        m.stream.free(last, c)
                    else:
                        last.then_inc(mm, 1)

            @block.vector
            def _(dve):
                st = Steps(dve, own)
                for n in range(8):
                    dve.wait_ge(g_in[n % 2], 32 * (n // 2 + 1))
                    if n % 4 == 3:
                        m.stream.wait_used(dve, PRB0 + n // 4)
                    else:
                        dve.wait_ge(mm, n // 4 * 3 + n % 4 + 1)
                    b = 2 * (n % 2)
                    a0, b0 = sg[:, n % 2, 0, :], sg[:, n % 2, 1, :]
                    dve.tensor_tensor(a0, a0, ps[:, b, :], ALU.mult).then_inc(used, 1)
                    dve.tensor_tensor(b0, b0, ps[:, b + 1, :], ALU.mult).then_inc(used, 1)
                    dve.wait_ge(used, 2 * n + 2)
                    dve.tensor_tensor(m.y_t[:, n, :], a0, b0, ALU.add).then_inc(done, 1)


def gather_semaphores(sem, tag):
    return dict(got=[sem(f"{tag}_got{n}") for n in range(2)], got_over=sem(f"{tag}_got_over"),
                got_back=[sem(f"{tag}_got_back{n}") for n in range(2 * NT)])


def clear_semaphores(nc, m):
    with nc.Block() as block:

        @block.gpsimd
        def _(pool):
            pool.sem_clear(m.phase_sems)


def moe(nc, m, c, sb, scale, shift, g_src):
    c.wt, c.slot = sb(f"{c.tag}_wt", [P, NT, 2]), sb(f"{c.tag}_slot", [P, NT, 2], U32)
    c.token, c.over = sb(f"{c.tag}_token", [P, c.NE + EXTRA], U32), sb(f"{c.tag}_over", [1, 1 + EXTRA], I32)
    with nc.sbuf_tensor(f"{c.tag}_a_t", [P, KD, T], F32) as a_t:
        m.a_t = a_t
        norm_and_transpose(nc, m, f"{c.tag}n", scale, shift, c.x_rows, a_t, g_src=g_src)
        route(nc, m, c)
    experts(nc, m, c)
    overflow(nc, m, c)
    combine(nc, m, c)


def program(nc, d, upto=99):
    with ExitStack() as ctx:
        sb = lambda name, shape, dt=F32: ctx.enter_context(nc.sbuf_tensor(name, shape, dt))
        sem = lambda name: ctx.enter_context(nc.semaphore(name))
        m = Shared()
        d["x_rows"] = nc.dram_tensor("x_rows", (T, D), F32, kind="Internal").ap()
        d["gates_t"] = nc.dram_tensor("gates_t", (16, P, T), F32, kind="Internal").ap()
        d["x_rows2"] = nc.dram_tensor("x_rows2", (T, D), F32, kind="Internal").ap()
        d["y_rows"] = nc.dram_tensor("y_rows", ((32 + EXTRA) * P, D), F32, kind="Internal").ap()
        m.x = sb("x", [P, NT, D])
        m.mods = sb("mods", [P, 6 * D])
        m.ring = sb("ring", [P, RING, SLOT])
        m.par = sb("par", [P, NCOL])
        m.rows = sb("rows", [P, NROW])
        m.ident, m.ones, m.tri = sb("ident", [P, P]), sb("ones", [P, P]), sb("tri", [P, P])
        m.upto, m.same = sb("upto", [P, P]), sb("same", [P, P])
        m.level = sb("level", [P, 6, P])
        m.t_row = sb("t_row", [P, T])
        m.w_ready = [sem(f"w_ready{n}") for n in range(RING)]
        m.w_free = [sem(f"w_free{n}") for n in range(RING)]
        m.x_in = sem("x_in")
        gathers = [gather_semaphores(sem, tag) for tag in ("m1", "m2")]
        with nc.semaphore("first_of_phases") as first:
            m.phase_sems = range(first.num, LAST_SEM)
        src = [d["w_ada"][n] for n in range(NADA)] + [d["w_in"][n] for n in range(NIN)] + [d["w_glu"]]
        src += [d["w_out"][n] for n in range(2)]
        src += [y for e in range(32) for y in (d["gu"][e], d["dn"][e])]
        src += [d["w_in2"][n] for n in range(NIN2)] + [d["proj_a"]] + [d["proj_b"][n] for n in range(2)]
        src += [d["w_out2"][n] for n in range(2)] + [None, None]
        src += [y for e in range(32) for y in (d["gu2"][e], d["dn2"][e])]
        assert len(src) == NCHUNK
        m.stream = Stream(m, src)
        m.stream.stop = {1: 17, 2: 18, 3: 18, 4: 20, 5: 20, 6: 84, 7: 100}.get(upto, NCHUNK)
        m.spare = m.mods[:, 0:2 * D]
        mod = lambda n: m.mods[:, n * D:(n + 1) * D]

        constants_and_modulation(nc, m, d)
        with ExitStack() as mix:
            sbm = lambda name, shape: mix.enter_context(nc.sbuf_tensor(name, shape, F32))
            m.u_t, m.qkv, m.z_t = sbm("u_t", [P, 4, T]), sbm("qkv", [P, 12, T]), sbm("z_t", [P, 4, T])
            m.y_t = m.a_t = sbm("y_t", [P, KD, T])
            m.gates = sbm("gates", [P, NT * 8])
            norm_and_transpose(nc, m, "n1", mod(1), mod(0), None, m.a_t)
            project_and_s5(nc, m, d)
            if upto < 3: return m
            delta_rule(nc, m)
            if upto < 4: return m
            mix_out(nc, m, OUT0, mod(2))
        if upto < 5: return m
        c = Experts(tag="m1", NE=32, NG=4, EG=8, NJ=32, HV=1, first=MOE0, router="w_router", bias=None,
                    gu=d["gu"], dn=d["dn"], gate=mod(5), x_rows=d["x_rows"], y_rows=d["y_rows"], **gathers[0])
        clear_semaphores(nc, m)
        moe(nc, m, c, sb, mod(4), mod(3), None)
        if upto < 7: return m
        clear_semaphores(nc, m)
        norm_and_transpose(nc, m, "nf", None, None, None, None, g_src=d["normf_g"], in_place=True)
        with ExitStack() as mix:
            second_mixer(nc, m, d, mix)
        if upto < 9: return m
        c = Experts(tag="m2", NE=16, NG=4, EG=4, NJ=32, HV=2, first=MOE20, router="w_router2",
                    bias=row_at(m.rows, "router_b2"), gu=d["gu2"], dn=d["dn2"], gate=None,
                    x_rows=d["x_rows2"], y_rows=d["y_rows"], **gathers[1])
        clear_semaphores(nc, m)
        moe(nc, m, c, sb, None, None, d["norm2_g2"])
        norm_and_transpose(nc, m, "nl", None, None, None, None, g_src=d["normf_g2"], final_out=d["out"])


_OUT = (1, T, D)


def _layouts(i):
    import numpy as np
    f = lambda a: np.ascontiguousarray(a)
    col = lambda a, n: a.reshape(n, P).T
    chunks = lambda w, k, n: f(w.reshape(k, P, -1, n).transpose(2, 1, 0, 3).reshape(-1, P, k * n))
    state = lambda a: a.reshape(NS5, P).T
    tiles = lambda a, k: a.reshape(k, P, -1).transpose(1, 0, 2).reshape(P, -1)
    taps = lambda w, n: w.T.reshape(n, P, 4).transpose(1, 0, 2).reshape(P, -1)
    bt = lambda b: b.reshape(NS5, P, G16).transpose(1, 0, 2).reshape(P, -1)
    ct = lambda c: c.transpose(0, 2, 1).reshape(NS5, P, G16).transpose(1, 0, 2).reshape(P, -1)
    w_in = i["w_in"][0]
    w2 = i["w_in_2"][0]
    turns = [w2[:, o + n * P:o + (n + 1) * P] for n in range(8) for o in (512, 1536)]
    w_in2 = np.concatenate(turns + [w2[:, 0:512], w2[:, 2560:]], 1)
    cols = dict(
        c=col(i["c"][0], 8), s5_d=col(i["s5_d"][0], 4), b_glu=col(i["b_glu"][0], 4), conv_w=taps(i["conv_w"][0], 12),
        gdn_g=i["gdn_norm_g"][0].reshape(P, 1), lam_re=state(i["lam_re"][0]), lam_im=state(i["lam_im"][0]),
        log_step=state(np.repeat(i["log_step"][0], 64)), b_re=bt(i["s5_b_re"][0]), b_im=bt(i["s5_b_im"][0]),
        c_re=ct(i["s5_c_re"][0]), c_im=ct(i["s5_c_im"][0]), w_gates=tiles(w_in[:, 2560:], KD),
        w_router=tiles(np.concatenate([i["w_router_grp"][0], i["w_router_exp"][0]], 1), KD),
        pool_scale=col(i["pool_scale_2"][0], 4), conv_w2=taps(i["conv_w_2"][0], 8), conv_b2=col(i["conv_b_2"][0], 8),
        b_r=col(i["rg_b_r_2"][0], 8), b_i=col(i["rg_b_i_2"][0], 8), lam2=col(i["rg_lambda_2"][0], 8),
        w_router2=tiles(np.concatenate([i["router_group_w_2"][0], i["router_expert_w_2"][0]], 1), KD))
    gu = lambda g, u, e: f(np.concatenate([g.reshape(-1, KD, P, 1, e).transpose(0, 2, 1, 3, 4),
                                           u.reshape(-1, KD, P, 1, e).transpose(0, 2, 1, 3, 4)], 3).reshape(-1, P, KD * 2 * e))
    half = lambda w: w.reshape(16, D, 2, 256).transpose(0, 2, 1, 3).reshape(32, D, 256)
    dn = lambda w: f(w.reshape(32, 2, P, D).transpose(0, 2, 1, 3).reshape(32, P, 2 * D))
    heads = lambda w: w.reshape(8, P, 64).transpose(1, 0, 2).reshape(P, -1)
    return dict(
        x=f(i["x"][0].reshape(NT, P, D).transpose(1, 0, 2)),
        cols=f(np.concatenate([cols[n].reshape(P, k) for n, k in COLS], 1)),
        rows=f(np.concatenate([i["a_log"][0], i["dt_bias"][0], i["router_group_b_2"][0], i["router_expert_b_2"][0]])),
        b_ada=f(i["b_ada"]), norm1_g=f(i["norm1_g"][0]), norm2_g=f(i["norm2_g"][0]), normf_g=f(i["normf_g"]),
        norm1_g2=f(i["norm1_g_2"][0]), norm2_g2=f(i["norm2_g_2"][0]), normf_g2=f(i["norm_f_g_2"]),
        w_ada=chunks(i["w_ada"][0], KD, HALF), w_in=chunks(w_in[:, :2560], KD, HALF),
        w_glu=chunks(i["w_glu"][0], 4, HALF)[0], w_out=chunks(i["w_out"][0], KD, HALF),
        gu=gu(i["w_gate"][0], i["w_up"][0], 256), dn=dn(i["w_down"][0]),
        w_in2=chunks(w_in2, KD, HALF), proj_a=chunks(i["proj_a_2"][0], 4, D)[0],
        proj_b=chunks(i["proj_b_2"][0], KD, HALF), w_out2=chunks(i["w_out_2"][0], KD, HALF),
        heads=f(np.concatenate([heads(i["rg_w_r_2"][0]), heads(i["rg_w_i_2"][0])], 1)),
        pool_w=f(i["pool_w_2"][0].transpose(1, 0, 2).reshape(P, -1)),
        gu2=gu(half(i["exp_w_gate_2"][0]), half(i["exp_w_up_2"][0]), 256), dn2=dn(i["exp_w_down_2"][0]))


def kernel(**inputs):
    import numpy as np
    import concourse.bacc as bacc
    from concourse.bass_utils import run_bass_kernel_spmd

    arrays = _layouts({k: np.asarray(v) for k, v in inputs.items()})
    nc = bacc.Bacc("TRN2", target_bir_lowering=False, num_devices=1)
    d = {k: nc.dram_tensor(f"in_{k}", v.shape, F32, kind="ExternalInput").ap() for k, v in arrays.items()}
    d["out"] = nc.dram_tensor("out", (T, D), F32, kind="ExternalOutput").ap()
    program(nc, d)
    r = run_bass_kernel_spmd(nc, [{f"in_{k}": v for k, v in arrays.items()}], core_ids=[0])
    return r.results[0]["out"].reshape(_OUT)
```

```python
from contextlib import ExitStack

import concourse.bass as bass
from concourse import mybir

F32 = mybir.dt.float32
I32 = mybir.dt.int32
U32 = mybir.dt.uint32
ALU = mybir.AluOpType
ACT = mybir.ActivationFunctionType
AX = mybir.AxisListType

P = 128
T = 512
NT = T // P
D = 1024
KD = D // P
HALF = 512
EPS = 1e-6
EXTRA = 7
LAST_SEM = 256
CH = 64
NH = 4
G16 = 16
NS5 = 16
TWO_PI = 6.283185307179586
ROUND = 12582912.0
BIG = 1.0e30

COLS = [("c", 8), ("s5_d", 4), ("b_glu", 4), ("conv_w", 48), ("gdn_g", 1), ("lam_re", 16), ("lam_im", 16),
        ("log_step", 16), ("b_re", 256), ("b_im", 256), ("c_re", 256), ("c_im", 256), ("w_gates", 64),
        ("w_router", 288), ("pool_scale", 4), ("conv_w2", 32), ("conv_b2", 8), ("b_r", 8), ("b_i", 8),
        ("lam2", 8), ("w_router2", 160)]
NCOL = sum(n for _, n in COLS)
ROWS = [("a_log", 4), ("dt_bias", 4), ("router_b2", 20)]
NROW = sum(n for _, n in ROWS)

ADA0, NADA = 0, 12
IN0, NIN = 12, 5
GLU0 = 17
OUT0 = 18
MOE0 = 20
IN20, NIN2 = 84, 9
PRA0 = 93
PRB0 = 94
OUT20 = 96
MOE20 = 100
NCHUNK = 164
POOL_AFTER = [26, 28, 30, 32]
RING = 4
SLOT = 4096


class Shared:
    pass


class Experts:

    def __init__(self, tag, NE, NG, EG, NJ, HV, first, router, bias, gu, dn, gate, x_rows, y_rows, got, got_over, got_back):
        self.tag, self.NE, self.NG, self.EG, self.NJ, self.HV = tag, NE, NG, EG, NJ, HV
        self.first, self.router, self.bias, self.gu, self.dn, self.gate = first, router, bias, gu, dn, gate
        self.x_rows, self.y_rows = x_rows, y_rows
        self.got, self.got_over, self.got_back = got, got_over, got_back


class Steps:

    def __init__(self, eng, sem):
        self.eng, self.sem, self.n = eng, sem, 0

    def mark(self, ins):
        ins.then_inc(self.sem, 1)
        self.n = self.n + 1
        return self.n

    def link(self, ins):
        self.eng.wait_ge(self.sem, self.mark(ins))


def at(ap, name):
    o = 0
    for n, k in COLS:
        if n == name:
            return ap[:, o:o + k]
        o += k


def row_at(ap, name):
    o = 0
    for n, k in ROWS:
        if n == name:
            return ap[:, o:o + k]
        o += k


def over(ap, k):
    return ap.unsqueeze(2).to_broadcast([ap.shape[0], ap.shape[1], k])


def rows_of(ap, k):
    return ap.unsqueeze(1).to_broadcast([ap.shape[0], k, ap.shape[1]])


class Stream:

    def __init__(self, m, src):
        self.m, self.src, self.stop = m, src, len(src)

    def load(self, sp, lo, hi):
        for n in range(lo, min(hi, self.stop)):
            s, dst = n % RING, self.m.ring[:, n % RING, :]
            if self.src[n] is None:
                continue
            if n >= RING:
                sp.wait_ge(self.m.w_free[s], self.frees(n - RING))
            src = self.src[n]
            sp.dma_start(dst[:, 0:src.shape[1]], src).then_inc(self.m.w_ready[s], 16)

    def loads(self, n):
        return 16 * sum(1 for k in range(n % RING, n + 1, RING) if self.src[k] is not None)

    def frees(self, n):
        return self.loads(n) // 16

    def wait(self, pe, n):
        pe.wait_ge(self.m.w_ready[n % RING], self.loads(n))

    def free(self, ins, n):
        ins.then_inc(self.m.w_free[n % RING], 1)

    def wait_used(self, eng, n):
        eng.wait_ge(self.m.w_free[n % RING], self.frees(n))


def constants_and_modulation(nc, m, d):
    with ExitStack() as ctx:
        sem = lambda name: ctx.enter_context(nc.semaphore(name))
        c_bc = ctx.enter_context(nc.sbuf_tensor("c_bc", [P, KD, 32], F32))
        fold = ctx.enter_context(nc.sbuf_tensor("fold", [P, P], F32))
        part = ctx.enter_context(nc.sbuf_tensor("ada_part", [P, 2, HALF], F32))
        c_act = ctx.enter_context(nc.sbuf_tensor("c_act", [P, KD], F32))
        b_row = ctx.enter_context(nc.sbuf_tensor("b_row", [1, 6 * D], F32))
        g_row = ctx.enter_context(nc.sbuf_tensor("g_row", [P, 2, D], F32))
        ps = ctx.enter_context(nc.psum_tensor("ada_ps", [P, 4, HALF], F32))
        par, const, c_done, cb_done = sem("a_par"), sem("a_const"), sem("a_cact"), sem("a_cbc")
        folded, out, fold_ready = sem("a_folded"), sem("a_out"), sem("a_fold")
        ev, g_in, own, pool_own = sem("a_ev"), sem("a_g"), sem("a_own"), sem("a_pool")

        with nc.Block() as block:

            @block.sync
            def _(sp):
                m.stream.load(sp, ADA0, ADA0 + 2)
                sp.wait_ge(par, 48)
                m.stream.load(sp, ADA0 + 2, RING)
                sp.dma_start(m.x[:], d["x"]).then_inc(m.x_in, 16)
                with sp.Fori(1, NADA // RING) as r:
                    for s in range(RING):
                        sp.wait_ge(m.w_free[s], r)
                        sp.dma_start(m.ring[:, s, :], d["w_ada"][bass.ds(r * RING + s, 1)].rearrange("o p n -> (o p) n"))\
                          .then_inc(m.w_ready[s], 16)
                m.stream.load(sp, IN0, IN0 + RING)

            @block.gpsimd
            def _(pool):
                st = Steps(pool, pool_own)
                pool.memset(m.ones[:], 1.0).then_inc(const, 1)
                st.link(pool.memset(m.strip[:], 0.0))
                st.link(pool.memset(m.strip[:, 7:8], 1.0))
                st.link(pool.memset(m.ident[:], 0.0))
                pool.affine_select(out=m.ident[:], in_=m.ident[:], compare_op=ALU.not_equal, fill=1.0, base=0,
                                   pattern=[[-1, P]], channel_multiplier=1).then_inc(const, 1)
                st.link(pool.memset(fold[:], 0.0))
                for g in range(4):
                    pool.memset(fold[32 * g:32 * g + 1, :], 1.0).then_inc(fold_ready, 1)
                    pool.wait_ge(fold_ready, g + 1)
                st.link(pool.memset(m.tri[:], 1.0))
                pool.affine_select(out=m.tri[:], in_=m.tri[:], compare_op=ALU.is_gt, fill=0.0, base=0,
                                   pattern=[[1, P]], channel_multiplier=-1).then_inc(const, 1)
                st.link(pool.memset(m.upto[:], 1.0))
                st.link(pool.affine_select(out=m.upto[:], in_=m.upto[:], compare_op=ALU.is_ge, fill=0.0, base=0,
                                           pattern=[[1, P]], channel_multiplier=-1))
                st.link(pool.memset(m.upto[0:CH, CH:P], 0.0))
                st.link(pool.memset(m.same[:], 1.0))
                st.link(pool.memset(m.same[0:CH, CH:P], 0.0))
                st.link(pool.memset(m.same[CH:P, 0:CH], 0.0))
                for n in range(6):
                    b = 1 << n
                    mk = m.level[:, n, :]
                    v = mk.rearrange("p (q r) -> p q r", r=2 * b)
                    st.link(pool.memset(mk, 1.0))
                    st.link(pool.affine_select(out=v, in_=v, compare_op=ALU.is_ge, fill=0.0, base=0,
                                               pattern=[[-2 * b, P // (2 * b)], [0, 2 * b]], channel_multiplier=1))
                    st.link(pool.affine_select(out=v, in_=v, compare_op=ALU.is_gt, fill=0.0, base=b,
                                               pattern=[[2 * b, P // (2 * b)], [0, 2 * b]], channel_multiplier=-1))
                    st.link(pool.memset(v[:, :, 0:b], 0.0))
                st.link(pool.iota(m.t_row[:], [[1, T]], base=0, channel_multiplier=0,
                                  allow_small_or_imprecise_dtypes=True))

            @block.scalar
            def _(act):
                act.dma_start(m.par[:], d["cols"]).then_inc(par, 16)
                act.dma_start(b_row[:], d["b_ada"]).then_inc(par, 16)
                act.dma_start(m.rows[:], d["rows"].partition_broadcast(P)).then_inc(par, 16)
                act.dma_start(g_row[:, 0, :], d["norm1_g"].partition_broadcast(P)).then_inc(g_in, 16)
                act.dma_start(g_row[:, 1, :], d["norm2_g"].partition_broadcast(P)).then_inc(g_in, 16)
                act.wait_ge(par, 48)
                act.activation(c_act[:], at(m.par, "c"), ACT.Silu).then_inc(c_done, 1)

                def groups_out(r):
                    for b in range(4):
                        act.wait_ge(m.w_free[b], r + 1)
                        if not (isinstance(r, int) and b < 2):
                            act.wait_ge(folded, r * RING + b - 1)
                        act.activation(part[:, b % 2, :], ps[:, b % 2, :], ACT.Copy).then_inc(ev, 1)

                groups_out(0)
                with act.Fori(1, NADA // RING) as r:
                    groups_out(r)

            @block.vector
            def _(dve):
                dve.wait_ge(c_done, 1)
                dve.wait_ge(const, 1)
                for k in range(KD):
                    dve.tensor_scalar(c_bc[:, k, :], m.ones[:, 0:32], c_act[:, k:k + 1], None, ALU.mult).then_inc(cb_done, 1)
                with dve.Fori(0, NADA // 2) as r:
                    for b in range(2):
                        dve.wait_ge(folded, r * 2 + b + 1)
                        dve.tensor_copy(m.mods[:, bass.ds((r * 2 + b) * HALF, HALF)], ps[:, 2 + b, :]).then_inc(out, 1)
                dve.wait_ge(out, NADA)
                dve.wait_ge(g_in, 32)
                for n in range(2):
                    sc = m.mods[:, (3 * n + 1) * D:(3 * n + 2) * D]
                    dve.scalar_tensor_tensor(sc, sc, 1.0, g_row[:, n, :], ALU.add, ALU.mult).then_inc(own, 1)
                dve.wait_ge(own, 2)

            @block.tensor
            def _(pe):
                pe.wait_ge(cb_done, KD)
                pe.wait_ge(par, 48)
                pe.wait_ge(const, 1)
                pe.wait_ge(fold_ready, 4)

                def fold_chunk(n, b, first):
                    pe.wait_ge(ev, n + 1)
                    if not first:
                        pe.wait_ge(out, n - 1)
                    pe.matmul(ps[:, 2 + b, :], fold[:], part[:, b, :], start=True, stop=False)
                    pe.matmul(ps[:, 2 + b, :], m.ones[0:1, :], b_row[0:1, bass.ds(n * HALF, HALF)], start=False, stop=True)\
                      .then_inc(folded, 1)

                def chunks(r):
                    for s in range(RING):
                        pe.wait_ge(m.w_ready[s], r * 16 + 16)
                        if not (isinstance(r, int) and s < 2):
                            pe.wait_ge(ev, r * RING + s - 1)
                        w = m.ring[:, s, :].rearrange("p (k n) -> p k n", k=KD)
                        for k in range(KD):
                            g = slice(32 * (k % 4), 32 * (k % 4) + 32)
                            last = pe.matmul(ps[g, s % 2, :], c_bc[:, k, :], w[:, k, :], start=(k < 4), stop=(k >= 4))
                        m.stream.free(last, s)
                        if not (isinstance(r, int) and s == 0):
                            fold_chunk(r * RING + s - 1, (s - 1) % 2, isinstance(r, int) and s < 3)

                chunks(0)
                with pe.Fori(1, NADA // RING) as r:
                    chunks(r)
                fold_chunk(NADA - 1, 1, False)


def sum_squares(act, m, t, junk, sq):
    if t:
        act.wait_ge(sq, t)
    act.activation(junk[:], m.x[:, t, :], ACT.Square, accum_out=m.ss[:, t:t + 1]).then_inc(sq, 1)


def norm_and_transpose(nc, m, tag, scale, shift, rows_out, a_t, g_src=None, final_out=None, in_place=False, summed=False):
    with ExitStack() as ctx:
        sem = lambda name: ctx.enter_context(nc.semaphore(f"{tag}_{name}"))
        sb = lambda name, shape: ctx.enter_context(nc.sbuf_tensor(f"{tag}_{name}", shape, F32))
        a = sb("a", [P, 2, D])
        junk = sb("junk", [P, D])
        ms, rstd = sb("ms", [P, NT]), sb("rstd", [P, NT])
        if g_src is not None:
            g_row = sb("g", [P, D])
            scale = g_row[:]
        ps = ctx.enter_context(nc.psum_tensor(f"{tag}_ps", [P, 4, HALF], F32))
        sq, inv, root, a_ready, tr, ev_a, ev_v = (sem(n) for n in ("sq", "inv", "root", "a", "tr", "eva", "evv"))
        sq2, own, g_in, stored = sem("sq2"), sem("own"), sem("gin"), [sem("st0"), sem("st1")]
        out = rows_out if final_out is None else final_out
        turned = final_out is None and not in_place

        with nc.Block() as block:

            @block.sync
            def _(sp):
                if g_src is not None:
                    sp.dma_start(g_row[:], g_src.partition_broadcast(P)).then_inc(g_in, 16)
                if out is not None:
                    for t in range(NT):
                        sp.wait_ge(a_ready, t + 1)
                        sp.dma_start(out[t * P:(t + 1) * P, :], a[:, t % 2, :]).then_inc(stored[t % 2], 16)
                    for s in stored:
                        sp.wait_ge(s, 16 * NT // 2)

            @block.scalar
            def _(act):
                act.wait_ge(m.x_in, 16)
                if not summed:
                    for t in range(NT):
                        sum_squares(act, m, t, junk, sq)
                act.wait_ge(inv, 1)
                act.activation(rstd[:], ms[:], ACT.Sqrt).then_inc(root, 1)
                if in_place:
                    for t in range(NT):
                        act.wait_ge(a_ready, t + 1)
                        sum_squares(act, m, t, junk, sq2)
                    act.wait_ge(sq2, NT)
                if turned:
                    for u in range(0, 2 * NT, 2):
                        act.wait_ge(tr, u + 1)
                        t, h = u // 2, u % 2
                        act.activation(a_t[:, 4 * h:4 * h + 4, t * P:(t + 1) * P],
                                       ps[:, u % 4, :].rearrange("p (k n) -> p k n", k=4), ACT.Copy).then_inc(ev_a, 1)

            @block.vector
            def _(dve):
                st = Steps(dve, own)
                if not summed:
                    dve.wait_ge(sq, NT)
                st.link(dve.tensor_scalar(ms[:], m.ss[:], 1.0 / D, EPS, ALU.mult, ALU.add))
                dve.reciprocal(ms[:], ms[:]).then_inc(inv, 1)
                dve.wait_ge(root, 1)
                if g_src is not None:
                    dve.wait_ge(g_in, 16)
                for t in range(NT):
                    if t >= 2 and turned:
                        dve.wait_ge(tr, 2 * (t - 1))
                    if t >= 2 and out is not None:
                        dve.wait_ge(stored[t % 2], 16)
                    to = m.x[:, t, :] if in_place else a[:, t % 2, :]
                    row = dve.scalar_tensor_tensor(to, m.x[:, t, :], rstd[:, t:t + 1], scale, ALU.mult, ALU.mult)
                    if shift is not None:
                        st.link(row)
                        row = dve.tensor_tensor(a[:, t % 2, :], a[:, t % 2, :], shift, ALU.add)
                    row.then_inc(a_ready, 1)
                    if t and turned:
                        u = 2 * t - 1
                        dve.wait_ge(tr, u + 1)
                        dve.tensor_copy(a_t[:, 4:8, (t - 1) * P:t * P],
                                        ps[:, u % 4, :].rearrange("p (k n) -> p k n", k=4)).then_inc(ev_v, 1)
                if turned:
                    dve.wait_ge(tr, 2 * NT)
                    dve.tensor_copy(a_t[:, 4:8, (NT - 1) * P:NT * P],
                                    ps[:, 3, :].rearrange("p (k n) -> p k n", k=4)).then_inc(ev_v, 1)

            @block.tensor
            def _(pe):
                if not turned:
                    return
                for t in range(NT):
                    pe.wait_ge(a_ready, t + 1)
                    for h in range(2):
                        u = 2 * t + h
                        if u >= 4:
                            pe.wait_ge((ev_a, ev_v)[h], t - 1)
                        for k in range(4):
                            c = 4 * h + k
                            last = pe.transpose(ps[:, u % 4, k * P:(k + 1) * P], a[:, t % 2, c * P:(c + 1) * P], m.ident[:])
                        last.then_inc(tr, 1)


def project_and_s5(nc, m, d):
    with ExitStack() as ctx:
        sem = lambda name: ctx.enter_context(nc.semaphore(f"s5_{name}"))
        sb = lambda name, shape: ctx.enter_context(nc.sbuf_tensor(f"s5_{name}", shape, F32))
        sc = sb("sc", [P, 20, NS5])
        (STEP, XR, RHO1, TH, K, R, HS, SN, CH2, BRE, BIM, DEN, CR, CI, RHO, TURN, T0, T1, T2, T3) = \
            (sc[:, n, :] for n in range(20))
        prod = [m.spare.rearrange("p (n t) -> p n t", n=4), sb("prod", [P, 4, T])[:]]
        wide = m.spare[:, 0:1024].rearrange("p (r n c) -> p r n c", r=2, n=NS5)
        bb = m.spare[:, 1024:1536].rearrange("p (r n c) -> p r n c", r=2, n=NS5)
        tb = m.spare[:, 1536:1792].rearrange("p (n c) -> p n c", n=NS5)
        b_t = sb("b_t", [P, 2, 4, P])
        c_t = sb("c_t", [P, 2, NS5, 32])
        tables = sb("tables", [P, 4, T])
        cos, sin = tables[:, 0:2, :], tables[:, 2:4, :]
        turn, near = sb("turn", [P, T]), sb("near", [P, T])
        zre, zim = sb("zre", [P, T]), sb("zim", [P, T])
        half_pi = sb("half_pi", [P, 1])
        dst = [m.u_t[:, n, :] for n in range(4)] + [m.qkv[:, n, :] for n in range(12)] + [m.z_t[:, n, :] for n in range(4)]
        pp = ctx.enter_context(nc.psum_tensor("s5_pp", [P, 2, HALF], F32))
        pb = ctx.enter_context(nc.psum_tensor("s5_pb", [P, 4, HALF], F32))
        py = ctx.enter_context(nc.psum_tensor("s5_py", [P, 2, HALF], F32))
        own, aown, lam_a, lam_v = sem("own"), sem("aown"), sem("lam_a"), sem("lam_v")
        wide_ready, btr, b_ready = sem("wide"), sem("btr"), sem("bready")
        turn_ready, table, bu, bu_used = sem("turn"), sem("table"), sem("bu"), sem("buused")
        prods, prods_used, y_used, gel, gel_mm, sig, yout = \
            (sem(n) for n in ("prods", "pused", "yused", "gel", "gmm", "sig", "yout"))

        mm, copied, gm, gev, zeroed, filled = (sem(n) for n in ("mm", "copied", "gm", "gev", "zeroed", "filled"))
        conv, sil, term, conv_own = sem("conv"), sem("sil"), sem("term"), sem("conv_own")
        conved, delayed = m.z_t[:, 2:4, :], m.z_t[:, 1, :]
        zero = prod[1].rearrange("p n t -> p (n t)")[:, 0:D]

        def product_of(eng, n):
            if n % 4 == 3:
                m.stream.wait_used(eng, IN0 + n // 4)
            else:
                eng.wait_ge(mm, n // 4 * 3 + n % 4 + 1)

        with nc.Block() as block:

            @block.sync
            def _(sp):
                sp.wait_ge(zeroed, 1)
                for n in range(EXTRA):
                    sp.dma_start(d["y_rows"][(32 + n) * P:(33 + n) * P, :], zero).then_inc(filled, 16)
                m.stream.load(sp, IN0 + RING, GLU0 + 1 + RING)

            @block.gpsimd
            def _(pool):
                pool.memset(zero, 0.0).then_inc(zeroed, 1)
                st = Steps(pool, conv_own)
                taps = at(m.par, "conv_w")
                for n in range(12):
                    o, q = conved[:, n % 2, :], m.qkv[:, n, :]
                    w = lambda k: taps[:, 4 * n + k:4 * n + k + 1]
                    pool.wait_ge(copied, n + 5)
                    pool.wait_ge(term, n + 1)
                    if n:
                        pool.wait_ge(conv, n)
                    for k in (1, 2, 3):
                        st.link(pool.tensor_scalar(delayed[:, k:], q[:, :T - k], w(3 - k), None, ALU.mult))
                        last = pool.tensor_tensor(o[:, k:], o[:, k:], delayed[:, k:], ALU.add)
                        if k < 3:
                            st.link(last)
                    last.then_inc(conv, 1)

            @block.vector
            def _(dve):
                st = Steps(dve, own)
                tt, ts = dve.tensor_tensor, dve.tensor_scalar
                dve.wait_ge(gm, 1)
                dve.tensor_copy(m.gates[:], pb[:, 0, 0:NT * 8]).then_inc(gev, 1)
                dve.wait_ge(lam_a, 1)
                lre, lim = at(m.par, "lam_re"), at(m.par, "lam_im")
                st.link(tt(XR, lre, STEP, ALU.mult))
                st.link(tt(TH, lim, STEP, ALU.mult))
                st.link(ts(T0, XR, 1.0 / 256, None, ALU.mult))
                st.link(ts(T1, T0, 1.0 / 6, 1.0, ALU.mult, ALU.add))
                for c in (5.0, 4.0, 3.0, 2.0):
                    st.link(tt(T1, T1, T0, ALU.mult))
                    st.link(ts(T1, T1, 1.0 / c, 1.0, ALU.mult, ALU.add))
                st.link(tt(RHO1, T1, T0, ALU.mult))
                for _ in range(8):
                    st.link(dve.scalar_tensor_tensor(RHO1, RHO1, 2.0, RHO1, ALU.add, ALU.mult))
                st.link(ts(RHO, RHO1, 1.0, None, ALU.add))
                st.link(ts(T0, TH, 1.0 / TWO_PI, None, ALU.mult))
                st.link(ts(K, T0, ROUND, -ROUND, ALU.add, ALU.add))
                st.link(tt(TURN, T0, K, ALU.subtract))
                dve.tensor_scalar(R, TURN, TWO_PI, None, ALU.mult).then_inc(lam_v, 1)
                dve.wait_ge(lam_a, 2)
                st.link(tt(T0, HS, HS, ALU.mult))
                st.link(ts(T0, T0, -2.0, None, ALU.mult))
                st.link(dve.scalar_tensor_tensor(T1, T0, 1.0, RHO1, ALU.add, ALU.mult))
                st.link(tt(BRE, T1, T0, ALU.add))
                st.link(tt(BIM, RHO, SN, ALU.mult))
                st.link(tt(T0, lre, lre, ALU.mult))
                st.link(tt(T1, lim, lim, ALU.mult))
                st.link(tt(DEN, T0, T1, ALU.add))
                st.link(dve.reciprocal(DEN, DEN))
                st.link(tt(T0, BRE, lre, ALU.mult))
                st.link(tt(T1, BIM, lim, ALU.mult))
                st.link(tt(T0, T0, T1, ALU.add))
                st.link(tt(CR, T0, DEN, ALU.mult))
                st.link(tt(T0, BIM, lre, ALU.mult))
                st.link(tt(T1, BRE, lim, ALU.mult))
                st.link(tt(T0, T0, T1, ALU.subtract))
                st.link(tt(CI, T0, DEN, ALU.mult))
                br = at(m.par, "b_re").rearrange("p (n h) -> p n h", h=G16)
                bi = at(m.par, "b_im").rearrange("p (n h) -> p n h", h=G16)
                for n, (x, y, op) in enumerate(((br, bi, ALU.subtract), (bi, br, ALU.add))):
                    st.link(tt(bb[:, n], x, over(CR, G16), ALU.mult))
                    st.link(tt(tb[:], y, over(CI, G16), ALU.mult))
                    st.link(tt(bb[:, n], bb[:, n], tb[:], op))
                st.link(dve.memset(wide[:], 0.0))
                for g in range(2):
                    s = slice(CH * g, CH * g + CH)
                    st.link(dve.tensor_copy(wide[s, 0, :, G16 * g:G16 * g + G16], bb[s, 0]))
                    dve.tensor_copy(wide[s, 1, :, G16 * g:G16 * g + G16], bb[s, 1]).then_inc(wide_ready, 1)
                st.link(dve.memset(c_t[:], 0.0))
                cr = at(m.par, "c_re").rearrange("p (n h) -> p n h", h=G16)
                ci = at(m.par, "c_im").rearrange("p (n h) -> p n h", h=G16)
                for g in range(2):
                    s = slice(CH * g, CH * g + CH)
                    h = slice(G16 * g, G16 * g + G16)
                    st.link(ts(c_t[s, 0, :, h], cr[s], 1.0, None, ALU.mult))
                    st.link(ts(c_t[s, 1, :, h], ci[s], -1.0, None, ALU.mult))
                for n in range(4):
                    dve.wait_ge(btr, n + 1)
                    dve.tensor_copy(b_t[:, 0:2, n, :], pb[:, n, 0:2 * P].rearrange("p (a c) -> p a c", a=2))\
                       .then_inc(b_ready, 1)

                def add_skip(q):
                    dve.wait_ge(prods_used, 4 * q + 4)
                    dve.scalar_tensor_tensor(m.u_t[:, q, :], m.u_t[:, q, :], at(m.par, "s5_d")[:, q:q + 1], py[:, q % 2, :],
                                             ALU.mult, ALU.add).then_inc(y_used, 1)

                dve.wait_ge(copied, 4)
                dve.wait_ge(filled, 16 * EXTRA)
                for i in range(NS5 + 1):
                    if i < NS5:
                        if i:
                            dve.wait_ge(table, 2 * i)
                        st.link(ts(turn[:], m.t_row[:], TURN[:, i:i + 1], None, ALU.mult))
                        st.link(ts(near[:], turn[:], ROUND, -ROUND, ALU.add, ALU.add))
                        tt(turn[:], turn[:], near[:], ALU.subtract).then_inc(turn_ready, 1)
                    if i == 0:
                        continue
                    j = i - 1
                    cs, sn = cos[:, j % 2, :], sin[:, j % 2, :]
                    b_re, b_im = pb[:, 2 * (j % 2), :], pb[:, 2 * (j % 2) + 1, :]
                    dve.wait_ge(table, 2 * j + 2)
                    dve.wait_ge(bu, j + 1)
                    if j >= 2:
                        dve.wait_ge(prods_used, j - 1)
                    t0, t1 = prod[j % 2][:, 0, :], prod[j % 2][:, 1, :]
                    st.link(tt(t0, b_re, cs, ALU.mult))
                    st.link(tt(t1, b_im, sn, ALU.mult))
                    st.link(tt(t0, t0, t1, ALU.add))
                    st.link(dve.tensor_tensor_scan(zre[:], RHO[:, j:j + 1].to_broadcast([P, T]), t0, 0.0, ALU.mult, ALU.add))
                    st.link(tt(t0, b_im, cs, ALU.mult))
                    bu_last = tt(t1, b_re, sn, ALU.mult)
                    bu_last.then_inc(bu_used, 1)
                    dve.wait_ge(bu_used, j + 1)
                    st.link(tt(t0, t0, t1, ALU.subtract))
                    st.link(dve.tensor_tensor_scan(zim[:], RHO[:, j:j + 1].to_broadcast([P, T]), t0, 0.0, ALU.mult, ALU.add))
                    for n, (tab, sign, z) in enumerate(((cs, 1.0, zre), (sn, -1.0, zim), (sn, 1.0, zre), (cs, 1.0, zim))):
                        dve.scalar_tensor_tensor(prod[j % 2][:, n, :], tab, sign, z[:], ALU.mult, ALU.mult).then_inc(prods, 1)
                    dve.wait_ge(prods, 4 * j + 4)
                    if i % 4 == 1 and i > 4:
                        add_skip((i - 5) // 4)
                add_skip(3)
                for q in range(4):
                    dve.wait_ge(sig, q + 1)
                    tt(m.y_t[:, q, :], m.u_t[:, q, :], prod[1][:, q, :], ALU.mult).then_inc(yout, 1)

            @block.scalar
            def _(act):
                st = Steps(act, aown)

                def copy_out(n):
                    product_of(act, n)
                    act.activation(dst[n], pp[:, n % 2, :], ACT.Copy).then_inc(copied, 1)

                st.link(act.activation(half_pi[:], m.ones[:, 0:1], ACT.Copy, scale=TWO_PI / 4))
                act.activation(STEP, at(m.par, "log_step"), ACT.Exp).then_inc(lam_a, 1)
                copy_out(0)
                copy_out(1)
                act.wait_ge(lam_v, 1)
                st.link(act.activation(HS, R, ACT.Sin, scale=0.5))
                act.activation(SN, R, ACT.Sin).then_inc(lam_a, 1)
                copy_out(2)
                copy_out(3)
                for i in range(NS5):
                    act.wait_ge(turn_ready, i + 1)
                    if i >= 2:
                        act.wait_ge(prods, 4 * (i - 1))
                    act.activation(sin[:, i % 2, :], turn[:], ACT.Sin, scale=TWO_PI).then_inc(table, 1)
                    st.link(act.activation(near[:], turn[:], ACT.Abs))
                    act.activation(cos[:, i % 2, :], near[:], ACT.Sin, scale=-TWO_PI, bias=half_pi[:]).then_inc(table, 1)
                    if 1 < i < 14:
                        act.wait_ge(conv, i - 1)
                        act.activation(m.qkv[:, i - 2, :], conved[:, i % 2, :], ACT.Silu).then_inc(sil, 1)
                    if i == 13:
                        act.wait_ge(conv, 12)
                    if i == 14:
                        act.wait_ge(sil, 12)
                    if i < 12:
                        product_of(act, 4 + i)
                        if i >= 2:
                            act.wait_ge(sil, i - 1)
                        act.activation(conved[:, i % 2, :], pp[:, i % 2, :], ACT.Copy,
                                       scale=at(m.par, "conv_w")[:, 4 * i + 3:4 * i + 4]).then_inc(term, 1)
                    copy_out(4 + i)
                for q in range(4):
                    act.wait_ge(y_used, q + 1)
                    act.activation(m.u_t[:, q, :], m.u_t[:, q, :], ACT.Gelu_apprx_tanh).then_inc(gel, 1)
                for q in range(4):
                    if q == 3:
                        m.stream.wait_used(act, GLU0)
                    else:
                        act.wait_ge(gel_mm, q + 1)
                    act.activation(prod[1][:, q, :], pb[:, q, :], ACT.Sigmoid, bias=at(m.par, "b_glu")[:, q:q + 1])\
                       .then_inc(sig, 1)

            @block.tensor
            def _(pe):
                def product(n):
                    c, j = IN0 + n // 4, n % 4
                    w = m.ring[:, c % RING, :].rearrange("p (k n) -> p k n", k=KD)
                    if j == 0:
                        m.stream.wait(pe, c)
                    if n >= 2:
                        pe.wait_ge(copied, n - 1)
                    for k in range(KD):
                        last = pe.matmul(pp[:, n % 2, :], w[:, k, j * P:(j + 1) * P], m.a_t[:, k, :],
                                         start=(k == 0), stop=(k == KD - 1))
                    if j == 3:
                        m.stream.free(last, c)
                    else:
                        last.then_inc(mm, 1)

                for t in range(NT):
                    for k in range(KD):
                        last = pe.matmul(pb[:, 0, t * 8:t * 8 + 8], m.a_t[:, k, t * P:(t + 1) * P],
                                         at(m.par, "w_gates")[:, k * 8:k * 8 + 8], start=(k == 0), stop=(k == KD - 1))
                last.then_inc(gm, 1)
                for n in range(4):
                    product(n)
                pe.wait_ge(gev, 1)
                pe.wait_ge(wide_ready, 2)
                for n in range(4):
                    for r in range(2):
                        last = pe.transpose(pb[:, n, r * P:(r + 1) * P],
                                            wide[:, r, 4 * n:4 * n + 4, :].rearrange("p a b -> p (a b)"), m.ident[:])
                    last.then_inc(btr, 1)
                pe.wait_ge(b_ready, 4)

                def inputs(i):
                    s = slice(32 * (i % 4), 32 * (i % 4) + 32)
                    if i >= 2:
                        pe.wait_ge(bu_used, i - 1)
                    for r in range(2):
                        last = pe.matmul(pb[:, 2 * (i % 2) + r, :], b_t[s, r, i // 4, :], m.u_t[s, i // 4, :],
                                         start=True, stop=True)
                    last.then_inc(bu, 1)

                def outputs(i):
                    q, s = i // 4, slice(32 * (i % 4), 32 * (i % 4) + 32)
                    pe.wait_ge(prods, 4 * i + 4)
                    if i % 4 == 0 and q >= 2:
                        pe.wait_ge(y_used, q - 1)
                    for n, w in enumerate((0, 0, 1, 1)):
                        last = pe.matmul(py[s, q % 2, :], c_t[:, w, i, :], prod[i % 2][:, n, :], start=(n == 0), stop=(n == 3))
                    last.then_inc(prods_used, 1)

                pe.wait_ge(copied, 4)
                inputs(0)
                for i in range(NS5):
                    product(4 + i)
                    if i + 1 < NS5:
                        inputs(i + 1)
                    if i:
                        outputs(i - 1)
                outputs(NS5 - 1)
                pe.wait_ge(gel, 4)
                m.stream.wait(pe, GLU0)
                w = m.ring[:, GLU0 % RING, 0:2048].rearrange("p (k n) -> p k n", k=4)
                pe.wait_ge(bu_used, NS5)
                for q in range(4):
                    for k in range(4):
                        last = pe.matmul(pb[:, q, :], w[:, k, q * P:(q + 1) * P], m.u_t[:, k, :], start=(k == 0), stop=(k == 3))
                    if q == 3:
                        m.stream.free(last, GLU0)
                    else:
                        last.then_inc(gel_mm, 1)


def delta_rule(nc, m):
    with ExitStack() as ctx:
        sb = lambda name, shape: ctx.enter_context(nc.sbuf_tensor(f"dr_{name}", shape, F32))
        g = Shared()
        by_head = lambda ap: ap.rearrange("p t (h n) -> p t h n", h=NH)
        g.lt = by_head(sb("lt", [P, NT, HALF])[:])
        g.xt = by_head(sb("xt", [P, NT, HALF])[:])
        g.qk = by_head(sb("qk", [P, NT, HALF])[:])
        g.xi = by_head(m.spare.rearrange("p (t n) -> p t n", t=NT))
        g.w = by_head(m.u_t[:])
        g.s = sb("s", [P, 2, HALF])
        g.tmp = sb("tmp", [P, 2, HALF])
        g.col = sb("col", [P, 12, NT * NH])
        g.gl = sb("gl", [P, NT, NH, 2])
        g.ps = ctx.enter_context(nc.psum_tensor("dr_ps", [P, 8, HALF], F32))
        lengths_and_gates(nc, m, g)
        decay_and_scores(nc, m, g)
        invert(nc, m, g)
        values(nc, m, g)
        recur(nc, m, g)
        gate_output(nc, m, g)


def lengths_and_gates(nc, m, g):
    with ExitStack() as ctx:
        sem = lambda name: ctx.enter_context(nc.semaphore(f"cv_{name}"))
        sq, ssum, rec, root, lens, normed = (sem(n) for n in ("sq", "ssum", "rec", "root", "lens", "normed"))
        length = g.w[0:8, 0].rearrange("p h n -> p (h n)")
        own, aown, ga, gv, gm, gc, gd = (sem(n) for n in ("own", "aown", "ga", "gv", "gm", "gc", "gd"))
        tmp = m.y_t
        (AD, NAB, SP, G, BETA, GC, EGC, BG, DT, EKT, EA, REL) = (g.col[:, n, :] for n in range(12))
        gates = m.gates[:].rearrange("p (t n) -> p t n", t=NT)
        v3 = lambda ap: ap.rearrange("p (t h) -> p t h", t=NT)
        g.G, g.BETA, g.GC, g.BG, g.EKT = G, BETA, GC, BG, EKT
        with nc.Block() as block:

            @block.scalar
            def _(act):
                st = Steps(act, aown)
                act.activation(v3(BETA), gates[:, :, 4:8], ACT.Sigmoid).then_inc(ga, 1)
                act.wait_ge(gv, 1)
                st.link(act.activation(NAB, AD, ACT.Abs))
                st.link(act.activation(NAB, NAB, ACT.Exp, scale=-1.0))
                st.link(act.activation(SP, NAB, ACT.Ln, bias=1.0))
                act.activation(EA[:, 0:NH], row_at(m.rows, "a_log"), ACT.Exp).then_inc(ga, 1)
                for n in range(8):
                    if n >= 4:
                        act.wait_ge(ssum, n - 3)
                    act.activation(tmp[:, 4 + n % 4, :], m.qkv[:, n, :], ACT.Square).then_inc(sq, 1)
                act.wait_ge(gc, 1)
                act.activation(EGC, GC, ACT.Exp).then_inc(gd, 1)
                act.activation(EKT, DT, ACT.Exp).then_inc(gd, 1)
                act.wait_ge(rec, 1)
                act.activation(length, length, ACT.Sqrt).then_inc(root, 1)

            @block.vector
            def _(dve):
                st = Steps(dve, own)
                ts, tt, stt = dve.tensor_scalar, dve.tensor_tensor, dve.scalar_tensor_tensor
                tt(v3(AD), gates[:, :, 0:4], rows_of(row_at(m.rows, "dt_bias"), NT), ALU.add).then_inc(gv, 1)
                dve.wait_ge(ga, 2)
                st.link(stt(SP, AD, 0.0, SP, ALU.max, ALU.add))
                tt(v3(G), v3(SP), rows_of(EA[:, 0:NH], NT), ALU.mult).then_inc(gv, 1)
                dve.wait_ge(gv, 2)
                st.link(ts(G, G, -1.0, None, ALU.mult))
                dve.tensor_scalar(REL, G, 1.0, None, ALU.mult).then_inc(gv, 1)
                dve.wait_ge(gm, 1)
                st.link(dve.tensor_copy(GC, g.ps[:, 2, 0:16]))
                tt(DT, g.ps[:, 2, 16:32], GC, ALU.subtract).then_inc(gc, 1)
                dve.wait_ge(gd, 1)
                st.link(tt(BG, BETA, EGC, ALU.mult))
                dve.wait_ge(ssum, 8)
                st.link(ts(length, g.ps[0:8, 0, :], EPS, None, ALU.add))
                dve.reciprocal(length, length).then_inc(rec, 1)
                for n in range(8):
                    dve.wait_ge(lens, n + 1)
                    q = m.qkv[:, n, :]
                    stt(q, q, P ** -0.5 if n < 4 else 1.0, g.ps[:, 4 + n % 4, :], ALU.mult, ALU.mult).then_inc(normed, 1)

            @block.tensor
            def _(pe):
                pe.wait_ge(gv, 3)
                pe.matmul(g.ps[:, 2, 0:16], m.upto[:], G, start=True, stop=True)
                pe.matmul(g.ps[:, 2, 16:32], m.same[:], G, start=True, stop=True).then_inc(gm, 1)
                for n in range(8):
                    pe.wait_ge(sq, n + 1)
                    pe.matmul(g.ps[0:8, 0, :], m.strip[:, 7 - n:15 - n], tmp[:, 4 + n % 4, :], start=(n == 0), stop=(n == 7))\
                      .then_inc(ssum, 1)
                pe.wait_ge(root, 1)
                for n in range(8):
                    if n >= 4:
                        pe.wait_ge(normed, n - 3)
                    pe.matmul(g.ps[:, 4 + n % 4, :], m.ident[0:8, n:n + 1].to_broadcast([8, P]), length, start=True, stop=True)\
                      .then_inc(lens, 1)


def decay_and_scores(nc, m, g):
    with ExitStack() as ctx:
        sem = lambda name: ctx.enter_context(nc.semaphore(f"ds_{name}"))
        rows, scores, diff, dec, masked, lt, x1, xi_ps, xi_ev, egr, qd, own, pown = \
            (sem(n) for n in ("rows", "sc", "diff", "dec", "msk", "lt", "x1", "xp", "xe", "egr", "qd", "own", "pown"))
        eg = m.y_t[:, 6, :]
        h4 = lambda ap: ap.rearrange("p (h n) -> p h n", h=NH)
        with nc.Block() as block:

            @block.gpsimd
            def _(pool):
                st = Steps(pool, pown)
                for t in range(NT):
                    pool.wait_ge(dec, t + 1)
                    d = h4(g.tmp[:, t % 2, :])
                    pool.tensor_tensor(d, d, rows_of(m.upto[:], NH), ALU.mult).then_inc(masked, 1)
                    pool.wait_ge(lt, t + 1)
                    st.link(pool.tensor_tensor(g.xt[:, t], g.lt[:, t], rows_of(m.level[:, 0, :], NH), ALU.mult))
                    pool.tensor_tensor(g.xt[:, t], rows_of(m.ident[:], NH), g.xt[:, t], ALU.subtract).then_inc(x1, 1)

            @block.tensor
            def _(pe):
                for t in range(NT):
                    b = 4 * (t % 2)
                    s = slice(t * P, (t + 1) * P)
                    if t >= 2:
                        pe.wait_ge(lt, t - 1)
                        pe.wait_ge(egr, t - 1)
                    for h in range(NH):
                        n = slice(h * P, (h + 1) * P)
                        c = slice(4 * t + h, 4 * t + h + 1)
                        pe.matmul(g.ps[:, b, n], g.G[:, c].to_broadcast([P, P]), m.upto[:], start=True, stop=True)
                        last = pe.matmul(g.ps[:, b + 1, n], g.BETA[:, c].to_broadcast([P, P]), m.ident[:], start=True, stop=True)
                    last.then_inc(rows, 1)
                    for h in range(NH):
                        n = slice(h * P, (h + 1) * P)
                        k = m.qkv[:, 4 + h, s]
                        pe.matmul(g.ps[:, b + 2, n], k, k, start=True, stop=True)
                        last = pe.matmul(g.ps[:, b + 3, n], k, m.qkv[:, h, s], start=True, stop=True)
                    last.then_inc(scores, 1)
                for t in range(NT):
                    pe.wait_ge(x1, t + 1)
                    pe.wait_ge(lt, NT)
                    for h in range(NH):
                        last = pe.transpose(g.ps[:, t, h * P:(h + 1) * P], g.xt[:, t, h, :], m.ident[:])
                    last.then_inc(xi_ps, 1)

            @block.vector
            def _(dve):
                st = Steps(dve, own)
                tt = dve.tensor_tensor
                for t in range(NT):
                    b = 4 * (t % 2)
                    d = h4(g.tmp[:, t % 2, :])
                    dve.wait_ge(rows, t + 1)
                    if t >= 2:
                        dve.wait_ge(lt, t - 1)
                    st.link(tt(d, h4(g.ps[:, b, :]), over(g.GC[:, 4 * t:4 * t + 4], P), ALU.subtract))
                    dve.tensor_scalar(d, d, 0.0, None, ALU.min).then_inc(diff, 1)
                    dve.wait_ge(egr, t + 1)
                    dve.wait_ge(scores, t + 1)
                    q = m.qkv[:, 0:NH, t * P:(t + 1) * P]
                    dve.tensor_copy(g.gl[:, t], h4(eg).rearrange("p h (c n) -> p h c n", c=2)[:, :, :, CH - 1]).then_inc(qd, 1)
                    dve.tensor_tensor(q, q, h4(eg), ALU.mult).then_inc(qd, 1)
                    dve.wait_ge(masked, t + 1)
                    st.link(tt(g.lt[:, t], h4(g.ps[:, b + 2, :]), d, ALU.mult))
                    st.link(tt(g.qk[:, t], h4(g.ps[:, b + 3, :]), d, ALU.mult))
                    tt(g.lt[:, t], g.lt[:, t], h4(g.ps[:, b + 1, :]), ALU.mult).then_inc(lt, 1)

            @block.scalar
            def _(act):
                for t in range(NT):
                    b = 4 * (t % 2)
                    act.wait_ge(diff, t + 1)
                    d = g.tmp[:, t % 2, :]
                    act.activation(d, d, ACT.Exp).then_inc(dec, 1)
                    if t:
                        act.wait_ge(qd, 2 * t)
                    act.activation(eg, g.ps[:, b, :], ACT.Exp).then_inc(egr, 1)
                for t in range(NT):
                    act.wait_ge(xi_ps, t + 1)
                    act.activation(g.xi[:, t], g.ps[:, t, :].rearrange("p (h n) -> p h n", h=NH), ACT.Copy).then_inc(xi_ev, 1)


def invert(nc, m, g):
    LV = 5
    steps = [(lv, t) for lv in range(1, LV + 1) for t in range(NT)]
    with ExitStack() as ctx:
        sem = lambda name: ctx.enter_context(nc.semaphore(f"iv_{name}"))
        cm_ready, cx, w_ev, upd, done = (sem(n) for n in ("cm", "cx", "wev", "upd", "done"))
        cm = m.y_t[:, 4:6, :]
        h4 = lambda ap: ap.rearrange("p (h n) -> p h n", h=NH)

        def updates(i):
            return 2 * (i + 1) - max(0, i + 1 - (LV - 1) * NT)

        with nc.Block() as block:

            @block.gpsimd
            def _(pool):
                for i, (lv, t) in enumerate(steps):
                    if i >= 2:
                        pool.wait_ge(cx, i - 1)
                    pool.tensor_tensor(h4(cm[:, i % 2, :]), g.lt[:, t], rows_of(m.level[:, lv, :], NH), ALU.mult)\
                        .then_inc(cm_ready, 1)

            @block.tensor
            def _(pe):
                def first(i):
                    lv, t = steps[i]
                    pe.wait_ge(cm_ready, i + 1)
                    if i >= 2:
                        pe.wait_ge(w_ev, i - 1)
                    if lv > 1:
                        pe.wait_ge(done, updates(i - NT))
                    for h in range(NH):
                        last = pe.matmul(g.ps[:, i % 2, h * P:(h + 1) * P], cm[:, i % 2, h * P:(h + 1) * P], g.xi[:, t, h, :],
                                         start=True, stop=True)
                    last.then_inc(cx, 1)

                def second(i):
                    lv, t = steps[i]
                    pe.wait_ge(w_ev, i + 1)
                    if i >= 2:
                        pe.wait_ge(done, updates(i - 2))
                    for h in range(NH):
                        n = slice(h * P, (h + 1) * P)
                        if lv < LV:
                            pe.matmul(g.ps[:, 2 + 2 * (i % 2), n], g.xt[:, t, h, :], g.w[:, t, h, :], start=True, stop=True)
                        last = pe.matmul(g.ps[:, 3 + 2 * (i % 2), n], g.w[:, t, h, :], g.xt[:, t, h, :], start=True, stop=True)
                    last.then_inc(upd, 1)

                first(0)
                for i in range(len(steps)):
                    if i + 1 < len(steps):
                        first(i + 1)
                    second(i)

            @block.scalar
            def _(act):
                for i, (lv, t) in enumerate(steps):
                    act.wait_ge(cx, i + 1)
                    if lv > 1:
                        act.wait_ge(upd, i - NT + 1)
                    act.activation(g.w[:, t], h4(g.ps[:, i % 2, :]), ACT.Copy).then_inc(w_ev, 1)

            @block.vector
            def _(dve):
                for i, (lv, t) in enumerate(steps):
                    dve.wait_ge(upd, i + 1)
                    if lv < LV:
                        dve.tensor_tensor(g.xi[:, t], g.xi[:, t], h4(g.ps[:, 2 + 2 * (i % 2), :]), ALU.subtract).then_inc(done, 1)
                    dve.tensor_tensor(g.xt[:, t], g.xt[:, t], h4(g.ps[:, 3 + 2 * (i % 2), :]), ALU.subtract).then_inc(done, 1)


def values(nc, m, g):
    with ExitStack() as ctx:
        sem = lambda name: ctx.enter_context(nc.semaphore(f"vl_{name}"))
        tr, sc, mm, ev = (sem(n) for n in ("tr", "sc", "mm", "ev"))
        vb, kb = m.y_t[:, 4:6, :], m.y_t[:, 6:8, :]
        h4 = lambda ap: ap.rearrange("p (h n) -> p h n", h=NH)
        with nc.Block() as block:

            @block.tensor
            def _(pe):
                def turn(t):
                    s = slice(t * P, (t + 1) * P)
                    if t >= 2:
                        pe.wait_ge(sc, 3 * (t - 1))
                    for h in range(NH):
                        n = slice(h * P, (h + 1) * P)
                        pe.transpose(g.ps[:, 2 * (t % 2), n], m.qkv[:, 8 + h, s], m.ident[:])
                        last = pe.transpose(g.ps[:, 2 * (t % 2) + 1, n], m.qkv[:, 4 + h, s], m.ident[:])
                    last.then_inc(tr, 1)

                turn(0)
                for t in range(NT):
                    if t + 1 < NT:
                        turn(t + 1)
                    pe.wait_ge(sc, 3 * t + 3)
                    if t >= 2:
                        pe.wait_ge(ev, 2 * (t - 1))
                    b = 4 + 2 * (t % 2)
                    for h in range(NH):
                        n = slice(h * P, (h + 1) * P)
                        pe.matmul(g.ps[:, b, n], g.xt[:, t, h, :], vb[:, t % 2, n], start=True, stop=True)
                        last = pe.matmul(g.ps[:, b + 1, n], kb[:, t % 2, n], g.xt[:, t, h, :], start=True, stop=True)
                    last.then_inc(mm, 1)

            @block.vector
            def _(dve):
                for t in range(NT):
                    dve.wait_ge(tr, t + 1)
                    if t >= 2:
                        dve.wait_ge(mm, t - 1)
                    c = slice(4 * t, 4 * t + 4)
                    pv, pk = h4(g.ps[:, 2 * (t % 2), :]), h4(g.ps[:, 2 * (t % 2) + 1, :])
                    dve.tensor_tensor(h4(vb[:, t % 2, :]), pv, over(g.BETA[:, c], P), ALU.mult).then_inc(sc, 1)
                    dve.tensor_tensor(h4(kb[:, t % 2, :]), pk, over(g.BG[:, c], P), ALU.mult).then_inc(sc, 1)
                    dve.tensor_tensor(g.lt[:, t], pk, over(g.EKT[:, c], P), ALU.mult).then_inc(sc, 1)

            @block.scalar
            def _(act):
                for t in range(NT):
                    act.wait_ge(mm, t + 1)
                    b = 4 + 2 * (t % 2)
                    act.activation(g.xi[:, t], h4(g.ps[:, b, :]), ACT.Copy).then_inc(ev, 1)
                    act.activation(g.w[:, t], h4(g.ps[:, b + 1, :]), ACT.Copy).then_inc(ev, 1)


def recur(nc, m, g):
    NCH = T // CH
    with ExitStack() as ctx:
        sem = lambda name: ctx.enter_context(nc.semaphore(f"rc_{name}"))
        vp, vn_r, so, oo, o_ev, sg_r, s_r = (sem(n) for n in ("vp", "vn", "so", "oo", "oev", "sg", "s"))
        vn = g.tmp
        h4 = lambda ap: ap.rearrange("p (h n) -> p h n", h=NH)
        with nc.Block() as block:

            @block.tensor
            def _(pe):
                for c in range(NCH):
                    t, s = c // 2, slice(CH * (c % 2), CH * (c % 2) + CH)
                    col = slice(CH * c, CH * c + CH)
                    state = g.s[:, c % 2, :]
                    if c:
                        pe.wait_ge(s_r, c)
                        for h in range(NH):
                            n = slice(h * P, (h + 1) * P)
                            last = pe.matmul(g.ps[s, c % 2, n], g.w[:, t, h, s], state[:, n], start=True, stop=True)
                        last.then_inc(vp, 1)
                        if c >= 2:
                            pe.wait_ge(o_ev, c - 1)
                    po = h4(g.ps[:, 2 + c % 2, 0:NH * CH])
                    pe.wait_ge(vn_r, c + 1)
                    if c < NCH - 1:
                        for h in range(NH):
                            n = slice(h * P, (h + 1) * P)
                            last = pe.matmul(g.ps[:, 4 + c % 2, n], g.lt[s, t, h, :], vn[s, c % 2, n], start=True, stop=True)
                        last.then_inc(so, 1)
                    for h in range(NH):
                        n = slice(h * P, (h + 1) * P)
                        if c:
                            pe.matmul(po[:, h, :], state[:, n], m.qkv[:, h, col], start=True, stop=False)
                        last = pe.matmul(po[:, h, :], vn[s, c % 2, n], g.qk[s, t, h, s], start=(c == 0), stop=True)
                    last.then_inc(oo, 1)

            @block.vector
            def _(dve):
                for c in range(NCH):
                    t, s = c // 2, slice(CH * (c % 2), CH * (c % 2) + CH)
                    if c >= 2:
                        dve.wait_ge(oo, c - 1)
                    if c == 0:
                        dve.tensor_copy(h4(vn[s, 0, :]), g.xi[s, t]).then_inc(vn_r, 1)
                    else:
                        dve.wait_ge(vp, c)
                        dve.tensor_tensor(h4(vn[s, c % 2, :]), g.xi[s, t], h4(g.ps[s, c % 2, :]), ALU.subtract).then_inc(vn_r, 1)
                    if c < NCH - 1:
                        if c == 0:
                            dve.wait_ge(so, 1)
                            dve.tensor_copy(g.s[:, 1, :], g.ps[:, 4, :]).then_inc(s_r, 1)
                        else:
                            dve.wait_ge(oo, c)
                            dve.tensor_tensor(h4(g.s[:, (c + 1) % 2, :]), h4(g.s[:, c % 2, :]), over(g.gl[:, t, :, c % 2], P),
                                              ALU.mult).then_inc(sg_r, 1)
                            dve.wait_ge(sg_r, c)
                            dve.wait_ge(so, c + 1)
                            dve.tensor_tensor(g.s[:, (c + 1) % 2, :], g.s[:, (c + 1) % 2, :], g.ps[:, 4 + c % 2, :], ALU.add)\
                               .then_inc(s_r, 1)

            @block.scalar
            def _(act):
                for c in range(NCH):
                    act.wait_ge(oo, c + 1)
                    act.activation(m.y_t[:, 4:8, CH * c:CH * c + CH], h4(g.ps[:, 2 + c % 2, 0:NH * CH]), ACT.Copy)\
                       .then_inc(o_ev, 1)


def gate_output(nc, m, g):
    with ExitStack() as ctx:
        sem = lambda name: ctx.enter_context(nc.semaphore(f"go_{name}"))
        sq, ssum, rec, root, rms, zs, own, fin = (sem(n) for n in ("sq", "ssum", "rec", "root", "rms", "zs", "own", "fin"))
        scale = g.w[0:8, 0].rearrange("p h n -> p (h n)")
        sqb = [g.tmp[:, 0, :], g.tmp[:, 1, :], g.s[:, 0, :], g.s[:, 1, :]]
        with nc.Block() as block:

            @block.scalar
            def _(act):
                for h in range(NH):
                    act.activation(sqb[h], m.y_t[:, 4 + h, :], ACT.Square).then_inc(sq, 1)
                for h in range(NH):
                    act.activation(m.z_t[:, h, :], m.z_t[:, h, :], ACT.Silu).then_inc(zs, 1)
                act.wait_ge(rec, 1)
                act.activation(scale, scale, ACT.Sqrt).then_inc(root, 1)

            @block.tensor
            def _(pe):
                for h in range(NH):
                    pe.wait_ge(sq, h + 1)
                    last = pe.matmul(g.ps[0:8, 4, :], m.strip[:, 7 - h:15 - h], sqb[h], start=(h == 0), stop=(h == NH - 1))
                last.then_inc(ssum, 1)
                pe.wait_ge(root, 1)
                for h in range(NH):
                    pe.matmul(g.ps[:, h, :], m.ident[0:8, h:h + 1].to_broadcast([8, P]), scale, start=True, stop=True)\
                      .then_inc(rms, 1)

            @block.vector
            def _(dve):
                st = Steps(dve, own)
                dve.wait_ge(ssum, 1)
                st.link(dve.tensor_scalar(scale, g.ps[0:8, 4, :], 1.0 / P, EPS, ALU.mult, ALU.add))
                dve.reciprocal(scale, scale).then_inc(rec, 1)
                for h in range(NH):
                    dve.wait_ge(rms, h + 1)
                    y = m.y_t[:, 4 + h, :]
                    st.link(dve.scalar_tensor_tensor(y, y, at(m.par, "gdn_g"), g.ps[:, h, :], ALU.mult, ALU.mult))
                    dve.wait_ge(zs, h + 1)
                    dve.tensor_tensor(y, y, m.z_t[:, h, :], ALU.mult).then_inc(fin, 1)


def mix_out(nc, m, chunk0=OUT0, gate=None):
    with ExitStack() as ctx:
        sem = lambda name: ctx.enter_context(nc.semaphore(f"mo{chunk0}_{name}"))
        ps = ctx.enter_context(nc.psum_tensor(f"mo{chunk0}_ps", [P, 4, HALF], F32))
        tmp = ctx.enter_context(nc.sbuf_tensor(f"mo{chunk0}_tmp", [P, 2, HALF], F32))
        junk = ctx.enter_context(nc.sbuf_tensor(f"mo{chunk0}_junk", [P, D], F32))
        mm, sc, ev, sq = sem("mm"), sem("sc"), sem("ev"), sem("sq")

        def product_of(eng, n):
            if n < 6:
                eng.wait_ge(mm, n + 1)
            else:
                m.stream.wait_used(eng, chunk0 + n % 2)

        with nc.Block() as block:

            @block.sync
            def _(sp):
                if gate is None:
                    m.stream.load(sp, chunk0 + RING + 2, chunk0 + RING + 4)
                m.stream.load(sp, chunk0 + RING, chunk0 + RING + 2)

            @block.tensor
            def _(pe):
                for n in range(2 * NT):
                    t, c = n // 2, n % 2
                    if t == 0:
                        m.stream.wait(pe, chunk0 + c)
                    if n >= 4:
                        pe.wait_ge(ev, n - 3)
                    w = m.ring[:, (chunk0 + c) % RING, :].rearrange("p (k n) -> p k n", k=KD)
                    for k in range(KD):
                        last = pe.matmul(ps[:, n % 4, :], m.y_t[:, k, t * P:(t + 1) * P], w[:, k, :], start=(k == 0),
                                         stop=(k == KD - 1))
                    if t == NT - 1:
                        m.stream.free(last, chunk0 + c)
                    else:
                        last.then_inc(mm, 1)

            @block.scalar
            def _(act):
                for t in range(NT):
                    act.wait_ge(ev, 2 * t + 2)
                    sum_squares(act, m, t, junk, sq)
                act.wait_ge(sq, NT)

            @block.vector
            def _(dve):
                for n in range(2 * NT):
                    t, c = n // 2, n % 2
                    product_of(dve, n)
                    x = m.x[:, t, c * HALF:(c + 1) * HALF]
                    y = ps[:, n % 4, :]
                    if gate is not None:
                        if n >= 2:
                            dve.wait_ge(ev, n - 1)
                        y = tmp[:, n % 2, :]
                        dve.tensor_tensor(y, ps[:, n % 4, :], gate[:, c * HALF:(c + 1) * HALF], ALU.mult).then_inc(sc, 1)
                        dve.wait_ge(sc, n + 1)
                    dve.tensor_tensor(x, x, y, ALU.add).then_inc(ev, 1)


def route(nc, m, c):
    NE, NG, EG = c.NE, c.NG, c.EG
    NL, NS = NG + NE, NE + EXTRA
    with ExitStack() as ctx:
        sem = lambda name: ctx.enter_context(nc.semaphore(f"{c.tag}r_{name}"))
        sb = lambda name, shape, dt=F32: ctx.enter_context(nc.sbuf_tensor(f"{c.tag}r_{name}", shape, dt))
        ps = ctx.enter_context(nc.psum_tensor(f"{c.tag}r_ps", [P, 3, HALF], F32))
        logit, ready, a_done, v_done, own, rank, hot, table = (sem(n) for n in ("lg", "ready", "act", "v", "own", "rank", "hot", "tab"))
        gl, goh, gex, gpen = (sb(n, [P, NT, NG]) for n in ("gl", "goh", "gex", "gpen"))
        el, oh1, oh2, cand, slots = (sb(n, [P, NT, NE]) for n in ("el", "oh1", "oh2", "cand", "slots"))
        both = sb("both", [P, NT, NE])
        one = sb("one", [P, 12, NT])
        (GMAX, GI, PSUM_, V1, I1, V2, I2, E2, R, DV, RLO, TMP) = (one[:, n, :] for n in range(12))
        iot, iot_far = sb("iot", [P, NS]), sb("iotf", [P, NS])
        r128 = sb("r128", [P, P])
        ids = sb("ids", [P, NT])
        ext = sb("ext", [P, 6, NE])
        (CNT, EX, INC, OFF1, DOFF, FAR) = (ext[:, n, :] for n in range(6))
        slot2, job2, lo2 = sb("slot2", [P, NT, 2]), sb("job2", [P, NT, 2]), sb("lo2", [P, NT, 2])
        roh, joh = sb("roh", [P, NT * 2, P]), sb("joh", [P, NT * 2, NS])
        ovf = sb("ovf", [1, 1 + EXTRA])
        in_x = sb("in_x", [1, 2, NE])
        flat = lambda ap: ap.rearrange("p a b -> p (a b)")
        e4 = lambda ap: ap.rearrange("p t (g e) -> p (t g) e", g=NG)
        with nc.Block() as block:

            @block.gpsimd
            def _(pool):
                for ap, pat, base, chan in ((iot[:], [[1, NS]], 0, 0), (iot_far[:], [[1, NS]], 64, 0), (r128[:], [[1, P]], 0, 0),
                                            (ids[:], [[P, NT]], 0, 1), (OFF1, [[P, NE]], 0, 0)):
                    pool.iota(ap, pat, base=base, channel_multiplier=chan, allow_small_or_imprecise_dtypes=True).then_inc(ready, 1)

            @block.tensor
            def _(pe):
                w = at(m.par, c.router).rearrange("p (k n) -> p k n", k=KD)
                for t in range(NT):
                    for k in range(KD):
                        last = pe.matmul(ps[:, 0, t * NL:(t + 1) * NL], m.a_t[:, k, t * P:(t + 1) * P], w[:, k, :],
                                         start=(k == 0), stop=(k == KD - 1))
                last.then_inc(logit, 1)
                pe.wait_ge(v_done, 2)
                for t in range(NT):
                    for i in range(t + 1):
                        pe.matmul(ps[:, 1, t * NE:(t + 1) * NE], (m.tri if i == t else m.ones)[:], both[:, i, :],
                                  start=(i == 0), stop=(i == t))
                for i in range(NT):
                    last = pe.matmul(ps[:, 1, NT * NE:(NT + 1) * NE], m.ones[:], both[:, i, :], start=(i == 0), stop=(i == NT - 1))
                last.then_inc(rank, 1)
                pe.wait_ge(hot, 1)
                for i in range(2 * NT):
                    last = pe.matmul(ps[:, 2, 0:NS], roh[:, i, :], joh[:, i, :], start=(i == 0), stop=(i == 2 * NT - 1))
                last.then_inc(table, 1)

            @block.scalar
            def _(act):
                act.wait_ge(v_done, 1)
                act.activation(gex[:], gex[:], ACT.Exp).then_inc(a_done, 1)
                act.wait_ge(v_done, 3)
                act.activation(E2, DV, ACT.Exp).then_inc(a_done, 1)

            @block.vector
            def _(dve):
                st = Steps(dve, own)
                tt, ts, stt, red = dve.tensor_tensor, dve.tensor_scalar, dve.scalar_tensor_tensor, dve.tensor_reduce

                def first_of(values, best, index, hot_out, tmp, n):
                    st.link(tt(tmp, values, over(best, n), ALU.is_ge))
                    st.link(stt(tmp, tmp, -64.0, rows_of(iot_far[:, 0:n], NT), ALU.mult, ALU.add))
                    st.link(red(index, tmp, AX.X, ALU.min))
                    st.link(tt(hot_out, rows_of(iot[:, 0:n], NT), over(index, n), ALU.is_equal))

                dve.wait_ge(ready, 5)
                dve.wait_ge(logit, 1)
                lg = ps[:, 0, 0:NT * NL].rearrange("p (t n) -> p t n", t=NT)
                if c.bias is None:
                    st.link(dve.tensor_copy(gl[:], lg[:, :, 0:NG]))
                    st.link(dve.tensor_copy(el[:], lg[:, :, NG:NL]))
                else:
                    st.link(tt(gl[:], lg[:, :, 0:NG], rows_of(c.bias[:, 0:NG], NT), ALU.add))
                    st.link(tt(el[:], lg[:, :, NG:NL], rows_of(c.bias[:, NG:NL], NT), ALU.add))
                st.link(red(GMAX, gl[:], AX.X, ALU.max))
                tt(gex[:], gl[:], over(GMAX, NG), ALU.subtract).then_inc(v_done, 1)
                first_of(gl[:], GMAX, GI, goh[:], gpen[:], NG)
                st.link(ts(gpen[:], goh[:], BIG, -BIG, ALU.mult, ALU.add))
                st.link(tt(e4(el[:]), e4(el[:]), over(flat(goh[:]), EG), ALU.mult))
                st.link(tt(e4(el[:]), e4(el[:]), over(flat(gpen[:]), EG), ALU.add))
                st.link(red(V1, el[:], AX.X, ALU.max))
                first_of(el[:], V1, I1, oh1[:], cand[:], NE)
                st.link(stt(el[:], oh1[:], -3 * BIG, el[:], ALU.mult, ALU.add))
                st.link(red(V2, el[:], AX.X, ALU.max))
                first_of(el[:], V2, I2, oh2[:], cand[:], NE)
                tt(both[:], oh1[:], oh2[:], ALU.add).then_inc(v_done, 1)
                tt(DV, V2, V1, ALU.subtract).then_inc(v_done, 1)
                dve.wait_ge(rank, 1)
                st.link(dve.tensor_copy(CNT, ps[:, 1, NT * NE:(NT + 1) * NE]))
                st.link(ts(EX, CNT, float(P), None, ALU.is_gt))
                for q in (2.0, 3.0):
                    st.link(stt(EX, CNT, q * P, EX, ALU.is_gt, ALU.add))
                st.link(dve.tensor_tensor_scan(INC, m.ones[:, 0:NE], EX, 0.0, ALU.mult, ALU.add))
                st.link(tt(DOFF, INC, EX, ALU.subtract))
                st.link(ts(FAR, DOFF, float(P), float((NE - 1) * P), ALU.mult, ALU.add))
                st.link(tt(FAR, FAR, OFF1, ALU.subtract))
                rk = ps[:, 1, 0:NT * NE].rearrange("p (t e) -> p t e", t=NT)
                st.link(ts(cand[:], rk, float(P), None, ALU.is_ge))
                st.link(tt(cand[:], cand[:], rows_of(FAR, NT), ALU.mult))
                st.link(tt(slots[:], rk, rows_of(OFF1, NT), ALU.add))
                st.link(tt(slots[:], slots[:], cand[:], ALU.add))
                for k, oh in enumerate((oh1, oh2)):
                    st.link(tt(cand[:], slots[:], oh[:], ALU.mult))
                    st.link(red(slot2[:, :, k], cand[:], AX.X, ALU.add))
                st.link(dve.tensor_copy(c.slot[:], slot2[:]))
                st.link(ts(job2[:], slot2[:], 63.5, 1.0 / P, ALU.subtract, ALU.mult))
                st.link(ts(job2[:], job2[:], ROUND, -ROUND, ALU.add, ALU.add))
                st.link(stt(lo2[:], job2[:], -float(P), slot2[:], ALU.mult, ALU.add))
                st.link(tt(roh[:], rows_of(r128[:], 2 * NT), over(flat(lo2[:]), P), ALU.is_equal))
                st.link(tt(joh[:], rows_of(iot[:], 2 * NT), over(flat(job2[:]), NS), ALU.is_equal))
                j3 = joh[:].rearrange("p (t k) n -> p t (k n)", t=NT)
                tt(j3, j3, over(ids[:], 2 * NS), ALU.mult).then_inc(hot, 1)
                dve.wait_ge(a_done, 2)
                st.link(red(PSUM_, gex[:], AX.X, ALU.add))
                st.link(ts(R, E2, 1.0, None, ALU.add))
                st.link(tt(R, R, PSUM_, ALU.mult))
                st.link(dve.reciprocal(c.wt[:, :, 0], R))
                st.link(tt(c.wt[:, :, 1], c.wt[:, :, 0], E2, ALU.mult))
                st.link(dve.tensor_copy(ovf[:, 0:1], INC[0:1, NE - 1:NE]))
                for n in range(EXTRA):
                    st.link(ts(in_x[:, 0], DOFF[0:1], float(n), None, ALU.is_le))
                    st.link(stt(in_x[:, 1], INC[0:1], float(n), in_x[:, 0], ALU.is_gt, ALU.mult))
                    st.link(tt(in_x[:, 1], in_x[:, 1], iot[0:1, 0:NE], ALU.mult))
                    st.link(red(ovf[:, 1 + n:2 + n], in_x[:, 1], AX.X, ALU.add))
                st.link(dve.tensor_copy(c.over[:], ovf[:]))
                dve.wait_ge(table, 1)
                st.link(dve.tensor_copy(c.token[:], ps[:, 2, 0:NS]))


def experts(nc, m, c):
    NJ, HV = c.NJ, c.HV
    with ExitStack() as ctx:
        sem = lambda name: ctx.enter_context(nc.semaphore(f"{c.tag}x_{name}"))
        sb = lambda name, shape, dt=F32: ctx.enter_context(nc.sbuf_tensor(f"{c.tag}x_{name}", shape, dt))
        xg, xt = sb("xg", [P, 2, D]), sb("xt", [P, KD, P])
        hs, h, ht, ysb = sb("hs", [P, 256]), sb("h", [P, 256]), sb("ht", [P, 2, P]), sb("y", [P, 2, D])
        idx = sb("idx", [P, 2], U32)
        ps = ctx.enter_context(nc.psum_tensor(f"{c.tag}x_ps", [P, 8, HALF], F32))
        got = c.got
        stored = [sem("st0"), sem("st1")]
        idx_r, tr, xa, xd, sl, hr, htr, hte, ya, yd = (sem(n) for n in ("idx", "tr", "xa", "xd", "sl", "hr", "htr", "hte", "ya", "yd"))
        GS, DS = [c.first % RING, (c.first + 2) % RING], [(c.first + 1) % RING, (c.first + 3) % RING]
        G0, D0 = ([m.stream.frees(c.first - RING + o + 2 * u) for u in range(2)] for o in (0, 1))
        with nc.Block() as block:

            def up_done(eng, j, u):
                eng.wait_ge(m.w_free[GS[u]], (j - u) // 2 + 1 + G0[u])

            def down_done(eng, j, u):
                eng.wait_ge(m.w_free[DS[u]], (j - u) // 2 + 1 + D0[u])

            @block.sync
            def _(sp):
                def load_up(j, u):
                    up_done(sp, j - 2, u)
                    sp.dma_start(m.ring[:, GS[u], :], c.gu[bass.ds(j, 1)].rearrange("o p n -> (o p) n")).then_inc(m.w_ready[GS[u]], 16)

                def load_down(j, u):
                    down_done(sp, j - 2, u)
                    sp.dma_start(m.ring[:, DS[u], 0:2048], c.dn[bass.ds(j, 1)].rearrange("o p n -> (o p) n"))\
                      .then_inc(m.w_ready[DS[u]], 16)

                def store(i, v):
                    sp.wait_ge(ya, i + 1)
                    sp.wait_ge(yd, i + 1)
                    sp.dma_start(c.y_rows[bass.ds(i * P, P), :], ysb[:, v, :]).then_inc(stored[v], 16)

                def done(i, u):
                    if HV == 1:
                        store(i * 2 + u, u)
                    elif u == 1:
                        store(i, 0)

                load_up(2, 0)
                with sp.Fori(0, NJ // 2 - 2) as i:
                    for u in range(2):
                        load_up(i * 2 + 3 + u, 1 - u)
                        load_down(i * 2 + 2 + u, u)
                        done(i, u)
                load_up(NJ - 1, 1)
                load_down(NJ - 2, 0)
                done(NJ // 2 - 2, 0)
                load_down(NJ - 1, 1)
                done(NJ // 2 - 2, 1)
                done(NJ // 2 - 1, 0)
                done(NJ // 2 - 1, 1)
                for v in range(3 - HV):
                    sp.wait_ge(stored[v], 16 * NJ // 2)
                m.stream.load(sp, c.first + 2 * NJ, c.first + 2 * NJ + RING)

            @block.gpsimd
            def _(pool):
                def gather(i, v):
                    pool.tensor_copy(idx[:, v:v + 1], c.token[:, bass.ds(i, 1)]).then_inc(idx_r, 1)
                    pool.drain()
                    pool.indirect_dma_start(xg[:, v, :], None, c.x_rows, bass.IndirectOffsetOnAxis(idx[:, v:v + 1], 0))\
                        .then_inc(got[v], 16)

                NI = NJ // HV
                gather(0, 0)
                gather(1, 1)
                with pool.Fori(1, NI // 2) as i:
                    for v in range(2):
                        pool.wait_ge(tr, i * 2 + v - 1)
                        gather(i * 2 + v, v)

            @block.tensor
            def _(pe):
                def turn(i, v, r):
                    pe.wait_ge(got[v], r * 16 + 16)
                    pe.wait_ge(xa, i)
                    pe.wait_ge(xd, i)
                    for k in range(KD):
                        last = pe.transpose(ps[:, k // 4, (k % 4) * P:(k % 4 + 1) * P], xg[:, v, k * P:(k + 1) * P], m.ident[:])
                    last.then_inc(tr, 1)

                def up(j, u, i):
                    pe.wait_ge(m.w_ready[GS[u]], ((j - u) // 2 + 1 + G0[u]) * 16)
                    pe.wait_ge(xa, i + 1)
                    pe.wait_ge(xd, i + 1)
                    w = m.ring[:, GS[u], :].rearrange("p (k n) -> p k n", k=KD)
                    for k in range(KD):
                        last = pe.matmul(ps[:, 2 + u, :], xt[:, k, :], w[:, k, :], start=(k == 0), stop=(k == KD - 1))
                    last.then_inc(m.w_free[GS[u]], 1)

                def turn_h(j):
                    pe.wait_ge(hr, j + 1)
                    for k in range(2):
                        last = pe.transpose(ps[:, 4, k * P:(k + 1) * P], h[:, k * P:(k + 1) * P], m.ident[:])
                    last.then_inc(htr, 1)

                def down(j, u, i):
                    pe.wait_ge(m.w_ready[DS[u]], ((j - u) // 2 + 1 + D0[u]) * 16)
                    pe.wait_ge(hte, j + 1)
                    if HV == 1 or u == 0:
                        pe.wait_ge(ya, i)
                        pe.wait_ge(yd, i)
                    w = m.ring[:, DS[u], 0:2048].rearrange("p (k n) -> p k n", k=2)
                    for k in range(2):
                        for n in range(2):
                            last = pe.matmul(ps[:, 6 + n, :], ht[:, k, :], w[:, k, n * HALF:(n + 1) * HALF],
                                             start=(k == 0 and (HV == 1 or u == 0)), stop=(k == 1 and (HV == 1 or u == 1)))
                    last.then_inc(m.w_free[DS[u]], 1)

                def job(j, u, r, last=False):
                    up(j, u, j)
                    if not last:
                        turn(j + 1, 1 - u, r + u)
                    if not (isinstance(j, int) and j == 0):
                        down(j - 1, 1 - u, j - 1)
                    turn_h(j)

                def halves(i, v, r, last=False):
                    up(i * 2, 0, i)
                    if not (isinstance(i, int) and i == 0):
                        down(i * 2 - 1, 1, i - 1)
                    turn_h(i * 2)
                    up(i * 2 + 1, 1, i)
                    if not last:
                        turn(i + 1, 1 - v, r + v)
                    down(i * 2, 0, i)
                    turn_h(i * 2 + 1)

                NI = NJ // HV
                one = job if HV == 1 else halves
                turn(0, 0, 0)
                one(0, 0, 0)
                one(1, 1, 0)
                with pe.Fori(1, NI // 2 - 1) as r:
                    one(r * 2, 0, r)
                    one(r * 2 + 1, 1, r)
                one(NI - 2, 0, NI // 2 - 1)
                one(NI - 1, 1, NI // 2 - 1, True)
                down(NJ - 1, 1, NI - 1)

            def stores_before(i, v):
                return ((i - v) // 2) * 16 if HV == 1 else i * 16

            def run(eng, x_in, mid, h_t, y_out):
                NI = NJ // HV

                def job(j, u, last=False):
                    mid(j, u)
                    if not last:
                        x_in(j + 1)
                    if not (isinstance(j, int) and j == 0):
                        y_out(j - 1, 1 - u, j - 1, 1 - u)
                    h_t(j)

                def halves(i, v, last=False):
                    mid(i * 2, 0)
                    if not (isinstance(i, int) and i == 0):
                        y_out(i * 2 - 1, 1, i - 1, 0)
                    h_t(i * 2)
                    mid(i * 2 + 1, 1)
                    if not last:
                        x_in(i + 1)
                    h_t(i * 2 + 1)

                one = job if HV == 1 else halves
                x_in(0)
                for i in range(4):
                    one(i, i % 2)
                with eng.Fori(2, NI // 2 - 1) as r:
                    one(r * 2, 0)
                    one(r * 2 + 1, 1)
                one(NI - 2, 0)
                one(NI - 1, 1, True)
                y_out(NJ - 1, 1, NI - 1, (NI - 1) % 2 if HV == 1 else 0)

            @block.scalar
            def _(act):
                def x_in(i):
                    act.wait_ge(tr, i + 1)
                    act.activation(xt[:, 0:4, :], ps[:, 0, :].rearrange("p (k n) -> p k n", k=4), ACT.Copy).then_inc(xa, 1)

                def silu(j, u):
                    up_done(act, j, u)
                    act.wait_ge(hr, j)
                    act.activation(hs[:], ps[:, 2 + u, 0:256], ACT.Silu).then_inc(sl, 1)

                def h_t(j):
                    act.wait_ge(htr, j + 1)
                    act.activation(ht[:].rearrange("p k n -> p (k n)"), ps[:, 4, 0:256], ACT.Copy).then_inc(hte, 1)

                def y_out(j, u, i, v):
                    down_done(act, j, u)
                    if not (isinstance(i, int) and i < 3 - HV):
                        act.wait_ge(stored[v], stores_before(i, v))
                    act.activation(ysb[:, v, 0:HALF], ps[:, 6, :], ACT.Copy).then_inc(ya, 1)

                run(act, x_in, silu, h_t, y_out)

            @block.vector
            def _(dve):
                def x_in(i):
                    dve.wait_ge(tr, i + 1)
                    dve.tensor_copy(xt[:, 4:8, :], ps[:, 1, :].rearrange("p (k n) -> p k n", k=4)).then_inc(xd, 1)

                def times_up(j, u):
                    dve.wait_ge(sl, j + 1)
                    dve.wait_ge(htr, j)
                    dve.tensor_tensor(h[:], hs[:], ps[:, 2 + u, 256:512], ALU.mult).then_inc(hr, 1)

                def y_out(j, u, i, v):
                    down_done(dve, j, u)
                    if not (isinstance(i, int) and i < 3 - HV):
                        dve.wait_ge(stored[v], stores_before(i, v))
                    dve.tensor_copy(ysb[:, v, HALF:D], ps[:, 7, :]).then_inc(yd, 1)

                run(dve, x_in, times_up, lambda j: None, y_out)


def overflow(nc, m, c):
    with ExitStack() as ctx:
        sem = lambda name: ctx.enter_context(nc.semaphore(f"{c.tag}o_{name}"))
        sb = lambda name, shape, dt=F32: ctx.enter_context(nc.sbuf_tensor(f"{c.tag}o_{name}", shape, dt))
        HV = c.HV
        wg, wd = sb("wg", [P, KD, HALF]), sb("wd", [P, 2, D])
        xg, xt = sb("xg", [P, D]), sb("xt", [P, KD, P])
        hs, h, ht, ysb = sb("hs", [P, 256]), sb("h", [P, 256]), sb("ht", [P, 2, P]), sb("y", [P, D])
        idx = sb("idx", [P, 1], U32)
        ps = ctx.enter_context(nc.psum_tensor(f"{c.tag}o_ps", [P, 8, HALF], F32))
        got = c.got_over
        wr, wr2, stored, idx_r, tr, xe, up, sl, hr, htr, hte, down, ye = \
            (sem(n) for n in ("wr", "wr2", "st", "idx", "tr", "xe", "up", "sl", "hr", "htr", "hte", "dn", "ye"))

        def tiles(eng, body):
            n = eng.value_load(c.over[0:1, 0:1], min_val=0, max_val=EXTRA)
            with eng.If(n > 0):
                with eng.Fori(0, n) as i:
                    body(i)

        with nc.Block() as block:

            @block.sync
            def _(sp):
                def body(i):
                    e = sp.value_load(c.over[0:1, bass.ds(i + 1, 1)], min_val=0, max_val=c.NE - 1)
                    row, begun = sp.snap((i + c.NE) * P), sp.snap(i + 1)
                    jobs = [sp.snap(e * HV + v) for v in range(HV)]
                    used = [sp.snap(i * HV + v) for v in range(HV)]
                    for v, job in enumerate(jobs):
                        if v == 0:
                            sp.wait_ge(idx_r, begun)
                        else:
                            sp.wait_ge(down, used[v])
                        sp.dma_start(wg[:].rearrange("p k n -> p (k n)"),
                                     c.gu[bass.ds(job, 1)].rearrange("o p n -> (o p) n")).then_inc(wr, 16)
                        sp.dma_start(wd[:].rearrange("p k n -> p (k n)"),
                                     c.dn[bass.ds(job, 1)].rearrange("o p n -> (o p) n")).then_inc(wr2, 16)
                    sp.wait_ge(ye, i * 2 + 2)
                    sp.dma_start(c.y_rows[bass.ds(row, P), :], ysb[:]).then_inc(stored, 16)

                tiles(sp, body)

            @block.gpsimd
            def _(pool):
                def body(i):
                    pool.tensor_copy(idx[:], c.token[:, bass.ds(i + c.NE, 1)]).then_inc(idx_r, 1)
                    pool.drain()
                    pool.indirect_dma_start(xg[:], None, c.x_rows, bass.IndirectOffsetOnAxis(idx[:], 0)).then_inc(got, 16)
                    pool.wait_ge(got, i * 16 + 16)
                    pool.wait_ge(tr, i + 1)
                    pool.wait_ge(stored, i * 16 + 16)

                tiles(pool, body)

            @block.tensor
            def _(pe):
                def body(i):
                    pe.wait_ge(got, i * 16 + 16)
                    for k in range(KD):
                        last = pe.transpose(ps[:, k // 4, (k % 4) * P:(k % 4 + 1) * P], xg[:, k * P:(k + 1) * P], m.ident[:])
                    last.then_inc(tr, 1)
                    pe.wait_ge(xe, i * 2 + 2)
                    for v in range(HV):
                        pe.wait_ge(wr, (i * HV + v) * 16 + 16)
                        pe.wait_ge(wr2, (i * HV + v) * 16 + 16)
                        for k in range(KD):
                            last = pe.matmul(ps[:, 2, :], xt[:, k, :], wg[:, k, :], start=(k == 0), stop=(k == KD - 1))
                        last.then_inc(up, 1)
                        pe.wait_ge(hr, i * HV + v + 1)
                        for k in range(2):
                            last = pe.transpose(ps[:, 4, k * P:(k + 1) * P], h[:, k * P:(k + 1) * P], m.ident[:])
                        last.then_inc(htr, 1)
                        pe.wait_ge(hte, i * HV + v + 1)
                        for k in range(2):
                            for n in range(2):
                                last = pe.matmul(ps[:, 6 + n, :], ht[:, k, :], wd[:, k, n * HALF:(n + 1) * HALF],
                                                 start=(k == 0 and v == 0), stop=(k == 1 and v == HV - 1))
                        last.then_inc(down, 1)

                tiles(pe, body)

            @block.scalar
            def _(act):
                def body(i):
                    act.wait_ge(tr, i + 1)
                    for q in range(2):
                        act.activation(xt[:, 4 * q:4 * q + 4, :], ps[:, q, :].rearrange("p (k n) -> p k n", k=4), ACT.Copy)\
                           .then_inc(xe, 1)
                    for v in range(HV):
                        act.wait_ge(up, i * HV + v + 1)
                        act.activation(hs[:], ps[:, 2, 0:256], ACT.Silu).then_inc(sl, 1)
                        act.wait_ge(htr, i * HV + v + 1)
                        act.activation(ht[:].rearrange("p k n -> p (k n)"), ps[:, 4, 0:256], ACT.Copy).then_inc(hte, 1)
                    act.wait_ge(down, i * HV + HV)
                    for q in range(2):
                        act.activation(ysb[:, q * HALF:(q + 1) * HALF], ps[:, 6 + q, :], ACT.Copy).then_inc(ye, 1)
                    act.wait_ge(stored, i * 16 + 16)

                tiles(act, body)

            @block.vector
            def _(dve):
                def body(i):
                    for v in range(HV):
                        dve.wait_ge(sl, i * HV + v + 1)
                        dve.tensor_tensor(h[:], hs[:], ps[:, 2, 256:512], ALU.mult).then_inc(hr, 1)

                tiles(dve, body)


def combine(nc, m, c):
    with ExitStack() as ctx:
        sem = lambda name: ctx.enter_context(nc.semaphore(f"{c.tag}c_{name}"))
        y = ctx.enter_context(nc.sbuf_tensor(f"{c.tag}c_y", [P, NT, 2, D], F32))
        got = c.got_back
        junk = ctx.enter_context(nc.sbuf_tensor(f"{c.tag}c_junk", [P, D], F32))
        own, done, sq = sem("own"), sem("done"), sem("sq")
        with nc.Block() as block:

            @block.gpsimd
            def _(pool):
                for n in range(2 * NT):
                    pool.indirect_dma_start(y[:, n // 2, n % 2, :], None, c.y_rows,
                                            bass.IndirectOffsetOnAxis(c.slot[:, n // 2, n % 2:n % 2 + 1], 0)).then_inc(got[n], 16)
                for n in range(2 * NT):
                    pool.wait_ge(got[n], 16)

            @block.scalar
            def _(act):
                for t in range(NT):
                    act.wait_ge(done, t + 1)
                    sum_squares(act, m, t, junk, sq)
                act.wait_ge(sq, NT)

            @block.vector
            def _(dve):
                st = Steps(dve, own)
                for t in range(NT):
                    a, b = y[:, t, 0, :], y[:, t, 1, :]
                    dve.wait_ge(got[2 * t], 16)
                    st.link(dve.tensor_scalar(a, a, c.wt[:, t, 0:1], None, ALU.mult))
                    dve.wait_ge(got[2 * t + 1], 16)
                    st.link(dve.scalar_tensor_tensor(a, b, c.wt[:, t, 1:2], a, ALU.mult, ALU.add))
                    if c.gate is not None:
                        st.link(dve.tensor_tensor(a, a, c.gate, ALU.mult))
                    dve.tensor_tensor(m.x[:, t, :], m.x[:, t, :], a, ALU.add).then_inc(done, 1)
                dve.wait_ge(done, NT)


def second_mixer(nc, m, d, mix):
    sbm = lambda name, shape: mix.enter_context(nc.sbuf_tensor(name, shape, F32))
    s = Shared()
    s.gates_t = d["gates_t"]
    m.a_t = m.y_t = sbm("a_t2", [P, KD, T])
    s.lru, s.gate = sbm("lru", [P, 8, T]), sbm("gelu", [P, 8, T])
    s.pool, s.pool_y = sbm("pool", [P, 4, T]), sbm("pool_y", [P, 4, T])
    s.heads, s.pool_w = sbm("heads", [P, 2, 8, 64]), sbm("pool_w", [P, 4, P])
    norm_and_transpose(nc, m, "n3", None, None, None, m.a_t, g_src=d["norm1_g2"], summed=True)
    project2(nc, m, d, s)
    merge(nc, m, s)
    mix_out(nc, m, OUT20, None)


def project2(nc, m, d, s):
    N = NIN2 * 4
    with ExitStack() as ctx:
        sem = lambda name: ctx.enter_context(nc.semaphore(f"p2_{name}"))
        sb = lambda name, shape: ctx.enter_context(nc.sbuf_tensor(f"p2_{name}", shape, F32))
        pz = ctx.enter_context(nc.psum_tensor("p2_pz", [P, 4, HALF], F32))
        ps = ctx.enter_context(nc.psum_tensor("p2_ps", [P, 4, HALF], F32))
        sg = sb("sg", [P, 2, HALF])
        dense = sb("dense", [P, 2, 2, P])
        c8 = sb("c8", [P, 4, 8])
        part = lambda n: m.mods[:, n * T:(n + 1) * T]
        xc = m.mods[:, 0:2 * T].rearrange("p (b t) -> p b t", b=2)
        r, i_, mu, inv, w2, w3 = (part(n) for n in range(2, 8))
        cnt = m.mods[:, 8 * T:12 * T].rearrange("p (g t) -> p g t", g=4)
        mm, ev_a, ev_v, stored, par = sem("mm"), sem("eva"), sem("evv"), [sem("st0"), sem("st1")], sem("par")
        own, pown, zeroed, dense_r, conv, gmm, ra, aa, sq, mu_r, mu_q, pin, pmm, pev, ca, cv, cnt_r, xdone = \
            (sem(n) for n in ("own", "pown", "zero", "dense", "conv", "gmm", "ra", "aa", "sq", "mur", "muq", "pin", "pmm",
                              "pev", "ca", "cv", "cnt", "xd"))
        taps = at(m.par, "conv_w2")

        def product_of(eng, n):
            if n % 4 == 3:
                m.stream.wait_used(eng, IN20 + n // 4)
            else:
                eng.wait_ge(mm, n // 4 * 3 + n % 4 + 1)

        def copied_out(eng, n):
            if n < 16:
                eng.wait_ge(ev_a if n % 2 else ev_v, n // 2 + 1)
            elif n < 20:
                eng.wait_ge(ev_v, n - 7)
            else:
                eng.wait_ge(ev_a, n - 11)

        def lru_tail(dve, st, n):
            tt, ts = dve.tensor_tensor, dve.tensor_scalar
            dve.wait_ge(aa, 2 * n + 2)
            st.link(ts(inv[:], mu[:], 1.0, None, ALU.add))
            st.link(dve.reciprocal(inv[:], inv[:]))
            dve.scalar_tensor_tensor(mu[:], mu[:], 2.0, inv[:], ALU.mult, ALU.mult).then_inc(mu_r, 1)
            st.link(tt(i_[:], i_[:], xc[:, n % 2, :], ALU.mult))
            dve.wait_ge(mu_q, n + 1)
            st.link(tt(i_[:], i_[:], mu[:], ALU.mult))
            st.link(dve.tensor_tensor_scan(s.lru[:, n, :], r[:], i_[:], 0.0, ALU.mult, ALU.add))
            copied_out(dve, 2 * n + 1)
            tt(s.lru[:, n, :], s.lru[:, n, :], s.gate[:, n, :], ALU.mult).then_inc(xdone, 1)

        with nc.Block() as block:

            @block.sync
            def _(sp):
                sp.dma_start(s.heads[:].rearrange("p a b c -> p (a b c)"), d["heads"]).then_inc(par, 16)
                sp.dma_start(s.pool_w[:].rearrange("p a b -> p (a b)"), d["pool_w"]).then_inc(par, 16)
                m.stream.load(sp, IN20 + RING, IN20 + NIN2)
                for n in range(20, N):
                    q = n - 20
                    copied_out(sp, n)
                    sp.dma_start(d["gates_t"][q], sg[:, q % 2, :]).then_inc(stored[q % 2], 16)
                    if n % 4 == 3:
                        m.stream.load(sp, IN20 + RING + n // 4, IN20 + RING + n // 4 + 1)
                for v in stored:
                    sp.wait_ge(v, 16 * 8)

            @block.tensor
            def _(pe):
                def gates_of(q):
                    pe.wait_ge(dense_r, 4 * q + 4)
                    pe.wait_ge(conv, q + 1)
                    if q >= 2:
                        pe.wait_ge(aa, 2 * (q - 1))
                    for k in range(2):
                        last = pe.matmul(ps[:, 2 * (q % 2) + k, :], dense[:, q % 2, k, :], xc[:, q % 2, :], start=True, stop=True)
                    last.then_inc(gmm, 1)

                pe.wait_ge(par, 32)
                for n in range(N):
                    c, j = IN20 + n // 4, n % 4
                    w = m.ring[:, c % RING, :].rearrange("p (k n) -> p k n", k=KD)
                    if j == 0:
                        m.stream.wait(pe, c)
                    if n >= 4:
                        copied_out(pe, n - 4)
                    for k in range(KD):
                        last = pe.matmul(pz[:, n % 4, :], w[:, k, j * P:(j + 1) * P], m.a_t[:, k, :],
                                         start=(k == 0), stop=(k == KD - 1))
                    if j == 3:
                        m.stream.free(last, c)
                    else:
                        last.then_inc(mm, 1)
                    if n % 2 and 3 <= n < 19:
                        gates_of((n - 3) // 2)
                    if n in POOL_AFTER:
                        g = POOL_AFTER.index(n)
                        pe.wait_ge(pin, g + 1)
                        if g == 0:
                            pe.wait_ge(aa, 16)
                        if g >= 2:
                            pe.wait_ge(pev, g - 1)
                        pe.matmul(ps[:, g % 2, :], s.pool_w[:, g, :], s.pool[:, g, :], start=True, stop=True).then_inc(pmm, 1)

            @block.scalar
            def _(act):
                st = Steps(act, sq)

                def coefficients(n):
                    act.wait_ge(gmm, n + 1)
                    if n:
                        act.wait_ge(xdone, n)
                    b = 2 * (n % 2)
                    act.activation(i_[:], ps[:, b + 1, :], ACT.Sigmoid, bias=at(m.par, "b_i")[:, n:n + 1]).then_inc(ra, 1)
                    st.link(act.activation(r[:], ps[:, b, :], ACT.Sigmoid, bias=at(m.par, "b_r")[:, n:n + 1]))
                    act.activation(mu[:], r[:], ACT.Tanh, scale=c8[:, 1, n:n + 1]).then_inc(aa, 1)
                    act.wait_ge(aa, 2 * n + 1)
                    act.activation(r[:], r[:], ACT.Exp, scale=c8[:, 0, n:n + 1]).then_inc(aa, 1)
                    act.wait_ge(mu_r, n + 1)
                    act.activation(mu[:], mu[:], ACT.Sqrt).then_inc(mu_q, 1)

                lam = at(m.par, "lam2")
                st.link(act.activation(c8[:, 0, :], lam, ACT.Abs))
                st.link(act.activation(c8[:, 0, :], c8[:, 0, :], ACT.Exp, scale=-1.0))
                act.activation(c8[:, 1, :], c8[:, 0, :], ACT.Ln, bias=1.0).then_inc(cv, 1)
                act.wait_ge(cv, 2)
                for n in range(8):
                    product_of(act, 2 * n + 1)
                    act.activation(s.gate[:, n, :], pz[:, (2 * n + 1) % 4, :], ACT.Gelu_apprx_tanh).then_inc(ev_a, 1)
                    if n:
                        coefficients(n - 1)
                coefficients(7)
                for n in range(20, N):
                    q = n - 20
                    product_of(act, n)
                    if q >= 2:
                        act.wait_ge(stored[q % 2], 16 * (q // 2))
                    act.activation(sg[:, q % 2, :], pz[:, n % 4, :], ACT.Sigmoid).then_inc(ev_a, 1)
                    if n in POOL_AFTER:
                        g = POOL_AFTER.index(n)
                        act.wait_ge(pmm, g + 1)
                        act.activation(s.pool_y[:, g, :], ps[:, g % 2, :], ACT.Copy, scale=at(m.par, "pool_scale")[:, g:g + 1])\
                           .then_inc(pev, 1)

            @block.gpsimd
            def _(pool):
                st = Steps(pool, pown)
                pool.memset(dense[:], 0.0).then_inc(zeroed, 1)
                for g in range(4):
                    pool.tensor_scalar(cnt[:, g, :], m.t_row[:], 1.0, float(2 << g), ALU.add, ALU.min).then_inc(cnt_r, 1)
                for g in range(4):
                    copied_out(pool, 16 + g)
                    pool.wait_ge(ca, g + 1)
                    st.link(pool.tensor_copy(w2[:], s.pool[:, g, :]))
                    src, dst = w2, w3
                    for k in range(g + 1):
                        h = 1 << k
                        st.link(pool.tensor_copy(dst[:, 0:h], src[:, 0:h]))
                        st.link(pool.tensor_tensor(dst[:, h:], src[:, h:], src[:, :T - h], ALU.add))
                        src, dst = dst, src
                    st.link(pool.tensor_tensor(src[:], src[:], cnt[:, g, :], ALU.mult))
                    pool.tensor_tensor(s.pool[:, g, :], src[:], s.pool[:, g, :], ALU.subtract).then_inc(pin, 1)
                    pool.wait_ge(pin, g + 1)

            @block.vector
            def _(dve):
                st = Steps(dve, own)
                tt, ts, stt = dve.tensor_tensor, dve.tensor_scalar, dve.scalar_tensor_tensor

                def copy_out(n, dst):
                    product_of(dve, n)
                    dve.tensor_copy(dst, pz[:, n % 4, :]).then_inc(ev_v, 1)

                lam = at(m.par, "lam2")
                dve.wait_ge(cv, 1)
                st.link(ts(c8[:, 2, :], lam, -1.0, 0.0, ALU.mult, ALU.max))
                st.link(tt(c8[:, 3, :], c8[:, 2, :], c8[:, 1, :], ALU.add))
                st.link(ts(c8[:, 0, :], c8[:, 3, :], -8.0, None, ALU.mult))
                ts(c8[:, 1, :], c8[:, 3, :], 8.0, None, ALU.mult).then_inc(cv, 1)
                dve.wait_ge(zeroed, 1)
                dve.wait_ge(par, 32)
                for g in range(4):
                    dve.wait_ge(cnt_r, g + 1)
                    dve.reciprocal(cnt[:, g, :], cnt[:, g, :]).then_inc(ca, 1)
                for n in range(8):
                    b = n % 2
                    copy_out(2 * n, s.lru[:, n, :])
                    if n >= 2:
                        dve.wait_ge(gmm, n - 1)
                        dve.wait_ge(xdone, n - 1)
                    for k in range(2):
                        for h in range(2):
                            p = slice(64 * h, 64 * h + 64)
                            dve.tensor_copy(dense[p, b, k, 64 * h:64 * h + 64], s.heads[p, k, n, :]).then_inc(dense_r, 1)
                    o, q = xc[:, b, :], s.lru[:, n, :]
                    w = lambda k: taps[:, 4 * n + k:4 * n + k + 1]
                    copied_out(dve, 2 * n)
                    st.link(ts(o, q, w(3), at(m.par, "conv_b2")[:, n:n + 1], ALU.mult, ALU.add))
                    st.link(stt(o[:, 1:], q[:, :T - 1], w(2), o[:, 1:], ALU.mult, ALU.add))
                    st.link(stt(o[:, 2:], q[:, :T - 2], w(1), o[:, 2:], ALU.mult, ALU.add))
                    stt(o[:, 3:], q[:, :T - 3], w(0), o[:, 3:], ALU.mult, ALU.add).then_inc(conv, 1)
                    if n:
                        lru_tail(dve, st, n - 1)
                copy_out(16, s.pool[:, 0, :])
                copy_out(17, s.pool[:, 1, :])
                lru_tail(dve, st, 7)
                copy_out(18, s.pool[:, 2, :])
                copy_out(19, s.pool[:, 3, :])


def merge(nc, m, s):
    with ExitStack() as ctx:
        sem = lambda name: ctx.enter_context(nc.semaphore(f"mg_{name}"))
        ps = ctx.enter_context(nc.psum_tensor("mg_ps", [P, 4, HALF], F32))
        sg = ctx.enter_context(nc.sbuf_tensor("mg_sg", [P, 2, 2, T], F32))
        mm, used, own, done, g_in = sem("mm"), sem("used"), sem("own"), sem("done"), [sem("g0"), sem("g1")]
        gates = s.gates_t
        with nc.Block() as block:

            @block.sync
            def _(sp):
                for n in range(8):
                    if n >= 2:
                        sp.wait_ge(done, n - 1)
                    sp.dma_start(sg[:, n % 2, 0, :], gates[n]).then_inc(g_in[n % 2], 16)
                    sp.dma_start(sg[:, n % 2, 1, :], gates[8 + n]).then_inc(g_in[n % 2], 16)
                m.stream.load(sp, PRA0 + RING, PRA0 + RING + 1)

            @block.tensor
            def _(pe):
                m.stream.wait(pe, PRA0)
                wa = m.ring[:, PRA0 % RING, :].rearrange("p (k n) -> p k n", k=4)
                for n in range(8):
                    c, j = PRB0 + n // 4, n % 4
                    if j == 0:
                        m.stream.wait(pe, c)
                    if n >= 2:
                        pe.wait_ge(used, 2 * (n - 1))
                    wb = m.ring[:, c % RING, :].rearrange("p (k n) -> p k n", k=KD)
                    b = 2 * (n % 2)
                    for k in range(4):
                        last = pe.matmul(ps[:, b, :], wa[:, k, n * P:(n + 1) * P], s.pool_y[:, k, :], start=(k == 0), stop=(k == 3))
                    if n == 7:
                        m.stream.free(last, PRA0)
                    for k in range(KD):
                        last = pe.matmul(ps[:, b + 1, :], wb[:, k, j * P:(j + 1) * P], s.lru[:, k, :], start=(k == 0),
                                         stop=(k == KD - 1))
                    if j == 3:
                        m.stream.free(last, c)
                    else:
                        last.then_inc(mm, 1)

            @block.vector
            def _(dve):
                st = Steps(dve, own)
                for n in range(8):
                    dve.wait_ge(g_in[n % 2], 32 * (n // 2 + 1))
                    if n % 4 == 3:
                        m.stream.wait_used(dve, PRB0 + n // 4)
                    else:
                        dve.wait_ge(mm, n // 4 * 3 + n % 4 + 1)
                    b = 2 * (n % 2)
                    a0, b0 = sg[:, n % 2, 0, :], sg[:, n % 2, 1, :]
                    dve.tensor_tensor(a0, a0, ps[:, b, :], ALU.mult).then_inc(used, 1)
                    dve.tensor_tensor(b0, b0, ps[:, b + 1, :], ALU.mult).then_inc(used, 1)
                    dve.wait_ge(used, 2 * n + 2)
                    dve.tensor_tensor(m.y_t[:, n, :], a0, b0, ALU.add).then_inc(done, 1)


def gather_semaphores(sem, tag):
    return dict(got=[sem(f"{tag}_got{n}") for n in range(2)], got_over=sem(f"{tag}_got_over"),
                got_back=[sem(f"{tag}_got_back{n}") for n in range(2 * NT)])


def clear_semaphores(nc, m):
    with nc.Block() as block:

        @block.gpsimd
        def _(pool):
            pool.sem_clear(m.phase_sems)


def moe(nc, m, c, sb, scale, shift, g_src):
    c.wt, c.slot = sb(f"{c.tag}_wt", [P, NT, 2]), sb(f"{c.tag}_slot", [P, NT, 2], U32)
    c.token, c.over = sb(f"{c.tag}_token", [P, c.NE + EXTRA], U32), sb(f"{c.tag}_over", [1, 1 + EXTRA], I32)
    with nc.sbuf_tensor(f"{c.tag}_a_t", [P, KD, T], F32) as a_t:
        m.a_t = a_t
        norm_and_transpose(nc, m, f"{c.tag}n", scale, shift, c.x_rows, a_t, g_src=g_src, summed=True)
        route(nc, m, c)
    experts(nc, m, c)
    overflow(nc, m, c)
    combine(nc, m, c)


def program(nc, d, upto=99):
    with ExitStack() as ctx:
        sb = lambda name, shape, dt=F32: ctx.enter_context(nc.sbuf_tensor(name, shape, dt))
        sem = lambda name: ctx.enter_context(nc.semaphore(name))
        m = Shared()
        d["x_rows"] = nc.dram_tensor("x_rows", (T, D), F32, kind="Internal").ap()
        d["gates_t"] = nc.dram_tensor("gates_t", (16, P, T), F32, kind="Internal").ap()
        d["x_rows2"] = nc.dram_tensor("x_rows2", (T, D), F32, kind="Internal").ap()
        d["y_rows"] = nc.dram_tensor("y_rows", ((32 + EXTRA) * P, D), F32, kind="Internal").ap()
        m.x = sb("x", [P, NT, D])
        m.ss = sb("ss", [P, NT])
        m.mods = sb("mods", [P, 6 * D])
        m.ring = sb("ring", [P, RING, SLOT])
        m.par = sb("par", [P, NCOL])
        m.rows = sb("rows", [P, NROW])
        m.ident, m.ones, m.tri = sb("ident", [P, P]), sb("ones", [P, P]), sb("tri", [P, P])
        m.strip = sb("strip", [P, 16])
        m.upto, m.same = sb("upto", [P, P]), sb("same", [P, P])
        m.level = sb("level", [P, 6, P])
        m.t_row = sb("t_row", [P, T])
        m.w_ready = [sem(f"w_ready{n}") for n in range(RING)]
        m.w_free = [sem(f"w_free{n}") for n in range(RING)]
        m.x_in = sem("x_in")
        gathers = [gather_semaphores(sem, tag) for tag in ("m1", "m2")]
        with nc.semaphore("first_of_phases") as first:
            m.phase_sems = range(first.num, LAST_SEM)
        src = [d["w_ada"][n] for n in range(NADA)] + [d["w_in"][n] for n in range(NIN)] + [d["w_glu"]]
        src += [d["w_out"][n] for n in range(2)]
        src += [y for e in range(32) for y in (d["gu"][e], d["dn"][e])]
        src += [d["w_in2"][n] for n in range(NIN2)] + [d["proj_a"]] + [d["proj_b"][n] for n in range(2)]
        src += [d["w_out2"][n] for n in range(2)] + [None, None]
        src += [y for e in range(32) for y in (d["gu2"][e], d["dn2"][e])]
        assert len(src) == NCHUNK
        m.stream = Stream(m, src)
        m.stream.stop = {1: 17, 2: 18, 3: 18, 4: 20, 5: 20, 6: 84, 7: 100}.get(upto, NCHUNK)
        m.spare = m.mods[:, 0:2 * D]
        mod = lambda n: m.mods[:, n * D:(n + 1) * D]

        constants_and_modulation(nc, m, d)
        with ExitStack() as mix:
            sbm = lambda name, shape: mix.enter_context(nc.sbuf_tensor(name, shape, F32))
            m.u_t, m.qkv, m.z_t = sbm("u_t", [P, 4, T]), sbm("qkv", [P, 12, T]), sbm("z_t", [P, 4, T])
            m.y_t = m.a_t = sbm("y_t", [P, KD, T])
            m.gates = sbm("gates", [P, NT * 8])
            norm_and_transpose(nc, m, "n1", mod(1), mod(0), None, m.a_t)
            project_and_s5(nc, m, d)
            if upto < 3: return m
            delta_rule(nc, m)
            if upto < 4: return m
            mix_out(nc, m, OUT0, mod(2))
        if upto < 5: return m
        c = Experts(tag="m1", NE=32, NG=4, EG=8, NJ=32, HV=1, first=MOE0, router="w_router", bias=None,
                    gu=d["gu"], dn=d["dn"], gate=mod(5), x_rows=d["x_rows"], y_rows=d["y_rows"], **gathers[0])
        clear_semaphores(nc, m)
        moe(nc, m, c, sb, mod(4), mod(3), None)
        if upto < 7: return m
        clear_semaphores(nc, m)
        norm_and_transpose(nc, m, "nf", None, None, None, None, g_src=d["normf_g"], in_place=True, summed=True)
        with ExitStack() as mix:
            second_mixer(nc, m, d, mix)
        if upto < 9: return m
        c = Experts(tag="m2", NE=16, NG=4, EG=4, NJ=32, HV=2, first=MOE20, router="w_router2",
                    bias=row_at(m.rows, "router_b2"), gu=d["gu2"], dn=d["dn2"], gate=None,
                    x_rows=d["x_rows2"], y_rows=d["y_rows"], **gathers[1])
        clear_semaphores(nc, m)
        moe(nc, m, c, sb, None, None, d["norm2_g2"])
        norm_and_transpose(nc, m, "nl", None, None, None, None, g_src=d["normf_g2"], final_out=d["out"], summed=True)


_OUT = (1, T, D)


def _layouts(i):
    import numpy as np
    f = lambda a: np.ascontiguousarray(a)
    col = lambda a, n: a.reshape(n, P).T
    chunks = lambda w, k, n: f(w.reshape(k, P, -1, n).transpose(2, 1, 0, 3).reshape(-1, P, k * n))
    state = lambda a: a.reshape(NS5, P).T
    tiles = lambda a, k: a.reshape(k, P, -1).transpose(1, 0, 2).reshape(P, -1)
    taps = lambda w, n: w.T.reshape(n, P, 4).transpose(1, 0, 2).reshape(P, -1)
    bt = lambda b: b.reshape(NS5, P, G16).transpose(1, 0, 2).reshape(P, -1)
    ct = lambda c: c.transpose(0, 2, 1).reshape(NS5, P, G16).transpose(1, 0, 2).reshape(P, -1)
    w_in = i["w_in"][0]
    w2 = i["w_in_2"][0]
    turns = [w2[:, o + n * P:o + (n + 1) * P] for n in range(8) for o in (512, 1536)]
    w_in2 = np.concatenate(turns + [w2[:, 0:512], w2[:, 2560:]], 1)
    cols = dict(
        c=col(i["c"][0], 8), s5_d=col(i["s5_d"][0], 4), b_glu=col(i["b_glu"][0], 4), conv_w=taps(i["conv_w"][0], 12),
        gdn_g=i["gdn_norm_g"][0].reshape(P, 1), lam_re=state(i["lam_re"][0]), lam_im=state(i["lam_im"][0]),
        log_step=state(np.repeat(i["log_step"][0], 64)), b_re=bt(i["s5_b_re"][0]), b_im=bt(i["s5_b_im"][0]),
        c_re=ct(i["s5_c_re"][0]), c_im=ct(i["s5_c_im"][0]), w_gates=tiles(w_in[:, 2560:], KD),
        w_router=tiles(np.concatenate([i["w_router_grp"][0], i["w_router_exp"][0]], 1), KD),
        pool_scale=col(i["pool_scale_2"][0], 4), conv_w2=taps(i["conv_w_2"][0], 8), conv_b2=col(i["conv_b_2"][0], 8),
        b_r=col(i["rg_b_r_2"][0], 8), b_i=col(i["rg_b_i_2"][0], 8), lam2=col(i["rg_lambda_2"][0], 8),
        w_router2=tiles(np.concatenate([i["router_group_w_2"][0], i["router_expert_w_2"][0]], 1), KD))
    gu = lambda g, u, e: f(np.concatenate([g.reshape(-1, KD, P, 1, e).transpose(0, 2, 1, 3, 4),
                                           u.reshape(-1, KD, P, 1, e).transpose(0, 2, 1, 3, 4)], 3).reshape(-1, P, KD * 2 * e))
    half = lambda w: w.reshape(16, D, 2, 256).transpose(0, 2, 1, 3).reshape(32, D, 256)
    dn = lambda w: f(w.reshape(32, 2, P, D).transpose(0, 2, 1, 3).reshape(32, P, 2 * D))
    heads = lambda w: w.reshape(8, P, 64).transpose(1, 0, 2).reshape(P, -1)
    return dict(
        x=f(i["x"][0].reshape(NT, P, D).transpose(1, 0, 2)),
        cols=f(np.concatenate([cols[n].reshape(P, k) for n, k in COLS], 1)),
        rows=f(np.concatenate([i["a_log"][0], i["dt_bias"][0], i["router_group_b_2"][0], i["router_expert_b_2"][0]])),
        b_ada=f(i["b_ada"]), norm1_g=f(i["norm1_g"][0]), norm2_g=f(i["norm2_g"][0]), normf_g=f(i["normf_g"]),
        norm1_g2=f(i["norm1_g_2"][0]), norm2_g2=f(i["norm2_g_2"][0]), normf_g2=f(i["norm_f_g_2"]),
        w_ada=chunks(i["w_ada"][0], KD, HALF), w_in=chunks(w_in[:, :2560], KD, HALF),
        w_glu=chunks(i["w_glu"][0], 4, HALF)[0], w_out=chunks(i["w_out"][0], KD, HALF),
        gu=gu(i["w_gate"][0], i["w_up"][0], 256), dn=dn(i["w_down"][0]),
        w_in2=chunks(w_in2, KD, HALF), proj_a=chunks(i["proj_a_2"][0], 4, D)[0],
        proj_b=chunks(i["proj_b_2"][0], KD, HALF), w_out2=chunks(i["w_out_2"][0], KD, HALF),
        heads=f(np.concatenate([heads(i["rg_w_r_2"][0]), heads(i["rg_w_i_2"][0])], 1)),
        pool_w=f(i["pool_w_2"][0].transpose(1, 0, 2).reshape(P, -1)),
        gu2=gu(half(i["exp_w_gate_2"][0]), half(i["exp_w_up_2"][0]), 256), dn2=dn(i["exp_w_down_2"][0]))


def kernel(**inputs):
    import numpy as np
    import concourse.bacc as bacc
    from concourse.bass_utils import run_bass_kernel_spmd

    arrays = _layouts({k: np.asarray(v) for k, v in inputs.items()})
    nc = bacc.Bacc("TRN2", target_bir_lowering=False, num_devices=1)
    d = {k: nc.dram_tensor(f"in_{k}", v.shape, F32, kind="ExternalInput").ap() for k, v in arrays.items()}
    d["out"] = nc.dram_tensor("out", (T, D), F32, kind="ExternalOutput").ap()
    program(nc, d)
    r = run_bass_kernel_spmd(nc, [{f"in_{k}": v for k, v in arrays.items()}], core_ids=[0])
    return r.results[0]["out"].reshape(_OUT)
```
